# Optimizing a Trainium2 kernel written in Bass

```python
import math
import jax, jax.numpy as jnp
from jax import lax
import numpy as np

D_MODEL = 2048
BATCH = 1
SEQ = 256
DEPTH = 1
DEC_BATCH = 8
DEC_SEQ = 8
PAST_LEN = 1024
PAGE_SIZE = 128

HEAD_DIM = 64
RW_WIDTH = D_MODEL // 2
RW_HEADS = RW_WIDTH // HEAD_DIM
AT_WIDTH = D_MODEL - RW_WIDTH
AT_HEADS = AT_WIDTH // HEAD_DIM
MIX_WIDTH = RW_WIDTH + AT_WIDTH
DECAY_LORA = 64
ICLR_LORA = 64
GATE_LORA = 128
GN_EPS = 64e-5
IDX_HEADS = 16
IDX_DIM = 64
TOPK_MAX = 256
Q_BLOCK = 128
N_BUCKETS = 32
MAX_DISTANCE = 128
MEM_TOKENS = 256
X_HEADS = 4
X_HEAD_DIM = 128
X_WIDTH = X_HEADS * X_HEAD_DIM
N_GROUPS = 4
EXPERTS_PER_GROUP = 8
N_EXPERTS = N_GROUPS * EXPERTS_PER_GROUP
TOP_K_EXPERT = 2
D_EXPERT = 512
MOE_BLOCK = 64
NORM_EPS = 1e-6

RW_SPLITS = [RW_WIDTH, 2 * RW_WIDTH, 3 * RW_WIDTH, 3 * RW_WIDTH + DECAY_LORA, 3 * RW_WIDTH + DECAY_LORA + ICLR_LORA]
RW_PROJ = 3 * RW_WIDTH + DECAY_LORA + ICLR_LORA + GATE_LORA
AT_SPLITS = [AT_WIDTH, 2 * AT_WIDTH, 3 * AT_WIDTH, 3 * AT_WIDTH + IDX_HEADS * IDX_DIM, 3 * AT_WIDTH + IDX_HEADS * IDX_DIM + IDX_DIM]
AT_PROJ = 3 * AT_WIDTH + IDX_HEADS * IDX_DIM + IDX_DIM + IDX_HEADS
PROJ_WIDTH = RW_PROJ + AT_PROJ

kernel_name = 'hymba_rwkv7_dsa_hiermoe_step'

def rmsnorm(x, g):
    xf = x.astype(jnp.float32)
    y = xf * lax.rsqrt(jnp.mean(xf * xf, -1, keepdims=True) + NORM_EPS)
    return (y * g.astype(jnp.float32)).astype(x.dtype)

def token_shift(f, prev_row, mu):
    f_prev = jnp.concatenate([prev_row[:, None].astype(f.dtype), f[:, :-1]], axis=1)
    return f + (f_prev - f) * mu

def rwkv_group(fs, wkv0, w0, w2, a0, a2, g2, k_k, k_a, r_k, ln_g, ln_b):
    B, T, _ = fs.shape
    f = fs.astype(jnp.float32)
    r, k, v, wd, ad, gd = jnp.split(f, RW_SPLITS, axis=-1)
    w = -jax.nn.softplus(-(w0 + jnp.tanh(wd) @ w2)) - 0.5
    decay = jnp.exp(-jnp.exp(w))
    a = jax.nn.sigmoid(a0 + ad @ a2)
    g = jax.nn.sigmoid(gd) @ g2
    heads = lambda z: z.reshape(B, T, RW_HEADS, HEAD_DIM)
    kk = heads(k * k_k)
    kk = kk / jnp.maximum(jnp.sqrt(jnp.sum(kk * kk, -1, keepdims=True)), 1e-12)
    k = heads(k * (1.0 + (a - 1.0) * k_a))
    r, v, a, decay = heads(r), heads(v), heads(a), heads(decay)

    def step(S, inp):
        r_t, k_t, v_t, kk_t, a_t, w_t = inp
        sa = jnp.einsum('bhij,bhj->bhi', S, -kk_t)
        S = S * w_t[:, :, None, :] + sa[..., None] * (kk_t * a_t)[:, :, None, :] + v_t[..., None] * k_t[:, :, None, :]
        return S, jnp.einsum('bhij,bhj->bhi', S, r_t)

    seq = tuple(jnp.moveaxis(z, 1, 0) for z in (r, k, v, kk, a, decay))
    S_T, y = lax.scan(step, wkv0.astype(jnp.float32), seq)
    y = jnp.moveaxis(y, 0, 1)
    mu = jnp.mean(y, -1, keepdims=True)
    var = jnp.mean(jnp.square(y - mu), -1, keepdims=True)
    y = ((y - mu) * lax.rsqrt(var + GN_EPS)).reshape(B, T, RW_WIDTH) * ln_g + ln_b
    bonus = jnp.sum(r * k * r_k, -1, keepdims=True) * v
    out = (y + bonus.reshape(B, T, RW_WIDTH)) * g
    return out.astype(fs.dtype), S_T

def split_attn(fat):
    B, T, _ = fat.shape
    q, k, v, iq, ik, iw = jnp.split(fat, AT_SPLITS, axis=-1)
    hd = lambda z: z.reshape(B, T, AT_HEADS, HEAD_DIM)
    return hd(q), hd(k), hd(v), iq.reshape(B, T, IDX_HEADS, IDX_DIM), ik, iw

def t5_bucket(dist):
    exact = N_BUCKETS // 2
    d = jnp.maximum(dist, 0)
    far = exact + (jnp.log(jnp.maximum(d, 1).astype(jnp.float32) / exact) / math.log(MAX_DISTANCE / exact) * (N_BUCKETS - exact)).astype(jnp.int32)
    return jnp.where(d < exact, d, jnp.minimum(far, N_BUCKETS - 1))

def indexer_scores(iq, iw, ik):
    dots = jnp.einsum('bqhd,bsd->bqhs', iq, ik).astype(jnp.float32)
    wts = iw.astype(jnp.float32) * (IDX_HEADS ** -0.5 * IDX_DIM ** -0.5)
    return jnp.einsum('bqhs,bqh->bqs', jax.nn.relu(dots), wts)

def select_keys(scores, q_pos, n_keys, topk):
    key_pos = jnp.arange(n_keys)
    scores = jnp.where(key_pos[None, None, :] <= q_pos[None, :, None], scores, -jnp.inf)
    return lax.top_k(scores, topk)[1]

def sparse_attend(q, k_sel, v_sel, q_pos, sel, rel_bias):
    dist = q_pos[None, :, None] - sel
    valid = dist >= 0
    bias = jnp.moveaxis(rel_bias[t5_bucket(dist)], -1, 2).astype(jnp.float32)
    logits = jnp.einsum('bqhd,bqkhd->bqhk', q, k_sel).astype(jnp.float32) * HEAD_DIM ** -0.5 + bias
    logits = jnp.where(valid[:, :, None, :], logits, -jnp.inf)
    p = jax.nn.softmax(logits, axis=-1)
    return jnp.einsum('bqhk,bqkhd->bqhd', p.astype(v_sel.dtype), v_sel)

def dsa_prompt(q, k, v, iq, ik, iw, rel_bias, topk):
    B, S = q.shape[:2]
    nb = S // Q_BLOCK
    blockify = lambda z: jnp.moveaxis(z.reshape(B, nb, Q_BLOCK, *z.shape[2:]), 1, 0)
    bidx = jnp.arange(B)[:, None, None]

    def one_block(args):
        i, qb, iqb, iwb = args
        q_pos = i * Q_BLOCK + jnp.arange(Q_BLOCK)
        sel = select_keys(indexer_scores(iqb, iwb, ik), q_pos, S, topk)
        return sparse_attend(qb, k[bidx, sel], v[bidx, sel], q_pos, sel, rel_bias)

    out = lax.map(one_block, (jnp.arange(nb), blockify(q), blockify(iq), blockify(iw)))
    return jnp.moveaxis(out, 0, 1).reshape(B, S, AT_WIDTH)

def dsa_sample(l, q, k_new, v_new, iq, ik_new, iw, cache_k, cache_v, cache_idx_k, page_table, rel_bias, topk):
    DB, T = q.shape[:2]
    past = page_table.shape[1] * PAGE_SIZE
    ik_past = cache_idx_k[l, page_table].reshape(DB, past, IDX_DIM)
    ik_all = jnp.concatenate([ik_past, ik_new.astype(ik_past.dtype)], axis=1)
    q_pos = past + jnp.arange(T)
    sel = select_keys(indexer_scores(iq, iw, ik_all), q_pos, past + T, topk)
    b3 = jnp.arange(DB)[:, None, None]
    ps = jnp.minimum(sel, past - 1)
    phys = page_table[b3, ps // PAGE_SIZE]
    off = ps % PAGE_SIZE
    ns = jnp.clip(sel - past, 0, T - 1)
    in_past = (sel < past)[..., None, None]
    k_sel = jnp.where(in_past, cache_k[l, phys, off], k_new[b3, ns].astype(cache_k.dtype))
    v_sel = jnp.where(in_past, cache_v[l, phys, off], v_new[b3, ns].astype(cache_v.dtype))
    return sparse_attend(q, k_sel, v_sel, q_pos, sel, rel_bias).reshape(DB, T, AT_WIDTH)

def memory_kv(mem, g_mem, w_ck, w_cv):
    B, M, _ = mem.shape
    hm = rmsnorm(mem, g_mem)
    return (hm @ w_ck).reshape(B, M, X_HEADS, X_HEAD_DIM), (hm @ w_cv).reshape(B, M, X_HEADS, X_HEAD_DIM)

def cross_attend(h, mk, mv, w_cq, w_co):
    B, T, _ = h.shape
    q = (h @ w_cq).reshape(B, T, X_HEADS, X_HEAD_DIM)
    logits = jnp.einsum('bthd,bmhd->bhtm', q, mk.astype(q.dtype)).astype(jnp.float32) * X_HEAD_DIM ** -0.5
    p = jax.nn.softmax(logits, axis=-1)
    o = jnp.einsum('bhtm,bmhd->bthd', p.astype(q.dtype), mv.astype(q.dtype)).reshape(B, T, X_WIDTH)
    return o @ w_co

def hier_route(h, w_rg, b_rg, w_re, b_re):
    N = h.shape[0]
    g_logits = (h @ w_rg).astype(jnp.float32) + b_rg.astype(jnp.float32)
    grp = jnp.argmax(g_logits, axis=-1)
    p_grp = jnp.take_along_axis(jax.nn.softmax(g_logits, axis=-1), grp[:, None], axis=1)
    e_logits = ((h @ w_re).astype(jnp.float32) + b_re.astype(jnp.float32)).reshape(N, N_GROUPS, EXPERTS_PER_GROUP)
    e_logits = jnp.take_along_axis(e_logits, grp[:, None, None], axis=1)[:, 0]
    vals, loc = lax.top_k(e_logits, TOP_K_EXPERT)
    gates = jax.nn.softmax(vals, axis=-1) * p_grp
    return gates, grp[:, None].astype(jnp.int32) * EXPERTS_PER_GROUP + loc.astype(jnp.int32)

def moe_ffn(h, w_rg, b_rg, w_re, b_re, w1, w3, w2):
    lead = h.shape[:-1]
    hf = h.reshape(-1, D_MODEL)
    N = hf.shape[0]
    gates, eids = hier_route(hf, w_rg, b_rg, w_re, b_re)
    M = N * TOP_K_EXPERT
    flat_e = eids.reshape(-1)
    flat_tok = jnp.repeat(jnp.arange(N, dtype=jnp.int32), TOP_K_EXPERT)
    flat_g = gates.reshape(-1)
    order = jnp.argsort(flat_e)
    se = flat_e[order]
    counts = jnp.bincount(flat_e, length=N_EXPERTS)
    padded = (counts + MOE_BLOCK - 1) // MOE_BLOCK * MOE_BLOCK
    pad_end = jnp.cumsum(padded)
    pad_start = pad_end - padded
    start = jnp.cumsum(counts) - counts
    dest = pad_start[se] + jnp.arange(M) - start[se]
    n_blocks = -(-M // MOE_BLOCK) + N_EXPERTS
    rows = n_blocks * MOE_BLOCK
    buf_tok = jnp.full((rows,), N, jnp.int32).at[dest].set(flat_tok[order])
    buf_g = jnp.zeros((rows,), jnp.float32).at[dest].set(flat_g[order])
    blk_e = jnp.minimum(jnp.searchsorted(pad_end, jnp.arange(n_blocks) * MOE_BLOCK, side='right'), N_EXPERTS - 1)
    h_pad = jnp.concatenate([hf, jnp.zeros((1, D_MODEL), hf.dtype)], axis=0)

    def run_block(args):
        tok, g, e = args
        xb = h_pad[tok]
        u = jax.nn.silu(xb @ w1[e]) * (xb @ w3[e])
        return (u @ w2[e]) * g[:, None].astype(xb.dtype)

    ys = lax.map(run_block, (buf_tok.reshape(n_blocks, MOE_BLOCK), buf_g.reshape(n_blocks, MOE_BLOCK), blk_e))
    out = jnp.zeros((N + 1, D_MODEL), ys.dtype).at[buf_tok].add(ys.reshape(rows, D_MODEL))[:N]
    return out.reshape(*lead, D_MODEL).astype(h.dtype)

def post_mixer(x, rw_out, at_out, mk, mv, w_out, g_cross, w_cq, w_co, g_ffn, w_rg, b_rg, w_re, b_re, w1, w3, w2):
    x = x + jnp.concatenate([rw_out, at_out.astype(rw_out.dtype)], axis=-1) @ w_out
    x = x + cross_attend(rmsnorm(x, g_cross), mk, mv, w_cq, w_co)
    return x + moe_ffn(rmsnorm(x, g_ffn), w_rg, b_rg, w_re, b_re, w1, w3, w2)

def setup_inputs(seed: int = 0) -> dict:
    key = jax.random.key(seed)
    ks = iter(jax.random.split(key, 64))
    f32 = jnp.float32
    nrm = lambda shape, scale=1.0: jax.random.normal(next(ks), shape, f32) * scale
    gain = lambda shape: 1.0 + jax.random.normal(next(ks), shape, f32) * 0.05
    L = DEPTH
    n_pages = PAST_LEN // PAGE_SIZE
    in_use = DEC_BATCH * n_pages
    n_pool = in_use + max(1, in_use // 4)
    inputs = {}
    inputs['x_prompt'] = nrm((BATCH, SEQ, D_MODEL))
    inputs['x_sample'] = nrm((DEC_BATCH, DEC_SEQ, D_MODEL))
    inputs['mem_prompt'] = nrm((BATCH, MEM_TOKENS, D_MODEL))
    inputs['cache_k'] = nrm((L, n_pool, PAGE_SIZE, AT_HEADS, HEAD_DIM))
    inputs['cache_v'] = nrm((L, n_pool, PAGE_SIZE, AT_HEADS, HEAD_DIM))
    inputs['cache_idx_k'] = nrm((L, n_pool, PAGE_SIZE, IDX_DIM))
    inputs['page_table'] = jax.random.permutation(next(ks), n_pool)[:in_use].reshape(DEC_BATCH, n_pages).astype(jnp.int32)
    inputs['state_wkv'] = nrm((L, DEC_BATCH, RW_HEADS, HEAD_DIM, HEAD_DIM))
    inputs['state_shift'] = nrm((L, DEC_BATCH, RW_PROJ))
    inputs['cache_mem_k'] = nrm((L, DEC_BATCH, MEM_TOKENS, X_HEADS, X_HEAD_DIM))
    inputs['cache_mem_v'] = nrm((L, DEC_BATCH, MEM_TOKENS, X_HEADS, X_HEAD_DIM))
    inputs['g_mix'] = gain((L, D_MODEL))
    inputs['w_in'] = nrm((L, D_MODEL, PROJ_WIDTH), D_MODEL ** -0.5)
    inputs['mu_shift'] = jax.random.uniform(next(ks), (L, RW_PROJ), f32, 0.0, 1.0)
    inputs['rw_w0'] = jax.random.uniform(next(ks), (L, RW_WIDTH), f32, -6.0, -1.0)
    inputs['rw_w2'] = nrm((L, DECAY_LORA, RW_WIDTH), 0.1 * DECAY_LORA ** -0.5)
    inputs['rw_a0'] = nrm((L, RW_WIDTH), 0.1)
    inputs['rw_a2'] = nrm((L, ICLR_LORA, RW_WIDTH), 0.5 * ICLR_LORA ** -0.5)
    inputs['rw_g2'] = nrm((L, GATE_LORA, RW_WIDTH), GATE_LORA ** -0.5)
    inputs['rw_kk'] = 0.85 + nrm((L, RW_WIDTH), 0.05)
    inputs['rw_ka'] = gain((L, RW_WIDTH))
    inputs['rw_rk'] = nrm((L, RW_HEADS, HEAD_DIM), 0.1)
    inputs['rw_ln_g'] = gain((L, RW_WIDTH))
    inputs['rw_ln_b'] = nrm((L, RW_WIDTH), 0.02)
    inputs['w_out'] = nrm((L, MIX_WIDTH, D_MODEL), MIX_WIDTH ** -0.5)
    inputs['g_cross'] = gain((L, D_MODEL))
    inputs['g_mem'] = gain((L, D_MODEL))
    inputs['w_cq'] = nrm((L, D_MODEL, X_WIDTH), D_MODEL ** -0.5)
    inputs['w_ck'] = nrm((L, D_MODEL, X_WIDTH), D_MODEL ** -0.5)
    inputs['w_cv'] = nrm((L, D_MODEL, X_WIDTH), D_MODEL ** -0.5)
    inputs['w_co'] = nrm((L, X_WIDTH, D_MODEL), X_WIDTH ** -0.5)
    inputs['g_ffn'] = gain((L, D_MODEL))
    inputs['w_rg'] = nrm((L, D_MODEL, N_GROUPS), D_MODEL ** -0.5)
    inputs['b_rg'] = nrm((L, N_GROUPS), 0.01)
    inputs['w_re'] = nrm((L, D_MODEL, N_EXPERTS), D_MODEL ** -0.5)
    inputs['b_re'] = nrm((L, N_EXPERTS), 0.01)
    inputs['w_e1'] = nrm((L, N_EXPERTS, D_MODEL, D_EXPERT), D_MODEL ** -0.5)
    inputs['w_e3'] = nrm((L, N_EXPERTS, D_MODEL, D_EXPERT), D_MODEL ** -0.5)
    inputs['w_e2'] = nrm((L, N_EXPERTS, D_EXPERT, D_MODEL), D_EXPERT ** -0.5)
    inputs['rel_bias'] = nrm((N_BUCKETS, AT_HEADS), 0.1)
    inputs['g_final'] = gain((D_MODEL,))
    return inputs

def reference(x_prompt, x_sample, mem_prompt, cache_k, cache_v, cache_idx_k, page_table, state_wkv, state_shift,
              cache_mem_k, cache_mem_v, g_mix, w_in, mu_shift, rw_w0, rw_w2, rw_a0, rw_a2, rw_g2, rw_kk, rw_ka,
              rw_rk, rw_ln_g, rw_ln_b, w_out, g_cross, g_mem, w_cq, w_ck, w_cv, w_co, g_ffn, w_rg, b_rg, w_re,
              b_re, w_e1, w_e3, w_e2, rel_bias, g_final):
    B, S, _ = x_prompt.shape
    DB, T, _ = x_sample.shape
    past = page_table.shape[1] * PAGE_SIZE
    topk_p = min(TOPK_MAX, S // 4)
    topk_s = min(TOPK_MAX, (past + T) // 4)
    xp, xs = x_prompt, x_sample
    kp, vp, ikp, wkvp, shp, mkp, mvp = [], [], [], [], [], [], []
    ks_, vs_, iks, wkvs, shs = [], [], [], [], []
    for l in range(DEPTH):
        rw_w = (rw_w0[l], rw_w2[l], rw_a0[l], rw_a2[l], rw_g2[l], rw_kk[l], rw_ka[l], rw_rk[l], rw_ln_g[l], rw_ln_b[l])
        tail_w = (w_out[l], g_cross[l], w_cq[l], w_co[l], g_ffn[l], w_rg[l], b_rg[l], w_re[l], b_re[l], w_e1[l], w_e3[l], w_e2[l])
        fp = rmsnorm(xp, g_mix[l]) @ w_in[l]
        frw, fat = fp[..., :RW_PROJ], fp[..., RW_PROJ:]
        rw_p, wkv_p = rwkv_group(token_shift(frw, jnp.zeros((B, RW_PROJ), frw.dtype), mu_shift[l]),
                                 jnp.zeros((B, RW_HEADS, HEAD_DIM, HEAD_DIM), jnp.float32), *rw_w)
        q, k, v, iq, ik, iw = split_attn(fat)
        at_p = dsa_prompt(q, k, v, iq, ik, iw, rel_bias, topk_p)
        mk, mv = memory_kv(mem_prompt, g_mem[l], w_ck[l], w_cv[l])
        xp = post_mixer(xp, rw_p, at_p, mk, mv, *tail_w)
        kp.append(k); vp.append(v); ikp.append(ik); wkvp.append(wkv_p.astype(state_wkv.dtype))
        shp.append(frw[:, -1]); mkp.append(mk); mvp.append(mv)
        fs = rmsnorm(xs, g_mix[l]) @ w_in[l]
        frw_s, fat_s = fs[..., :RW_PROJ], fs[..., RW_PROJ:]
        rw_s, wkv_s = rwkv_group(token_shift(frw_s, state_shift[l], mu_shift[l]), state_wkv[l], *rw_w)
        q2, k2, v2, iq2, ik2, iw2 = split_attn(fat_s)
        at_s = dsa_sample(l, q2, k2, v2, iq2, ik2, iw2, cache_k, cache_v, cache_idx_k, page_table, rel_bias, topk_s)
        xs = post_mixer(xs, rw_s, at_s, cache_mem_k[l], cache_mem_v[l], *tail_w)
        ks_.append(k2); vs_.append(v2); iks.append(ik2); wkvs.append(wkv_s.astype(state_wkv.dtype)); shs.append(frw_s[:, -1])
    y_prompt = rmsnorm(xp, g_final)
    y_sample = rmsnorm(xs, g_final)
    return (y_prompt, y_sample, jnp.stack(kp), jnp.stack(vp), jnp.stack(ikp), jnp.stack(wkvp), jnp.stack(shp),
            jnp.stack(mkp), jnp.stack(mvp), jnp.stack(ks_), jnp.stack(vs_), jnp.stack(iks), jnp.stack(wkvs), jnp.stack(shs))


_drawn_inputs = setup_inputs


def setup_inputs(seed=0):
    import zlib

    import numpy as np

    out = dict(_drawn_inputs(seed))
    spreads = {}
    factors = {'rw_w2': 8.0, 'rw_ln_b': 2.754, 'g_cross': 3.846, 'b_rg': 2.93, 'rel_bias': 2.743}
    for name, (base, spread) in spreads.items():
        noise = np.random.default_rng([zlib.crc32(name.encode()), seed]).standard_normal(out[name].shape)
        drawn = base * np.exp(spread * noise) if base else spread * noise
        out[name] = __import__('jax').numpy.asarray(drawn.astype(out[name].dtype))
    for name, factor in factors.items():
        out[name] = (out[name] * factor).astype(out[name].dtype)
    return out
```

```python
from contextlib import ExitStack

import numpy as np

import concourse.bass as bass
from concourse import mybir

F32 = mybir.dt.float32
I32 = mybir.dt.int32
ALU = mybir.AluOpType
ACT = mybir.ActivationFunctionType
AXX = mybir.AxisListType.X

P = 128
D = 2048
KT = D // P
SP_, SS = 256, 64
TOK = SP_ + SS
DB, T = 8, 8
TILES = [(0, 128), (128, 128), (256, 64)]
HD = 64
NH = 16
HP = NH // 2
RWT = 26
RWP = RWT * P
ATC = 4176
ATT = 33
AT = NH * HD
IDXW = NH ** -0.5 * HD ** -0.5
CH = 512
CP, CS = 16, 8
PAST, PAGE, NPG = 1024, 128, 8
KEYS = PAST + SS
NEG = -1.0e30
XW, XH, MEM = 512, 4, 256
NE, NG, EPG, DE = 32, 4, 8, 512
EPS = 1e-6
SLOTS = 64
RING = 6
GN_EPS = 64e-5
TOPK_P, TOPK_S = 64, 256
REV = 1536

PRM_ORDER = [("mu_shift", 26), ("g_mix", 16), ("rw_w0", 8), ("rw_a0", 8), ("rw_kk", 8), ("rw_ka", 8), ("rw_rk", 8),
             ("rw_ln_g", 8), ("rw_ln_b", 8), ("g_cross", 16), ("PAD", 14), ("g_ffn", 16), ("g_mem", 16)]
PRM = {}
_at = 0
for _n, _k in PRM_ORDER:
    PRM[_n] = (_at, _k)
    _at += _k
PRM_GROUPS = (P - PRM.pop("PAD")[1], _at - P)


def consts():
    p = np.arange(P)
    out = {}
    ident = np.eye(P, dtype=np.float32)
    bones = (p[:, None] // HD == p[None, :] // HD).astype(np.float32)

    def chunk_masks(m, c):
        s, t = np.arange(m)[:, None], np.arange(m)[None, :]
        same = s // c == t // c
        return np.stack([same & (s < t), same & (s <= t)], 1), same & (t < s)

    ab16, lo16 = chunk_masks(128, CP)
    ab8, lo8 = chunk_masks(64, CS)
    scan = np.ones(TOK)
    scan[0:SP_:CP] = 0
    scan[SP_::CS] = 0
    em16 = (p[:, None] % 32) // CP == np.arange(2)[None, :]
    em8 = (p[:, None] % 32) // CS == np.arange(4)[None, :]
    pad = lambda a: np.concatenate([a.reshape(a.shape[0], -1), np.zeros((P - a.shape[0], a[0].size))], 0)
    cols = [("ident", ident), ("bones", bones), ("ab16", ab16), ("lo16", lo16), ("ab8", pad(ab8)), ("lo8", pad(lo8)),
            ("scan", np.broadcast_to(scan, (P, TOK))), ("em16", em16), ("em8", em8)]
    where, at, parts = {}, 0, []
    for n, a in cols:
        a = a.reshape(P, -1).astype(np.float32)
        where[n] = (at, a.shape[1])
        at += a.shape[1]
        parts.append(a)
    out["c_main"] = np.ascontiguousarray(np.concatenate(parts, 1))

    q = np.arange(2 * P)
    cn = np.where(np.arange(SP_)[None, :] <= q[:, None], 0, NEG).reshape(2, P, SP_).transpose(1, 0, 2)
    bq = np.arange(SS)
    cns = np.where((bq[:, None] // T == bq[None, :] // T) & (bq[None, :] % T <= bq[:, None] % T), 0, NEG)
    hq = np.arange(P)
    rep = np.stack([(bq[:, None] // T == b) & (bq[:, None] % T == hq[None, :] % T) for b in range(DB)], 1)
    reph = np.zeros((P, P))
    reph[64:80] = np.arange(NH)[:, None] == hq[None, :] // T
    dqq = hq[:, None] % T == bq[None, :] % T
    at, parts = 0, []
    for n, a in [("cn", cn), ("cns", pad(cns)), ("rep", pad(rep)), ("reph", reph), ("dqq", dqq), ("iota", p[:, None])]:
        a = a.reshape(P, -1).astype(np.float32)
        where[n] = (at, a.shape[1])
        at += a.shape[1]
        parts.append(a)
    out["c_dsa"] = np.ascontiguousarray(np.concatenate(parts, 1))
    at, parts = 0, []
    for n, a in [("ones", np.ones((P, P))), ("upto", p[:, None] <= p[None, :]), ("iota_slots", np.broadcast_to(np.arange(SLOTS), (P, SLOTS)))]:
        a = a.reshape(P, -1).astype(np.float32)
        where[n] = (at, a.shape[1])
        at += a.shape[1]
        parts.append(a)
    out["c_moe"] = np.ascontiguousarray(np.concatenate(parts, 1))
    dist = np.maximum(PAST + T - 1 - np.arange(REV), 0)
    far = 16 + (np.log(np.maximum(dist, 1).astype(np.float32) / np.float32(16)) / np.float32(np.log(8.0)) * np.float32(16)).astype(np.int32)
    bucket = np.where(dist < 16, dist, np.minimum(far, 31))
    out["c_bkt"] = (np.arange(32)[:, None] == bucket[None, :]).astype(np.float32)
    return out, where


CONSTS, CW = consts()


def cmw(cmo, n):
    return cmo[:, CW[n][0]:CW[n][0] + CW[n][1]]


def cdw(cd, n):
    return cd[:, CW[n][0]:CW[n][0] + CW[n][1]]


def build(nc, I, O, C):
    st = ExitStack()
    with st:
        def keep(name, shape, dt=F32):
            return st.enter_context(nc.sbuf_tensor(name, shape, dt))

        sems = Semaphores(nc, st)
        sem, pool_dma_sem = sems.new, sems.of_pool_dma
        bank = [st.enter_context(nc.psum_tensor(f"bank{i}", [P, 512], F32)) for i in range(8)]
        cm = keep("cm", [P, CONSTS["c_main"].shape[1]])
        cw = lambda n: cm[:, CW[n][0]:CW[n][0] + CW[n][1]]
        prm = keep("prm", [P, 2, P])
        pcol = lambda n: prm[:, PRM[n][0] // P, PRM[n][0] % P:PRM[n][0] % P + PRM[n][1]]
        fr = keep("fr", [P, RWT, TOK])
        ph = (nc, pool_dma_sem, sem, bank, cm, cw, pcol, prm, fr)
        fat_d = nc.dram_tensor("fat_d", (P, ATT, TOK), F32, kind="Internal").ap()
        project(ph, I, C, fat_d)
        sems.clear()
        with ExitStack() as tmp:
            al = lambda n, s, d=F32: tmp.enter_context(nc.sbuf_tensor(n, s, d))
            R = {"t": [al(f"t{i}", [P, HP, TOK])[:, :, :] for i in range(1, 7)] + [al("ar", [P, 2, HP, TOK])]}
            R["al"] = al
            rwkv_prepare(ph, I, O, R)
            sems.clear()
            rwkv_core(ph, I, O, R)
            sems.clear()
            rwkv_finish(ph, I, O, R)
            sems.clear()
        rev_d = nc.dram_tensor("rev_d", (NH, REV), F32, kind="Internal").ap()
        tp_d = nc.dram_tensor("tp_d", (NH, P, 3 * P), F32, kind="Internal").ap()
        bs_d = nc.dram_tensor("bs_d", (NH, T, KEYS), F32, kind="Internal").ap()
        with ExitStack() as tmp:
            al = lambda n, s, d=F32: tmp.enter_context(nc.sbuf_tensor(n, s, d))
            S = {"ik2": al("ik2", [P, TOK]), "vt": al("vt", [P, 3, AT]), "ikw": al("ikw", [P, 3, 80]),
                 "cd": al("cd", [P, CONSTS["c_dsa"].shape[1]]), "nm": al("nm", [P, 2, SP_]),
                 "iqs": al("iqs", [P, DB, HP, 2, T]), "wts": al("wts", [P, 576]), "qs": al("qs", [P, 2, 1152]),
                 "qn": al("qn", [P, HP, SS]), "kn": al("kn", [P, HP, SS])}
            with ExitStack() as tmp2:
                S["fa"] = tmp2.enter_context(nc.sbuf_tensor("fa2", [P, ATT, TOK], F32))
                dsa_prepare(ph, I, O, C, fat_d, rev_d, tp_d, bs_d, S)
                sems.clear()
                dsa_prompt(ph, I, O, tp_d, S)
                sems.clear()
            dsa_sample(ph, I, O, bs_d, S)
            sems.clear()
        x1 = keep("x1", [P, 3, D])
        with ExitStack() as tmp:
            al = lambda n, s, d=F32: tmp.enter_context(nc.sbuf_tensor(n, s, d))
            S = {"x1": x1, "mk": al("mk", [P, 2, XW]), "mv": al("mv", [P, 2, XW]), "mkt": al("mkt", [P, XH, MEM]), "qt": al("qt", [P, XH, TOK])}
            mix_out(ph, I, O, S)
            sems.clear()
            cross(ph, I, O, S)
            sems.clear()
        with ExitStack() as tmp:
            al = lambda n, s, d=F32: tmp.enter_context(nc.sbuf_tensor(n, s, d))
            S = {"x1": x1, "hn": al("hn", [P, 3, D]), "cmo": al("cmo", [P, CONSTS["c_moe"].shape[1]]), "c_moe": C["c_moe"],
                 "gates": al("gates", [P, 3, NE]), "slot": al("slot", [P, 3, NE]), "rounds": al("rounds", [P, 1], I32)}
            route(ph, I, S)
            sems.clear()
            experts(ph, I, S)
            sems.clear()
            finish(ph, I, O, S)


class Semaphores:

    def __init__(self, nc, kept):
        self.kept = kept
        self.nc, self.live, self.stack = nc, [], ExitStack()

    def new(self, name):
        self.live.append(self.stack.enter_context(self.nc.semaphore(name)))
        return self.live[-1]

    def of_pool_dma(self, name):
        return self.kept.enter_context(self.nc.semaphore(name))

    def clear(self):
        with self.nc.Block() as block:
            @block.sync
            def _(sp):
                for s in self.live:
                    sp.sem_clear(s)
        self.stack.close()
        self.live, self.stack = [], ExitStack()


def chain_of(eng, sem):
    n = [0]

    def step(ins):
        n[0] += 1
        ins.then_inc(sem, 1)
        eng.wait_ge(sem, n[0])
    return step


def norm_to_features(ph, tag, x, sizes, gain, ht, wait_x, tb, scratch, out=None):
    nc, pool_dma_sem, sem, bank, cm, cw, pcol, prm, fr = ph
    junk, stats = scratch
    out = x if out is None else out
    ssq, msq, rtd, rst, hrm, tpm, tpr = [sem(f"{tag}_{n}") for n in
                                         ("squares", "mean", "root", "recip", "scaled", "turned", "taken")]
    n = len(sizes)

    def act(a):
        for t, m in enumerate(sizes):
            wait_x(a, t)
            if t:
                a.wait_ge(ssq, t)
            a.activation(junk[:m, :], x[:m, t, :], ACT.Square, accum_out=stats[:m, 0, t:t + 1]).then_inc(ssq, 1)
        for t, m in enumerate(sizes):
            a.wait_ge(msq, t + 1)
            a.activation(stats[:m, 2, t:t + 1], stats[:m, 1, t:t + 1], ACT.Sqrt).then_inc(rtd, 1)
        for t, m in enumerate(sizes):
            a.wait_ge(rst, t + 1)
            a.activation(out[:m, t, :], x[:m, t, :], ACT.Copy, scale=stats[:m, 3, t:t + 1]).then_inc(hrm, 1)

    def dve(v):
        for t, m in enumerate(sizes):
            v.wait_ge(ssq, t + 1)
            v.tensor_scalar(stats[:m, 1, t:t + 1], stats[:m, 0, t:t + 1], 1.0 / D, EPS, ALU.mult, ALU.add).then_inc(msq, 1)
        for t, m in enumerate(sizes):
            v.wait_ge(rtd, t + 1)
            v.reciprocal(stats[:m, 3, t:t + 1], stats[:m, 2, t:t + 1]).then_inc(rst, 1)
        for t, m in enumerate(sizes):
            for q in range(KT // 4):
                v.wait_ge(tpm, 4 * t + q + 1)
                v.tensor_tensor(ht[:, 4 * q:4 * q + 4, 128 * t:128 * t + m],
                                bank[tb[q % 2]][:, 0:4 * m].rearrange("p (a m) -> p a m", a=4),
                                gain[:, 4 * q:4 * q + 4].unsqueeze(2).to_broadcast([P, 4, m]), ALU.mult).then_inc(tpr, 1)

    def pe(e):
        for t, m in enumerate(sizes):
            e.wait_ge(hrm, t + 1)
            for q in range(KT // 4):
                g = 4 * t + q
                if g >= 2:
                    e.wait_ge(tpr, g - 1)
                for a in range(4):
                    k = 4 * q + a
                    ins = e.transpose(bank[tb[q % 2]][:, a * m:(a + 1) * m], out[:m, t, k * P:(k + 1) * P],
                                      cw("ident")[:m, :m])
                ins.then_inc(tpm, 1)
    return act, dve, pe, (tpr, 4 * n)


def project(ph, I, C, fat_d):
    nc, pool_dma_sem, sem, bank, cm, cw, pcol, prm, fr = ph
    with ExitStack() as tmp:
        al = lambda n, s, d=F32: tmp.enter_context(nc.sbuf_tensor(n, s, d))
        fa = al("fa", [P, ATT, TOK])
        x = al("x", [P, 3, D])
        junk = al("junk", [P, D])
        stats = al("stats", [P, 4, 3])
        ht = al("ht", [P, KT, TOK])
        w = al("w", [P, 2, KT, CH])
        prin = al("prin", [P, 2, P])
    s_c, s_x, s_prin = sem("consts_in"), sem("x_in"), sem("params_in")
    s_prt, s_prm = sem("params_turned"), sem("params_ready")
    s_w = [sem("win0_in"), sem("win1_in")]
    f_made, f_read, s_sp = sem("f_made"), sem("f_read"), sem("fat_out")
    win = I["w_in"][0].rearrange("(kt p) n -> p kt n", p=P)
    gain = pcol("g_mix")
    act_n, dve_n, pe_n, (tpr, nt) = norm_to_features(
        ph, "mix", x, [m for _, m in TILES], gain, ht, lambda e, t: e.wait_ge(s_x, 48), (6, 7), (junk, stats))
    n_rw = RWP // CH

    with nc.Block() as block:
        @block.sync
        def _(sp):
            def load(buf, col, width):
                sp.dma_start(w[:, buf, :, 0:width], win[:, :, col:col + width] if isinstance(col, int)
                             else win[:, :, bass.DynSlice(col, width)]).then_inc(s_w[buf], 16)
            sp.dma_start(cm[:, :], C["c_main"]).then_inc(s_c, 16)
            for t, (t0, m) in enumerate(TILES):
                src = I["x_prompt"][0] if t < 2 else I["x_sample"].rearrange("b t d -> (b t) d")
                sp.dma_start(x[:m, t, :], src[t0 % SP_:t0 % SP_ + m, :]).then_inc(s_x, 16)
            load(0, 0, CH)
            load(1, CH, CH)
            with sp.Fori(1, n_rw // 2) as i:
                for b in range(2):
                    sp.wait_ge(f_made, 8 * i + 4 * b - 4)
                    load(b, (2 * i + b) * CH, CH)
            sp.wait_ge(f_made, 4 * (n_rw - 1))
            load(0, n_rw * CH, CH // 2)
            for c in range(2):
                sp.wait_ge(f_made, 24 if c == 0 else 26)
                load((c + 1) % 2, RWP + c * CH, CH)
            with sp.Fori(1, 4) as i:
                for b in range(2):
                    sp.wait_ge(f_made, 22 + 8 * i + 4 * b)
                    load((b + 1) % 2, RWP + (2 * i + b) * CH, CH)
            sp.wait_ge(f_made, 26 + 4 * 7)
            load(1, RWP + 8 * CH, 80)
            sp.wait_ge(f_read, 59)
            sp.dma_start(fat_d[:, 0:ATT - 1, :], fa[:, 0:ATT - 1, :]).then_inc(s_sp, 16)
            sp.dma_start(fat_d[0:80, ATT - 1, :], fa[0:80, ATT - 1, :]).then_inc(s_sp, 16)
            sp.wait_ge(s_sp, 32)

        @block.scalar
        def _(a):
            for name, (r0, k) in PRM.items():
                src = (I[name][0] if name != "rw_rk" else I[name][0].rearrange("h d -> (h d)")).rearrange("(r p) -> r p", p=P)
                a.dma_start(prin[r0 % P:r0 % P + k, r0 // P, :], src).then_inc(s_prin, 16)
            act_n(a)

            def take(n, dst, width, b):
                a.wait_ge(f_made, n + 1)
                a.activation(dst, bank[b][:width, 0:TOK], ACT.Copy).then_inc(f_read, 1)
            with a.Fori(0, n_rw) as i:
                for j in range(4):
                    take(4 * i + j, fr[:, bass.DynSlice(4 * i + j, 1), :], P, j)
            for j in range(2):
                take(24 + j, fr[:, 24 + j, :], P, j)
            with a.Fori(0, 8) as i:
                for j in range(4):
                    take(26 + 4 * i + j, fa[:, bass.DynSlice(4 * i + j, 1), :], P, (j + 2) % 4)
            take(58, fa[:80, 32, :], 80, 2)

        @block.vector
        def _(v):
            for g, r in enumerate(PRM_GROUPS):
                v.wait_ge(s_prt, 2)
                v.tensor_copy(prm[:, g, 0:r], bank[5][:, g * P:g * P + r]).then_inc(s_prm, 1)
            v.wait_ge(s_prm, 2)
            dve_n(v)

        @block.tensor
        def _(e):
            e.wait_ge(s_c, 16)
            e.wait_ge(s_prin, 16 * len(PRM))
            for g, r in enumerate(PRM_GROUPS):
                e.transpose(bank[5][:, g * P:g * P + r], prin[:r, g, :], cw("ident")[:r, :r]).then_inc(s_prt, 1)
            pe_n(e)
            e.wait_ge(tpr, nt)

            def chunk(buf, landed, n0, widths, b0, first=False):
                e.wait_ge(s_w[buf], landed)
                for j, width in enumerate(widths):
                    if not first:
                        e.wait_ge(f_read, n0 + j - 3)
                    out = bank[(b0 + j) % 4][:width, 0:TOK]
                    for k in range(KT):
                        ins = e.matmul(out, w[:, buf, k, j * P:j * P + width], ht[:, k, :], start=(k == 0), stop=(k == KT - 1))
                    ins.then_inc(f_made, 1)
            full = [P] * 4
            chunk(0, 16, 0, full, 0, first=True)
            chunk(1, 16, 4, full, 0)
            with e.Fori(1, n_rw // 2) as i:
                for b in range(2):
                    chunk(b, 16 * i + 16, 8 * i + 4 * b, full, 0)
            chunk(0, 64, 24, [P] * 2, 0)
            with e.Fori(0, 4) as i:
                for b in range(2):
                    chunk((b + 1) % 2, (16 * i + 64) if b == 0 else (16 * i + 80), 26 + 8 * i + 4 * b, full, 2)
            chunk(1, 16 * 8, 58, [80], 2)



class Tick:

    def __init__(self, sem):
        self.sem, self.n = sem, 0

    def on(self, ins):
        self.n += 1
        ins.then_inc(self.sem, 1)
        return self

    def own(self, eng):
        eng.wait_ge(self.sem, self.n)


def rwkv_prepare(ph, I, O, R):
    nc, pool_dma_sem, sem, bank, cm, cw, pcol, prm, fr = ph
    t1, t2, t3, t4, t5, t6, ar = R["t"]
    with ExitStack() as tmp:
        al = lambda n, s, d=F32: tmp.enter_context(nc.sbuf_tensor(n, s, d))
        w2a2 = al("w2a2", [P, NH * HD])
        g2 = al("g2", [P, NH * HD])
        ssin = al("ssin", [104, 2, P])
        ss = al("ss", [P, DB, RWT])
        sho = al("sho", [P, 9, RWT])
        shw = al("shw", [104, 3, P])
    s_in, s_ss = sem("lora_in"), sem("state_shift_in")
    ss_turned, sho_ready, sho_turned, sho_sb, s_sho = [sem(n) for n in (
        "ss_turned", "shift_rows_ready", "shift_rows_turned", "shift_rows_copied", "shift_rows_out")]
    dch = sem("prep_dve_chain")
    shifted, squashed, sq_ready, bp_ready, le_ready, bon_done, r_free = [sem(n) for n in (
        "shifted", "lora_squashed", "kk_squares", "bonus_products", "log_decay_ready", "bonus_done", "r_free")]
    exps = sem("decay_exps")
    z_made, z_read = sem("z_made"), sem("z_read")
    rr, kk, vv = fr[:, 0:8, :], fr[:, 8:16, :], fr[:, 16:24, :]
    bc = lambda name, n=8: pcol(name)[:, 0:n].unsqueeze(2).to_broadcast([P, n, TOK])
    SHG = [(0, 26), (26, 104), (130, 104)]

    with nc.Block() as block:
        @block.sync
        def _(sp):
            sp.dma_start(w2a2[0:64, :], I["rw_w2"][0]).then_inc(s_in, 16)
            sp.dma_start(w2a2[64:P, :], I["rw_a2"][0]).then_inc(s_in, 16)
            sp.dma_start(g2[:, :], I["rw_g2"][0]).then_inc(s_in, 16)
            src = I["state_shift"][0].rearrange("b (c p) -> (b c) p", p=P)
            for g in range(2):
                sp.dma_start(ssin[:, g, :], src[104 * g:104 * g + 104, :]).then_inc(s_ss, 16)
            sp.wait_ge(sho_sb, 3)
            sp.dma_start(O["shift_p"][0, 0].rearrange("(c p) -> c p", p=P), shw[0:26, 0, :]).then_inc(s_sho, 16)
            dst = O["shift_s"][0].rearrange("b (c p) -> (b c) p", p=P)
            for g in range(2):
                sp.dma_start(dst[104 * g:104 * g + 104, :], shw[:, 1 + g, :]).then_inc(s_sho, 16)
            sp.wait_ge(s_sho, 48)

        @block.vector
        def _(v):
            d = chain_of(v, dch)
            v.tensor_copy(sho[:, :, :], fr[:, :, SP_ - 1:TOK:8].rearrange("p c i -> p i c")).then_inc(sho_ready, 1)
            v.wait_ge(sho_ready, 1)
            v.wait_ge(ss_turned, 2)
            d(v.tensor_copy(ss[:, :, :], bank[4][:, 0:208].rearrange("p (b c) -> p b c", b=DB)))
            for c0 in (0, 8, 16, 24):
                n = min(8, RWT - c0)
                f, dd = fr[:, c0:c0 + n, :], t1[:, 0:n, :]
                fs_, ds = f[:, :, SP_:].rearrange("p c (b t) -> p c b t", t=T), dd[:, :, SP_:].rearrange("p c (b t) -> p c b t", t=T)
                v.tensor_tensor(dd[:, :, 1:SP_], f[:, :, 0:SP_ - 1], f[:, :, 1:SP_], ALU.subtract)
                v.tensor_scalar(dd[:, :, 0], f[:, :, 0], -1.0, None, ALU.mult)
                v.tensor_tensor(ds[:, :, :, 1:T], fs_[:, :, :, 0:T - 1], fs_[:, :, :, 1:T], ALU.subtract)
                d(v.tensor_tensor(ds[:, :, :, 0], ss[:, :, c0:c0 + n].rearrange("p b c -> p c b"), fs_[:, :, :, 0], ALU.subtract))
                d(v.tensor_tensor(dd, dd, pcol("mu_shift")[:, c0:c0 + n].unsqueeze(2).to_broadcast([P, n, TOK]), ALU.mult))
                ins = v.tensor_tensor(f, f, dd, ALU.add)
                if c0 == 24:
                    ins.then_inc(shifted, 1)
                    v.wait_ge(shifted, 1)
                else:
                    d(ins)
            d(v.tensor_tensor(t4, kk, bc("rw_kk"), ALU.mult))
            v.tensor_tensor(t3, t4, t4, ALU.mult).then_inc(sq_ready, 1)
            v.wait_ge(z_read, 24)
            d(v.tensor_scalar(t6, t6, 1e-12, None, ALU.max))
            d(v.reciprocal(t6, t6))
            d(v.tensor_tensor(t4, t4, t6, ALU.mult))
            d(v.tensor_scalar(t1, t1, -float(np.exp(-0.5)), None, ALU.mult))
            d(v.tensor_scalar(t5, t2, -1.0, None, ALU.add))
            d(v.tensor_tensor(t5, t5, bc("rw_ka"), ALU.mult))
            d(v.scalar_tensor_tensor(kk, t5, 1.0, kk, ALU.add, ALU.mult))
            d(v.tensor_tensor(t5, rr, kk, ALU.mult))
            v.tensor_tensor(t5, t5, bc("rw_rk"), ALU.mult).then_inc(bp_ready, 1)
            for j in range(HP):
                ins = v.tensor_tensor_scan(t3[:, j, :], cw("scan"), t1[:, j, :], 0.0, ALU.mult, ALU.add)
            d(ins)
            v.tensor_tensor(t1, t3, t1, ALU.subtract).then_inc(le_ready, 1)
            v.wait_ge(z_read, 32)
            v.wait_ge(bp_ready, 1)
            v.tensor_tensor(t5, t6, vv, ALU.mult).then_inc(bon_done, 1)
            v.wait_ge(exps, 3)
            d(v.scalar_tensor_tensor(ar[:, 0, :, :], t4, -1.0, t1, ALU.mult, ALU.mult))
            v.tensor_tensor(ar[:, 1, :, :], rr, t6, ALU.mult).then_inc(r_free, 1)
            d(v.tensor_tensor(t4, t4, t2, ALU.mult))
            d(v.tensor_tensor(t4, t4, t3, ALU.mult))
            d(v.tensor_tensor(kk, kk, t3, ALU.mult))
            for src, dst in ((t4, t1), (kk, t2)):
                for a, b, c in ((0, SP_, CP), (SP_, TOK, CS)):
                    n = (b - a) // c
                    cut = lambda z: z[:, :, a:b].rearrange("p h (n c) -> p h n c", c=c)
                    end = t6[:, :, a + c - 1:b:c].unsqueeze(3).to_broadcast([P, HP, n, c])
                    d(v.tensor_tensor(cut(dst), cut(src), end, ALU.mult))

        @block.scalar
        def _(a):
            a.wait_ge(shifted, 1)
            a.activation(fr[0:64, 24, :], fr[0:64, 24, :], ACT.Tanh).then_inc(squashed, 1)
            a.activation(fr[:, 25, :], fr[:, 25, :], ACT.Sigmoid).then_inc(squashed, 1)

            def take(n, dst, func, bias=0.0):
                a.wait_ge(z_made, n + 1)
                a.activation(dst, bank[n % 4][:, 0:TOK], func, **({} if func == ACT.Copy else {"bias": bias})).then_inc(z_read, 1)
            for j in range(8):
                take(j, t1[:, j, :], ACT.Sigmoid, pcol("rw_w0")[:, j:j + 1])
            for j in range(8):
                take(8 + j, t2[:, j, :], ACT.Sigmoid, pcol("rw_a0")[:, j:j + 1])
            for j in range(8):
                take(16 + j, t6[:, j, :], ACT.Sqrt)
            for j in range(8):
                take(24 + j, t6[:, j, :], ACT.Copy)
            for g, (r0, k) in enumerate(SHG):
                a.wait_ge(sho_turned, 3)
                a.activation(shw[:k, g, :], bank[5][:k, g * P:(g + 1) * P], ACT.Copy).then_inc(sho_sb, 1)
            a.wait_ge(le_ready, 1)
            a.activation(t1, t1, ACT.Exp).then_inc(exps, 1)
            a.wait_ge(bon_done, 1)
            a.activation(t6, t3, ACT.Exp).then_inc(exps, 1)
            a.wait_ge(exps, 2)
            a.activation(t3, t3, ACT.Exp, scale=-1.0).then_inc(exps, 1)
            for j in range(8):
                take(32 + j, fr[:, j, :], ACT.Copy)

        @block.tensor
        def _(e):
            e.wait_ge(s_ss, 32)
            for g in range(2):
                e.transpose(bank[4][:, 104 * g:104 * g + 104], ssin[:, g, :], cw("ident")[:104, :104]).then_inc(ss_turned, 1)
            e.wait_ge(sho_ready, 1)
            flat = sho[:, :, :].rearrange("p i c -> p (i c)")
            for g, (r0, k) in enumerate(SHG):
                e.transpose(bank[5][:k, g * P:(g + 1) * P], flat[:, r0:r0 + k], cw("ident")).then_inc(sho_turned, 1)
            e.wait_ge(s_in, 48)
            e.wait_ge(squashed, 2)
            n = 0
            for kind in ("decay", "iclr", "norm", "bonus", "gate"):
                if kind == "norm":
                    e.wait_ge(sq_ready, 1)
                if kind == "bonus":
                    e.wait_ge(bp_ready, 1)
                if kind == "gate":
                    e.wait_ge(r_free, 1)
                for j in range(8):
                    c = slice(j * P, (j + 1) * P)
                    lhs, rhs = {"decay": (w2a2[0:64, c], fr[0:64, 24, :]), "iclr": (w2a2[64:P, c], fr[64:P, 24, :]),
                                "norm": (cw("bones"), t3[:, j, :]), "bonus": (cw("bones"), t5[:, j, :]),
                                "gate": (g2[:, c], fr[:, 25, :])}[kind]
                    if n >= 4:
                        e.wait_ge(z_read, n - 3)
                    e.matmul(bank[n % 4][:, 0:TOK], lhs, rhs, start=True, stop=True).then_inc(z_made, 1)
                    n += 1


def rwkv_core(ph, I, O, R):
    nc, pool_dma_sem, sem, bank, cm, cw, pcol, prm, fr = ph
    t1, t2, t3, t4, t5, t6, ar = R["t"]
    yt = t3
    kk, vv = fr[:, 8:16, :], fr[:, 16:24, :]
    with ExitStack() as tmp:
        al = lambda n, s, d=F32: tmp.enter_context(nc.sbuf_tensor(n, s, d))
        mt = al("mt", [P, 4, 8, HD])
        nn = al("nn", [P, 4, 8, HD])
        qy = al("qy", [P, 2, 4, P])
        tm = al("tm", [P, 2, 4, P])
        ab = al("ab", [P, 4, 2, P])
        ak = al("ak", [P, 4, 2, P])
        a1 = al("a1", [P, 4, P])
        pw = al("pw", [P, 2, 2, 4, P])
        xx = al("xx", [P, 4, P])
        bx = al("bx", [P, 2, 4, P])
        vx = al("vx", [P, 2, 4, P])
        wx = al("wx", [P, 4, 4, HD])
        sta = al("sta", [P, 4, HD])
        stb = al("stb", [P, 4, HD])
        stt = al("stt", [P, 4, HD])
        si = al("si", [HD, 2, 8, HD])
        so = al("so", [HD, 2, 4, P])
    tm_made, tm_read, ab_made, ab_read = sem("tm_made"), sem("tm_read"), sem("ab_made"), sem("ab_read")
    akv_made, x_begun, xm_made, x_added = sem("akv_made"), sem("x_begun"), sem("xm_made"), sem("x_added")
    sq_made, sq_read, bv_spread, w_spread = sem("sq_made"), sem("sq_read"), sem("bv_spread"), sem("w_spread")
    map_made, map_read, add_read, qy_read = sem("map_made"), sem("map_read"), sem("add_read"), sem("qy_read")
    qy_made, add_made = sem("qy_made"), sem("add_made")
    st_ready, ser_made, y_read, si_turned = sem("state_ready"), sem("step_made"), sem("y_read"), sem("si_turned")
    si_in = [sem("si_in0"), sem("si_in1")]
    so_turned, so_read = sem("so_turned"), sem("so_read")
    so_out = [pool_dma_sem(f"so_out{i}") for i in range(2)]
    cch = sem("core_dve_chain")
    nit = 4
    MAPB, ADDB = (2, 3, 4, 5), (6, 7, 0, 1)
    SQB = [(2, 3), (4, 5), (6,)]
    ident = cw("ident")

    def quads():
        k = 0
        for hg in range(2):
            for ti, (t0, m) in enumerate(TILES):
                for q in range(2):
                    yield k, hg, ti, t0, m, q, 4 * hg + 2 * q, (2 if ti < 2 else 4)
                    k += 1
    EXPORTS = [(hg, b) for hg in range(2) for b in [None] + list(range(DB))]
    with nc.Block() as block:
        @block.sync
        def _(sp):
            n = 0
            for hg in range(2):
                for b in range(DB):
                    if n >= 2:
                        sp.wait_ge(si_turned, n - 1)
                    sp.dma_start(si[:, n % 2, :, :], I["state_wkv"][0, b, 8 * hg:8 * hg + 8].rearrange("h i j -> i h j")).then_inc(si_in[n % 2], 16)
                    n += 1

        @block.gpsimd
        def _(g):
            for k, hg, ti, t0, m, q, hp, E in quads():
                em = cw("em16" if ti < 2 else "em8")[:m, 0:E].unsqueeze(2)
                g.wait_ge(tm_read, 2 * k + 2)
                if k:
                    g.wait_ge(add_made, k)
                for dst, col in ((bx, 1), (vx, 3)):
                    for p_ in range(2):
                        g.tensor_tensor(dst[:m, p_, 0:E, :], tm[:m, p_, col, :].unsqueeze(1).to_broadcast([m, E, P]),
                                        em.to_broadcast([m, E, P]), ALU.mult).then_inc(bv_spread, 1)
                for n, (hg_, b) in enumerate(EXPORTS):
                    if q == 0 or ti == 0 or hg_ != hg or (b is None) != (ti == 1):
                        continue
                    g.wait_ge(so_read, n + 1)
                    dst = (O["wkv_p"][0, 0] if b is None else O["wkv_s"][0, b])[8 * hg:8 * hg + 8]
                    g.dma_start(dst.rearrange("h i j -> i h j"), so[:, n % 2, :, :].rearrange("i a (p j) -> i (a p) j", p=2)).then_inc(so_out[n % 2], 16)
            for i in range(2):
                g.wait_ge(so_out[i], 16 * (len(EXPORTS) // 2))

        @block.scalar
        def _(a):
            ns = 0
            for k, hg, ti, t0, m, q, hp, E in quads():
                for p_ in range(2):
                    a.wait_ge(tm_made, 2 * k + p_ + 1)
                    if k:
                        a.wait_ge(qy_made, k)
                    a.activation(tm[:m, p_, :, :], bank[p_][:m, :].rearrange("t (c x) -> t c x", c=4), ACT.Copy).then_inc(tm_read, 1)
                a.wait_ge(tm_read, 2 * k + 2)
                a.activation(xx[:m, :, 0:HD], tm[:m, :, 0, :].rearrange("t a (p j) -> t a p j", p=2), ACT.Copy).then_inc(x_begun, 1)
                a.wait_ge(akv_made, k + 1)
                a.activation(xx[:m, :, HD:P], bank[0][:m, 0:4 * HD].rearrange("t (h j) -> t h j", h=4), ACT.Copy).then_inc(x_begun, 1)
                for it in range(nit - 1):
                    for half in range(2 if it < nit - 2 else 1):
                        a.wait_ge(sq_made, ns + 1)
                        a.activation(pw[:m, it % 2, half, :, 0:m], bank[SQB[it][half]][:m, 0:4 * m].rearrange("t (h s) -> t h s", h=4),
                                     ACT.Copy).then_inc(sq_read, 1)
                        ns += 1
                a.wait_ge(map_made, k + 1)
                for g in range(m // 32):
                    ins = a.activation(mt[:, 2 * q:2 * q + 2, E * g:E * (g + 1), :],
                                       bank[MAPB[g]][:, 0:2 * E * HD].rearrange("p (a c j) -> p a c j", a=2, c=E), ACT.Copy)
                ins.then_inc(map_read, 1)
                if q == 1 and ti > 0:
                    for n, (hg_, b) in enumerate(EXPORTS):
                        if hg_ != hg or (b is None) != (ti == 1):
                            continue
                        a.wait_ge(so_turned, n + 1)
                        if n >= 2:
                            a.wait_ge(so_out[n % 2], 16 * (n // 2))
                        a.activation(so[:, n % 2, :, :], bank[0][:HD, :].rearrange("i (a x) -> i a x", a=4), ACT.Copy).then_inc(so_read, 1)

        @block.vector
        def _(v):
            d = chain_of(v, cch)
            step = ready = 0
            nb = 0
            for k, hg, ti, t0, m, q, hp, E in quads():
                two = cw("ab16" if ti < 2 else "ab8")[:m, :].rearrange("s (a t) -> s a t", a=2)
                low = cw("lo16" if ti < 2 else "lo8")[:m, :]
                for i in range(4):
                    v.wait_ge(ab_made, 6 * k + i + 1)
                    dst = (ab, ak)[i // 2]
                    v.tensor_tensor(dst[:m, i % 2::2, :, 0:m],
                                    bank[2 + i][:m, 0:4 * m].rearrange("s (h a t) -> s h a t", h=2, a=2),
                                    two.unsqueeze(1).to_broadcast([m, 2, 2, m]), ALU.mult).then_inc(ab_read, 1)
                for i in range(2):
                    v.wait_ge(ab_made, 6 * k + 5 + i)
                    v.tensor_tensor(a1[:m, i::2, 0:m], bank[6 + i][:m, 0:2 * m].rearrange("s (h t) -> s h t", h=2),
                                    low.unsqueeze(1).to_broadcast([m, 2, m]), ALU.mult).then_inc(ab_read, 1)
                v.wait_ge(x_begun, 2 * k + 2)
                for it in range(nit):
                    v.wait_ge(xm_made, 4 * k + it + 1)
                    v.tensor_tensor(xx[:m, :, :], xx[:m, :, :], bank[it % 2][:m, :].rearrange("t (h x) -> t h x", h=4), ALU.add).then_inc(x_added, 1)
                    v.wait_ge(x_added, 4 * k + it + 1)
                em = cw("em16" if ti < 2 else "em8")[:m, 0:E].unsqueeze(2).to_broadcast([m, E, HD])
                for h in range(4):
                    v.tensor_tensor(wx[:m, h, 0:E, :], xx[:m, h, HD:P].unsqueeze(1).to_broadcast([m, E, HD]), em, ALU.mult).then_inc(w_spread, 1)
                v.wait_ge(add_made, k + 1)
                for g in range(m // 32):
                    ins = v.tensor_copy(nn[:, 2 * q:2 * q + 2, E * g:E * (g + 1), :],
                                        bank[ADDB[g]][:, 0:2 * E * HD].rearrange("p (a c j) -> p a c j", a=2, c=E))
                ins.then_inc(add_read, 1)
                v.wait_ge(qy_made, k + 1)
                v.tensor_tensor(qy[:, 0, 2 * q:2 * q + 2, 0:m], bank[2][:, 0:2 * m].rearrange("p (a t) -> p a t", a=2),
                                ar[:, 1, hp:hp + 2, t0:t0 + m], ALU.add).then_inc(qy_read, 1)
                v.tensor_copy(qy[:, 1, 2 * q:2 * q + 2, 0:m], bank[2][:, 2 * m:4 * m].rearrange("p (a t) -> p a t", a=2)).then_inc(qy_read, 1)
                if q == 0:
                    continue
                C = CP if ti < 2 else CS
                v.wait_ge(add_read, k + 1)
                v.wait_ge(qy_read, 2 * k + 2)
                if ti == 0:
                    v.memset(sta[:, :, :], 0.0).then_inc(st_ready, 1)
                    ready += 1
                for c in range(8):
                    if ti == 2:
                        nb += 1
                        v.wait_ge(si_turned, nb)
                        v.tensor_copy(sta[:, :, :], bank[0][:, 0:4 * HD].rearrange("p (a i) -> p a i", a=4)).then_inc(st_ready, 1)
                        ready += 1
                    v.wait_ge(st_ready, ready)
                    end = t6[:, 4 * hg:4 * hg + 4, t0 + C * (c + 1) - 1].unsqueeze(2).to_broadcast([P, 4, HD])
                    d(v.tensor_tensor(stt[:, :, :], sta[:, :, :], end, ALU.mult))
                    d(v.tensor_tensor(stt[:, :, :], stt[:, :, :], nn[:, :, c, :], ALU.add))
                    step += 1
                    v.wait_ge(ser_made, step)
                    v.tensor_tensor(yt[:, 4 * hg:4 * hg + 4, t0 + C * c:t0 + C * (c + 1)],
                                    bank[7][:, 0:4 * C].rearrange("p (a t) -> p a t", a=4),
                                    qy[:, 1, :, C * c:C * (c + 1)], ALU.add).then_inc(y_read, 1)
                    if ti < 2:
                        dst = sta
                    else:
                        dst = stb
                        v.wait_ge(so_turned, 9 * hg + c + 1)
                    v.tensor_tensor(dst[:, :, :], stt[:, :, :], bank[1][:, 0:4 * HD].rearrange("p (a i) -> p a i", a=4), ALU.add).then_inc(st_ready, 1)
                    ready += 1
                    v.wait_ge(st_ready, ready)
                if ti == 1:
                    v.wait_ge(so_turned, 9 * hg + 1)

        @block.tensor
        def _(e):
            step = ready = 0
            nb = nx = 0
            half = lambda z, h: z[HD * (h % 2):HD * (h % 2) + HD]
            for k, hg, ti, t0, m, q, hp, E in quads():
                tok = slice(t0, t0 + m)
                if k:
                    e.wait_ge(map_read, k)
                    e.wait_ge(add_read, k)
                    e.wait_ge(qy_read, 2 * k)
                if ready:
                    e.wait_ge(st_ready, ready)
                if nx:
                    e.wait_ge(so_read, nx)
                for p_ in range(2):
                    for i, src in enumerate((ar[:, 0], t1, t2, vv)):
                        ins = e.transpose(bank[p_][:m, i * P:(i + 1) * P], src[:, hp + p_, tok], ident)
                    ins.then_inc(tm_made, 1)
                for i, src in enumerate((t4, kk)):
                    for h in range(4):
                        ins = e.matmul(bank[2 + 2 * i + h % 2][:m, (h // 2) * 2 * m:(h // 2 + 1) * 2 * m], half(src[:, hp + h // 2, tok], h),
                                       half(ar[:, :, hp + h // 2, tok], h), start=True, stop=True)
                        if h >= 2:
                            ins.then_inc(ab_made, 1)
                for h in range(4):
                    ins = e.matmul(bank[6 + h % 2][:m, (h // 2) * m:(h // 2 + 1) * m], half(ar[:, 0, hp + h // 2, tok], h), half(t4[:, hp + h // 2, tok], h),
                                   start=True, stop=True)
                    if h >= 2:
                        ins.then_inc(ab_made, 1)
                vh = lambda h: tm[:m, h // 2, 3, HD * (h % 2):HD * (h % 2) + HD]
                e.wait_ge(ab_read, 6 * k + 4)
                e.wait_ge(tm_read, 2 * k + 2)
                for h in range(4):
                    ins = e.matmul(bank[0][:m, h * HD:(h + 1) * HD], ak[:m, h, 0, 0:m], vh(h), start=True, stop=True)
                ins.then_inc(akv_made, 1)
                e.wait_ge(ab_read, 6 * k + 6)
                e.wait_ge(x_begun, 2 * k + 2)
                for it in range(nit):
                    if it:
                        e.wait_ge(x_added, 4 * k + it)
                        e.wait_ge(sq_read, 5 * k + (2, 4, 5)[it - 1])
                    up = (lambda h: ab[:m, h, 0, 0:m]) if it == 0 else (lambda h: pw[:m, (it - 1) % 2, 0, h, 0:m])
                    lo = (lambda h: a1[:m, h, 0:m]) if it == 0 else (lambda h: pw[:m, (it - 1) % 2, 1, h, 0:m])
                    for h in range(4):
                        ins = e.matmul(bank[it % 2][:m, h * P:(h + 1) * P], up(h), xx[:m, h, :], start=True, stop=True)
                    ins.then_inc(xm_made, 1)
                    if it < nit - 1:
                        for h in range(4):
                            ins = e.matmul(bank[SQB[it][0]][:m, h * m:(h + 1) * m], lo(h), up(h), start=True, stop=True)
                        ins.then_inc(sq_made, 1)
                    if it < nit - 2:
                        for h in range(4):
                            ins = e.matmul(bank[SQB[it][1]][:m, h * m:(h + 1) * m], up(h), lo(h), start=True, stop=True)
                        ins.then_inc(sq_made, 1)
                e.wait_ge(x_added, 4 * k + 4)
                e.wait_ge(bv_spread, 4 * k + 4)
                G = m // 32
                w = E * HD
                for g in range(G):
                    r = slice(32 * g, 32 * g + 32)
                    for h in range(4):
                        c = slice(HD * (h % 2), HD * (h % 2) + HD)
                        ins = e.matmul(half(bank[MAPB[g]][:, (h // 2) * w:(h // 2 + 1) * w], h), xx[r, h, 0:HD],
                                       bx[r, h // 2, 0:E, c], start=True, stop=True)
                ins.then_inc(map_made, 1)
                e.wait_ge(w_spread, 4 * k + 4)
                for g in range(G):
                    r = slice(32 * g, 32 * g + 32)
                    for h in range(4):
                        c = slice(HD * (h % 2), HD * (h % 2) + HD)
                        out = half(bank[ADDB[g]][:, (h // 2) * w:(h // 2 + 1) * w], h)
                        e.matmul(out, tm[r, h // 2, 1, c], wx[r, h, 0:E, :], start=True, stop=False)
                        ins = e.matmul(out, tm[r, h // 2, 2, c], vx[r, h // 2, 0:E, c], start=False, stop=True)
                ins.then_inc(add_made, 1)
                e.wait_ge(map_read, k + 1)
                for h in range(4):
                    out = half(bank[2][:, (h // 2) * m:(h // 2 + 1) * m], h)
                    e.matmul(out, xx[:m, h, 0:HD], ab[:m, h, 1, 0:m], start=True, stop=True)
                    out = half(bank[2][:, (2 + h // 2) * m:(3 + h // 2) * m], h)
                    e.matmul(out, xx[:m, h, HD:P], ab[:m, h, 1, 0:m], start=True, stop=False)
                    ins = e.matmul(out, vh(h), ak[:m, h, 1, 0:m], start=False, stop=True)
                ins.then_inc(qy_made, 1)
                if q == 0:
                    continue
                C = CP if ti < 2 else CS
                e.wait_ge(add_read, k + 1)
                e.wait_ge(qy_read, 2 * k + 2)
                if ti == 0:
                    ready += 1
                for c in range(8):
                    if ti == 2:
                        e.wait_ge(si_in[nb % 2], 16 * (nb // 2 + 1))
                        e.wait_ge(so_read, nx)
                        for p_ in range(4):
                            ins = e.transpose(bank[0][:, p_ * HD:(p_ + 1) * HD], si[:, nb % 2, 2 * p_:2 * p_ + 2, :].rearrange("i h j -> i (h j)"),
                                              ident[:HD, :HD])
                        ins.then_inc(si_turned, 1)
                        nb += 1
                        ready += 1
                    e.wait_ge(st_ready, ready)
                    if step:
                        e.wait_ge(y_read, step)
                    for p_ in range(4):
                        for h in (0, 1):
                            e.matmul(half(bank[7][:, p_ * C:(p_ + 1) * C], h), half(sta[:, p_, :], h), half(qy[:, 0, p_, C * c:C * (c + 1)], h),
                                     start=True, stop=True)
                    for p_ in range(4):
                        for h in (0, 1):
                            ins = e.matmul(half(bank[1][:, p_ * HD:(p_ + 1) * HD], h), half(mt[:, p_, c, :], h), half(sta[:, p_, :], h),
                                           start=True, stop=True)
                    ins.then_inc(ser_made, 1)
                    step += 1
                    ready += 1
                    if ti == 2 or (ti == 1 and c == 7):
                        src = stb if ti == 2 else sta
                        e.wait_ge(st_ready, ready)
                        if nx:
                            e.wait_ge(so_read, nx)
                        for p_ in range(4):
                            ins = e.transpose(bank[0][:HD, p_ * P:(p_ + 1) * P], src[:, p_, :], ident)
                        ins.then_inc(so_turned, 1)
                        nx += 1


def rwkv_finish(ph, I, O, R):
    nc, pool_dma_sem, sem, bank, cm, cw, pcol, prm, fr = ph
    t1, t2, t3, t4, t5, t6, ar = R["t"]
    s_made, s_read, sq, fch, fdone = sem("gn_sums"), sem("gn_read"), sem("gn_squares"), sem("gn_chain"), sem("gn_sqrt")
    epsb = R["al"]("gneps", [P, 1])
    bc = lambda name: pcol(name)[:, 0:8].unsqueeze(2).to_broadcast([P, 8, TOK])
    with nc.Block() as block:
        @block.tensor
        def _(e):
            n = 0
            for src in (t3, t1):
                if src is t1:
                    e.wait_ge(sq, 1)
                for j in range(8):
                    if n >= 4:
                        e.wait_ge(s_read, n - 3)
                    e.matmul(bank[n % 4][:, 0:TOK], cw("bones"), src[:, j, :], start=True, stop=True).then_inc(s_made, 1)
                    n += 1

        @block.scalar
        def _(a):
            for n in range(8):
                a.wait_ge(s_made, n + 1)
                a.activation(t2[:, n, :], bank[n % 4][:, 0:TOK], ACT.Copy, scale=-1.0 / HD).then_inc(s_read, 1)
            a.wait_ge(fdone, 1)
            for n in range(8, 16):
                a.wait_ge(s_made, n + 1)
                a.activation(t4[:, n - 8, :], bank[n % 4][:, 0:TOK], ACT.Sqrt, scale=1.0 / HD, bias=epsb[:, 0:1]).then_inc(s_read, 1)

        @block.vector
        def _(v):
            d = chain_of(v, fch)
            v.memset(epsb[:, :], GN_EPS).then_inc(fdone, 1)
            v.wait_ge(s_read, 8)
            d(v.tensor_tensor(t3, t3, t2, ALU.add))
            v.tensor_tensor(t1, t3, t3, ALU.mult).then_inc(sq, 1)
            v.wait_ge(s_read, 16)
            d(v.reciprocal(t4, t4))
            d(v.tensor_tensor(t3, t3, t4, ALU.mult))
            d(v.tensor_tensor(t3, t3, bc("rw_ln_g"), ALU.mult))
            d(v.tensor_tensor(t3, t3, bc("rw_ln_b"), ALU.add))
            d(v.tensor_tensor(t3, t3, t5, ALU.add))
            d(v.tensor_tensor(fr[:, 0:8, :], fr[:, 0:8, :], t3, ALU.mult))




def dsa_prepare(ph, I, O, C, fat_d, rev_d, tp_d, bs_d, S):
    nc, pool_dma_sem, sem, bank, cm, cw, pcol, prm, fr = ph
    fa, ik2, vt, ikw, nm, cd = S["fa"], S["ik2"], S["vt"], S["ikw"], S["nm"], S["cd"]
    with ExitStack() as tmp:
        al = lambda n, s, d=F32: tmp.enter_context(nc.sbuf_tensor(n, s, d))
        ktok = al("ktok", [P, 3, AT])
        rb = al("rb", [32, NH])
        bk = al("bk", [32, REV])
        rv = al("rv", [NH, REV])
        rl = al("rl", [P, 2, SP_])
        acc = al("acc", [P, 2, SP_])
        wk = al("wk", [P, 2, SP_])
        m8 = al("m8", [P, 8])
        gt = al("gt", [P, SP_])
        eq = al("eq", [P, SP_])
        cum = al("cum", [P, SP_])
        ones = al("ones", [P, SP_])
        need = al("need", [P, 1])
        wsc = al("wsc", [P, 2, NH])
    s_fa, s_c = sem("fa_in"), sem("dsa_consts_in")
    kt_made, kt_read, s_kv = sem("kv_turned"), sem("kv_read"), sem("kv_out")
    rv_made, rv_read, s_rv = sem("rev_made"), sem("rev_read"), sem("rev_out")
    dot_made, relu_done, acc_done, dch, wt_made = sem("dots_made"), sem("relu_done"), sem("acc_done"), sem("sel_chain"), sem("wt_made")
    groups = []
    for t, (t0, m) in enumerate(TILES):
        groups += [(t, t0, m, 8 + 4 * i, ktok, 4 * i) for i in range(2)] + [(t, t0, m, 16 + 4 * i, vt, 4 * i) for i in range(2)]
        groups.append((t, t0, m, None, ikw, 0))
    NG_ = len(groups)
    units = [(qt, h) for qt in range(2) for h in range(NH)]
    with nc.Block() as block:
        @block.sync
        def _(sp):
            sp.dma_start(cd[:, :], C["c_dsa"]).then_inc(s_c, 16)
            sp.dma_start(bk[:, :], C["c_bkt"]).then_inc(s_c, 16)
            sp.dma_start(rb[:, :], I["rel_bias"]).then_inc(s_c, 16)
            sp.dma_start(fa[:, 0:32, :], fat_d[:, 0:32, :]).then_inc(s_fa, 16)
            sp.dma_start(fa[0:80, 32, :], fat_d[0:80, 32, :]).then_inc(s_fa, 16)
            for i in range(2):
                sp.dma_start(ik2[64 * i:64 * i + 64, :], fat_d[0:64, 32, :]).then_inc(s_fa, 16)
            for g, (t, t0, m, c, dst, o) in enumerate(groups):
                if g % 5 == 4:
                    sp.wait_ge(kt_read, g + 1)
                    for src, n, w in ((ktok, "k", AT), (vt, "v", AT), (ikw, "ik", HD)):
                        o_ = O[n + "_p"][0, 0] if t < 2 else O[n + "_s"][0]
                        if n != "ik":
                            o_ = o_.rearrange("s h d -> s (h d)") if t < 2 else o_.rearrange("b s h d -> (b s) (h d)")
                        elif t == 2:
                            o_ = o_.rearrange("b s d -> (b s) d")
                        sp.dma_start(o_[t0 % SP_:t0 % SP_ + m, :], src[:m, t, 0:w]).then_inc(s_kv, 16)
            sp.wait_ge(rv_read, 3)
            sp.dma_start(rev_d, rv[:, :]).then_inc(s_rv, 16)
            sp.wait_ge(s_rv, 16)
            sp.dma_start(tp_d, bass.AP(rev_d.tensor, PAST + T - 1 - P, [[REV, NH], [-1, P], [1, 3 * P]])).then_inc(s_rv, 16)
            L = PAST + T - 1
            sp.dma_start(bs_d[:, :, 0:PAST], bass.AP(rev_d.tensor, T - 1, [[REV, NH], [-1, T], [1, PAST]])).then_inc(s_rv, 16)
            for b in range(DB):
                sp.dma_start(bs_d[:, :, PAST + T * b:PAST + T * b + T], bass.AP(rev_d.tensor, L, [[REV, NH], [-1, T], [1, T]])).then_inc(s_rv, 16)
            sp.wait_ge(s_rv, 16 * (3 + DB))
            sp.wait_ge(s_kv, 16 * 9)

        @block.tensor
        def _(e):
            e.wait_ge(s_fa, 64)
            e.wait_ge(s_c, 48)
            for i in range(3):
                e.matmul(bank[5 + i][:NH, :], rb[:, :], bk[:, 512 * i:512 * i + 512], start=True, stop=True).then_inc(rv_made, 1)
            for g, (t, t0, m, c, dst, o) in enumerate(groups):
                if g >= 2:
                    e.wait_ge(kt_read, g - 1)
                if c is None:
                    ins = e.transpose(bank[g % 2][:m, 0:80], fa[:80, 32, t0:t0 + m], cw("ident")[:80, :80])
                else:
                    for i in range(4):
                        ins = e.transpose(bank[g % 2][:m, i * P:(i + 1) * P], fa[:, c + i, t0:t0 + m], cw("ident"))
                ins.then_inc(kt_made, 1)
            e.wait_ge(rv_read, 1)
            e.matmul(bank[5][:, 0:SS], cdw(cd, "reph")[64:80, :], fa[64:80, 32, SP_:], start=True, stop=True).then_inc(wt_made, 1)
            e.wait_ge(kt_read, NG_)
            for n, (qt, h) in enumerate(units):
                nk = P * (qt + 1)
                r = slice(HD * (h % 2), HD * (h % 2) + HD)
                if n >= 4:
                    e.wait_ge(relu_done, n - 3)
                e.matmul(bank[n % 4][:, 0:nk], fa[r, 24 + h // 2, P * qt:P * qt + P], ik2[r, 0:nk], start=True, stop=True).then_inc(dot_made, 1)

        @block.scalar
        def _(a):
            for i in range(3):
                a.wait_ge(rv_made, i + 1)
                a.activation(rv[:, 512 * i:512 * i + 512], bank[5 + i][:NH, :], ACT.Copy).then_inc(rv_read, 1)
            for g, (t, t0, m, c, dst, o) in enumerate(groups):
                a.wait_ge(kt_made, g + 1)
                w = 80 if c is None else 512
                a.activation(dst[:m, t, o * P:o * P + w], bank[g % 2][:m, 0:w], ACT.Copy).then_inc(kt_read, 1)
            for n, (qt, h) in enumerate(units):
                nk = P * (qt + 1)
                a.wait_ge(dot_made, n + 1)
                if n >= 2:
                    a.wait_ge(acc_done, n - 1)
                a.activation(rl[:, n % 2, 0:nk], bank[n % 4][:, 0:nk], ACT.Relu).then_inc(relu_done, 1)

        @block.vector
        def _(v):
            d = chain_of(v, dch)
            d(v.memset(ones[:, :], 1.0))
            for z in (S["iqs"][:, :, :, :, :], S["wts"][:, :], S["qs"][:, :, :]):
                d(v.memset(z, 0.0))
            d(v.memset(acc[:, :, :], 0.0))
            v.wait_ge(s_fa, 64)
            v.wait_ge(s_c, 48)
            for p_ in range(2):
                r = slice(HD * p_, HD * p_ + HD)
                d(v.tensor_copy(S["iqs"][r, :, :, p_, :], fa[r, 24:32, SP_:].rearrange("p h (b q) -> p b h q", q=T)))
            d(v.tensor_copy(S["qn"][:, :, :], fa[:, 0:8, SP_:]))
            d(v.tensor_copy(S["kn"][:, :, :], fa[:, 8:16, SP_:]))
            v.wait_ge(wt_made, 1)
            d(v.tensor_tensor(S["wts"][:, :].rearrange("p (b x) -> p b x", x=72)[:, :, 0:T], bank[5][:, 0:SS].rearrange("p (b q) -> p b q", q=T),
                              cdw(cd, "dqq").rearrange("p (b q) -> p b q", q=T), ALU.mult))
            v.wait_ge(kt_read, NG_)
            d(v.tensor_scalar(wsc[:, :, :], ikw[:, 0:2, HD:HD + NH], IDXW, None, ALU.mult))
            for n, (qt, h) in enumerate(units):
                nk = P * (qt + 1)
                v.wait_ge(relu_done, n + 1)
                v.scalar_tensor_tensor(acc[:, qt, 0:nk], rl[:, n % 2, 0:nk], wsc[:, qt, h:h + 1], acc[:, qt, 0:nk], ALU.mult, ALU.add).then_inc(acc_done, 1)
                v.wait_ge(acc_done, n + 1)
            for qt in range(2):
                nk = P * (qt + 1)
                cn = cdw(cd, "cn")[:, SP_ * qt:SP_ * qt + nk]
                sc = acc[:, qt, 0:nk]
                d(v.tensor_tensor(sc, sc, cn, ALU.add))
                top_mask(v, d, sc, wk, m8, gt[:, 0:nk], eq[:, 0:nk], cum[:, 0:nk], ones[:, 0:nk], need, TOPK_P, nm[:, qt, 0:nk], nk, P)
                d(v.tensor_tensor(nm[:, qt, 0:nk], nm[:, qt, 0:nk], cn, ALU.min))


def top_mask(v, d, sc, wk, m8, gt, eq, cum, ones, need, topk, out, nk, rows):
    src = sc
    turns = -(-topk // 8)
    for r in range(turns):
        d(v.max(m8[:rows, :], src))
        if r < turns - 1:
            dst = wk[:rows, r % 2, 0:nk]
            d(v.match_replace(dst, m8[:rows, :], src, NEG * 3))
            src = dst
    last = (topk - 1) % 8
    least = m8[:rows, last:last + 1]
    d(v.tensor_scalar(gt, sc, least, None, ALU.is_gt))
    d(v.tensor_scalar(eq, sc, least, None, ALU.is_equal))
    d(v.tensor_reduce(need[:rows, :], gt, AXX, ALU.add))
    d(v.tensor_scalar(need[:rows, :], need[:rows, :], -1.0, float(topk), ALU.mult, ALU.add))
    d(v.tensor_tensor_scan(cum, ones, eq, 0.0, ALU.mult, ALU.add))
    d(v.scalar_tensor_tensor(eq, cum, need[:rows, :], eq, ALU.is_le, ALU.mult))
    d(v.tensor_tensor(gt, gt, eq, ALU.add))
    if out is not None:
        d(v.tensor_scalar(out, gt, -1.0, -NEG, ALU.add, ALU.mult))


def dsa_prompt(ph, I, O, tp_d, S):
    nc, pool_dma_sem, sem, bank, cm, cw, pcol, prm, fr = ph
    fa, vt, nm = S["fa"], S["vt"], S["nm"]
    with ExitStack() as tmp:
        al = lambda n, s, d=F32: tmp.enter_context(nc.sbuf_tensor(n, s, d))
        bp = al("bp", [P, 2, 2, SP_])
        lg = al("lg", [P, 2, 2, SP_])
        pt = al("pt", [P, 2, 4, P])
        sm = al("sm", [P, 3, 2, 2])
    s_bp = [sem("bias_in0"), sem("bias_in1")]
    bm_done, qk_made, lg_done, mx_done, ex_done, rc_done = [sem("p_" + n) for n in ("bm", "qk", "logits", "max", "exp", "recip")]
    nrm, pt_made, pt_read, o_made, o_read, dch = [sem("p_" + n) for n in ("norm", "turned", "taken", "o", "o_read", "chain")]
    units = [(qt, hp) for qt in range(2) for hp in range(HP)]
    def take(a, n):
        qt, hp = units[n]
        a.wait_ge(pt_made, n + 1)
        a.activation(pt[:, n % 2, :, :].rearrange("p (h j) q -> p h j q", h=2)[:, :, 0:qt + 1, :],
                     bank[4 + n % 2][:, :].rearrange("p (h j q) -> p h j q", h=2, j=2)[:, :, 0:qt + 1, :], ACT.Copy).then_inc(pt_read, 1)
        a.wait_ge(o_made, n + 1)
        a.activation(fr[:, 8 + hp, P * qt:P * qt + P], bank[6 + n % 2][:, 0:P], ACT.Copy).then_inc(o_read, 1)

    with nc.Block() as block:
        @block.sync
        def _(sp):
            for n, (qt, hp) in enumerate(units):
                nk = P * (qt + 1)
                if n >= 2:
                    sp.wait_ge(lg_done, 2 * (n - 1))
                src = tp_d[2 * hp:2 * hp + 2, :, P * (1 - qt):P * (1 - qt) + nk].rearrange("h p s -> p h s")
                sp.dma_start(bp[:, n % 2, :, 0:nk], src).then_inc(s_bp[n % 2], 16)

        @block.gpsimd
        def _(g):
            for n, (qt, hp) in enumerate(units):
                nk = P * (qt + 1)
                g.wait_ge(s_bp[n % 2], 16 * (n // 2 + 1))
                g.tensor_tensor(bp[:, n % 2, :, 0:nk], bp[:, n % 2, :, 0:nk], nm[:, qt, 0:nk].unsqueeze(1).to_broadcast([P, 2, nk]), ALU.add).then_inc(bm_done, 1)

        @block.tensor
        def _(e):
            def qk(n):
                qt, hp = units[n]
                nk = P * (qt + 1)
                if n >= 2:
                    e.wait_ge(lg_done, 2 * (n - 1))
                for p_ in range(2):
                    r = slice(HD * p_, HD * p_ + HD)
                    e.matmul(bank[2 * (n % 2) + p_][:, 0:nk], fa[r, hp, P * qt:P * qt + P], fa[r, 8 + hp, 0:nk], start=True, stop=True).then_inc(qk_made, 1)
            qk(0)
            for n, (qt, hp) in enumerate(units):
                if n + 1 < len(units):
                    qk(n + 1)
                e.wait_ge(nrm, n + 1)
                if n >= 2:
                    e.wait_ge(pt_read, n - 1)
                for p_ in range(2):
                    for j in range(qt + 1):
                        ins = e.transpose(bank[4 + n % 2][:, (2 * p_ + j) * P:(2 * p_ + j + 1) * P], lg[:, n % 2, p_, j * P:(j + 1) * P], cw("ident"))
                ins.then_inc(pt_made, 1)
                e.wait_ge(pt_read, n + 1)
                if n >= 2:
                    e.wait_ge(o_read, n - 1)
                for p_ in range(2):
                    for j in range(qt + 1):
                        ins = e.matmul(bank[6 + n % 2][HD * p_:HD * p_ + HD, 0:P], vt[:, j, hp * P + HD * p_:hp * P + HD * p_ + HD],
                                       pt[:, n % 2, 2 * p_ + j, :], start=(j == 0), stop=(j == qt))
                ins.then_inc(o_made, 1)

        @block.scalar
        def _(a):
            for n, (qt, hp) in enumerate(units):
                nk = P * (qt + 1)
                a.wait_ge(mx_done, n + 1)
                for p_ in range(2):
                    a.activation(lg[:, n % 2, p_, 0:nk], lg[:, n % 2, p_, 0:nk], ACT.Exp, bias=sm[:, 0, n % 2, p_:p_ + 1],
                                 accum_out=sm[:, 1, n % 2, p_:p_ + 1]).then_inc(ex_done, 1)
                if n:
                    take(a, n - 1)
            take(a, len(units) - 1)

        @block.vector
        def _(v):
            for n, (qt, hp) in enumerate(units):
                nk = P * (qt + 1)
                v.wait_ge(bm_done, n + 1)
                if n >= 2:
                    v.wait_ge(pt_made, n - 1)
                for p_ in range(2):
                    v.wait_ge(qk_made, 2 * n + p_ + 1)
                    v.scalar_tensor_tensor(lg[:, n % 2, p_, 0:nk], bank[2 * (n % 2) + p_][:, 0:nk], HD ** -0.5, bp[:, n % 2, p_, 0:nk],
                                           ALU.mult, ALU.add).then_inc(lg_done, 1)
                v.wait_ge(lg_done, 2 * n + 2)
                v.tensor_reduce(sm[:, 0, n % 2, :], lg[:, n % 2, :, 0:nk], AXX, ALU.max, negate=True).then_inc(mx_done, 1)
                v.wait_ge(ex_done, 2 * n + 2)
                v.reciprocal(sm[:, 2, n % 2, :], sm[:, 1, n % 2, :]).then_inc(rc_done, 1)
                v.wait_ge(rc_done, n + 1)
                v.tensor_tensor(lg[:, n % 2, :, 0:nk], lg[:, n % 2, :, 0:nk], sm[:, 2, n % 2, :].unsqueeze(2).to_broadcast([P, 2, nk]), ALU.mult).then_inc(nrm, 1)


def dsa_sample(ph, I, O, bs_d, S):
    nc, pool_dma_sem, sem, bank, cm, cw, pcol, prm, fr = ph
    ik2, vt, cd, iqs, wts, qs, qn, kn = [S[n] for n in ("ik2", "vt", "cd", "iqs", "wts", "qs", "qn", "kn")]
    with ExitStack() as tmp:
        al = lambda n, s, d=F32: tmp.enter_context(nc.sbuf_tensor(n, s, d))
        pti = al("pti", [P, DB * NPG], I32)
        row = al("row", [P, DB * NPG], I32)
        kp = al("kp", [P, NPG, AT])
        vp = al("vp", [P, NPG, AT])
        ki = al("ki", [P, 2, NPG, HD])
        kd = al("kd", [P, NPG, 2, HD])
        kit = al("kit", [P, 2, 512])
        rl = al("srl", [P, KEYS])
        sc = al("ssc", [SS, KEYS])
        wk = al("swk", [SS, 2, KEYS])
        nms = al("nms", [SS, KEYS])
        m8 = al("sm8", [SS, 8])
        need = al("sneed", [SS, 1])
        ktr = al("ktr", [P, HP, 512])
        bs = al("bs", [P, KEYS])
        lg = al("slg", [P, KEYS])
        pt = al("spt", [P, 9, P])
        sm = al("ssm", [P, 4])
    gt, eq, cum, ones = rl[0:SS, :], lg[0:SS, :], pt[0:SS, :, :].rearrange("p a b -> p (a b)")[:, 0:KEYS], ktr[0:SS, :, :].rearrange("p a b -> p (a b)")[:, 0:KEYS]
    s_pt, s_bs, row_ready = sem("page_table_in"), sem("sample_bias_in"), sem("rows_ready")
    s_ki = [pool_dma_sem(f"ki_in{i}") for i in range(2)]
    kd_done, kit_made, kit_read, dot_made, relu_done, sc_made = [sem("s_" + n) for n in ("dup", "ki_turned", "ki_taken", "dots", "relu", "scores")]
    sch = sem("s_sel_chain")
    ck = I["cache_k"][0].rearrange("n p h d -> (n p) (h d)")
    cv = I["cache_v"][0].rearrange("n p h d -> (n p) (h d)")
    ci = I["cache_idx_k"][0].rearrange("n p d -> (n p) d")
    cols = [(0, 512), (512, 1024), (1024, KEYS)]

    def gather(g, dst, src, col):
        return g.indirect_dma_start(out=dst, out_offset=None, in_=src,
                                    in_offset=bass.IndirectOffsetOnAxis(ap=row[:, col:col + 1], axis=0))
    with nc.Block() as block:
        @block.sync
        def _(sp):
            sp.dma_start(pti[:, :], I["page_table"].rearrange("b n -> (b n)").partition_broadcast(P)).then_inc(s_pt, 16)
            sp.dma_start(bs[:, :], bs_d.rearrange("h q s -> (h q) s")).then_inc(s_bs, 16)
            sp.wait_ge(s_bs, 16)

        @block.gpsimd
        def _(g):
            g.wait_ge(row_ready, 1)
            for b in range(DB):
                if b >= 2:
                    g.wait_ge(kd_done, b - 1)
                for n in range(NPG):
                    gather(g, ki[:, b % 2, n, :], ci, NPG * b + n).then_inc(s_ki[b % 2], 16)

        @block.scalar
        def _(a):
            for b in range(DB):
                for i in range(2):
                    a.wait_ge(kit_made, 2 * b + i + 1)
                    if b:
                        a.wait_ge(dot_made, 3 * (b - 1) + i + 1)
                    a.activation(kit[:, i, :], bank[i][:, :], ACT.Copy).then_inc(kit_read, 1)
                for i, (c0, c1) in enumerate(cols):
                    a.wait_ge(dot_made, 3 * b + i + 1)
                    if b:
                        a.wait_ge(sc_made, b)
                    a.activation(rl[:, c0:c1], bank[2 + i][:, 0:c1 - c0], ACT.Relu).then_inc(relu_done, 1)

        @block.tensor
        def _(e):
            for b in range(DB):
                e.wait_ge(kd_done, b + 1)
                for i in range(2):
                    if b:
                        e.wait_ge(kit_read, 2 * (b - 1) + i + 1)
                    for n in range(4):
                        ins = e.transpose(bank[i][:, n * P:(n + 1) * P], kd[:, 4 * i + n, :, :].rearrange("p a d -> p (a d)"), cw("ident"))
                    ins.then_inc(kit_made, 1)
                for i, (c0, c1) in enumerate(cols):
                    if i < 2:
                        e.wait_ge(kit_read, 2 * b + i + 1)
                    if b:
                        e.wait_ge(relu_done, 3 * (b - 1) + i + 1)
                    rhs = kit[:, i, :] if i < 2 else ik2[:, SP_:]
                    e.matmul(bank[2 + i][:, 0:c1 - c0], iqs[:, b, :, :, :].rearrange("p h a q -> p (h a q)"), rhs, start=True, stop=True).then_inc(dot_made, 1)
                for i, (c0, c1) in enumerate(cols):
                    e.wait_ge(relu_done, 3 * b + i + 1)
                    ins = e.matmul(bank[5 + i][:SS, 0:c1 - c0], wts[:, SS * b:SS * b + SS], rl[:, c0:c1], start=(b == 0), stop=(b == DB - 1))
                ins.then_inc(sc_made, 1)

        @block.vector
        def _(v):
            d = chain_of(v, sch)
            v.wait_ge(s_pt, 16)
            v.tensor_scalar(row[:, :], pti[:, :], float(PAGE), cdw(cd, "iota"), ALU.mult, ALU.add).then_inc(row_ready, 1)
            for b in range(DB):
                v.wait_ge(s_ki[b % 2], 16 * NPG * (b // 2 + 1))
                if b:
                    v.wait_ge(kit_made, 2 * b)
                src = ki[:, b % 2, :, :]
                v.tensor_copy(kd[:, :, :, :], src.unsqueeze(2).to_broadcast([P, NPG, 2, HD])).then_inc(kd_done, 1)
            v.wait_ge(sc_made, DB)
            for i, (c0, c1) in enumerate(cols):
                if i < 2:
                    d(v.tensor_scalar(sc[:, c0:c1], bank[5 + i][:SS, 0:c1 - c0], IDXW, None, ALU.mult))
                else:
                    d(v.scalar_tensor_tensor(sc[:, c0:c1], bank[5 + i][:SS, 0:c1 - c0], IDXW, cdw(cd, "cns")[0:SS, :], ALU.mult, ALU.add))
            d(v.memset(ones, 1.0))
            top_mask(v, d, sc[:, :], wk, m8, gt, eq, cum, ones, need, TOPK_S, nms[:, :], KEYS, SS)
            d(v.tensor_tensor(nms[:, PAST:], nms[:, PAST:], cdw(cd, "cns")[0:SS, :], ALU.min))

    s_k = [pool_dma_sem(f"k_page_in{i}") for i in range(2)]
    s_v = pool_dma_sem("v_pages_in")
    ktr_made, ktr_read, qs_ready, qk_made = [sem("a_" + n) for n in ("k_turned", "k_taken", "q_spread", "logits_made")]
    lg_done, mx_done, ex_done, rc_done, nrm = [sem("a_" + n) for n in ("logits", "max", "exp", "recip", "norm")]
    pt_made, pt_read, o_made, o_read = [sem("a_" + n) for n in ("p_turned", "p_taken", "o_made", "o_read")]
    with nc.Block() as block:
        @block.gpsimd
        def _(g):
            for b in range(DB):
                for i in range(2):
                    if b:
                        g.wait_ge(ktr_made, 16 * (b - 1) + 8 * i + 8)
                    for n in range(4):
                        gather(g, kp[:, 4 * i + n, :], ck, NPG * b + 4 * i + n).then_inc(s_k[i], 16)
                if b:
                    g.wait_ge(o_made, b)
                for n in range(NPG):
                    gather(g, vp[:, n, :], cv, NPG * b + n).then_inc(s_v, 16)

        @block.tensor
        def _(e):
            for b in range(DB):
                e.wait_ge(qs_ready, 2 * b + 2)
                for i in range(2):
                    e.wait_ge(s_k[i], 64 * (b + 1))
                    for hp in range(HP):
                        g = 16 * b + 8 * i + hp
                        if g >= 2:
                            e.wait_ge(ktr_read, g - 1)
                        for n in range(4):
                            ins = e.transpose(bank[g % 2][:, n * P:(n + 1) * P], kp[:, 4 * i + n, hp * P:(hp + 1) * P], cw("ident"))
                        ins.then_inc(ktr_made, 1)
                        if hp == 0:
                            if b:
                                e.wait_ge(lg_done, 3 * (b - 1) + i + 1)
                            e.matmul(bank[2 + i][:, :], cdw(cd, "rep")[0:SS, P * b:P * b + P], nms[:, 512 * i:512 * i + 512], start=True, stop=False)
                        if hp:
                            e.wait_ge(ktr_read, g)
                            e.matmul(bank[2 + i][:, :], qs[:, b % 2, (hp - 1) * P:hp * P], ktr[:, hp - 1, :], start=False, stop=False)
                    e.wait_ge(ktr_read, 16 * b + 8 * i + 8)
                    e.matmul(bank[2 + i][:, :], qs[:, b % 2, 7 * P:8 * P], ktr[:, 7, :], start=False, stop=True).then_inc(qk_made, 1)
                if b:
                    e.wait_ge(lg_done, 3 * b)
                e.matmul(bank[4][:, 0:SS], cdw(cd, "rep")[0:SS, P * b:P * b + P], nms[:, PAST:], start=True, stop=False)
                for hp in range(HP):
                    ins = e.matmul(bank[4][:, 0:SS], qs[:, b % 2, hp * P:(hp + 1) * P], kn[:, hp, :], start=False, stop=(hp == 7))
                ins.then_inc(qk_made, 1)
                e.wait_ge(nrm, b + 1)
                for c in range(3):
                    if 3 * b + c >= 2:
                        e.wait_ge(pt_read, 3 * b + c - 1)
                    for n in range(4 * c, min(4 * c + 4, 9)):
                        w = P if n < 8 else SS
                        ins = e.transpose(bank[5 + (3 * b + c) % 2][:w, (n % 4) * P:(n % 4 + 1) * P], lg[:, n * P:n * P + w], cw("ident"))
                    ins.then_inc(pt_made, 1)
                e.wait_ge(pt_read, 3 * b + 3)
                e.wait_ge(s_v, 16 * NPG * (b + 1))
                if b:
                    e.wait_ge(o_read, 2 * b)
                for hp in range(HP):
                    for n in range(9):
                        w = P if n < 8 else SS
                        lhs = vp[:, n, hp * P:(hp + 1) * P] if n < 8 else vt[0:SS, 2, hp * P:(hp + 1) * P]
                        ins = e.matmul(bank[7][:, hp * 2 * T:(hp + 1) * 2 * T], lhs, pt[:w, n, hp * 2 * T:(hp + 1) * 2 * T], start=(n == 0), stop=(n == 8))
                ins.then_inc(o_made, 1)

        @block.scalar
        def _(a):
            for b in range(DB):
                for g in range(16 * b, 16 * b + 16):
                    a.wait_ge(ktr_made, g + 1)
                    if g % 8 == 0 and g:
                        a.wait_ge(qk_made, 3 * ((g // 8 - 1) // 2) + (g // 8 - 1) % 2 + 1)
                    a.activation(ktr[:, g % 8, :], bank[g % 2][:, :], ACT.Copy).then_inc(ktr_read, 1)
                a.wait_ge(mx_done, b + 1)
                a.activation(lg[:, :], lg[:, :], ACT.Exp, bias=sm[:, 0:1], accum_out=sm[:, 1:2]).then_inc(ex_done, 1)
                for c in range(3):
                    a.wait_ge(pt_made, 3 * b + c + 1)
                    n, w = (4, P) if c < 2 else (1, SS)
                    a.activation(pt[:w, 4 * c:4 * c + n, :], bank[5 + (3 * b + c) % 2][:w, 0:n * P].rearrange("p (n q) -> p n q", n=n), ACT.Copy).then_inc(pt_read, 1)
                a.wait_ge(o_made, b + 1)
                for p_ in range(2):
                    r = slice(HD * p_, HD * p_ + HD)
                    a.activation(fr[r, 8:16, SP_ + T * b:SP_ + T * b + T],
                                 bank[7][r, 0:P].rearrange("p (h a q) -> p h a q", a=2, q=T)[:, :, p_, :], ACT.Copy).then_inc(o_read, 1)

        @block.vector
        def _(v):
            for b in range(DB):
                if b >= 2:
                    v.wait_ge(qk_made, 3 * (b - 1))
                for p_ in range(2):
                    r = slice(HD * p_, HD * p_ + HD)
                    v.tensor_copy(qs[r, b % 2, :].rearrange("p (h x) -> p h x", x=144)[:, :, T * p_:T * p_ + T], qn[r, :, T * b:T * b + T]).then_inc(qs_ready, 1)
                if b:
                    v.wait_ge(pt_made, 3 * b)
                for i, (c0, c1) in enumerate(cols):
                    v.wait_ge(qk_made, 3 * b + i + 1)
                    v.scalar_tensor_tensor(lg[:, c0:c1], bank[2 + i][:, 0:c1 - c0], HD ** -0.5, bs[:, c0:c1], ALU.mult, ALU.add).then_inc(lg_done, 1)
                v.wait_ge(lg_done, 3 * b + 3)
                v.tensor_reduce(sm[:, 0:1], lg[:, :], AXX, ALU.max, negate=True).then_inc(mx_done, 1)
                v.wait_ge(ex_done, b + 1)
                v.reciprocal(sm[:, 2:3], sm[:, 1:2]).then_inc(rc_done, 1)
                v.wait_ge(rc_done, b + 1)
                v.tensor_scalar(lg[:, :], lg[:, :], sm[:, 2:3], None, ALU.mult).then_inc(nrm, 1)


def mix_out(ph, I, O, S):
    nc, pool_dma_sem, sem, bank, cm, cw, pcol, prm, fr = ph
    x1, mk, mv, mkt, qt_ = S["x1"], S["mk"], S["mv"], S["mkt"], S["qt"]
    with ExitStack() as tmp:
        al = lambda n, s, d=F32: tmp.enter_context(nc.sbuf_tensor(n, s, d))
        xn = al("xn", [P, 3, D])
        junk = al("junk2", [P, D])
        stats = al("stats2", [P, 4, 3])
        stats_m = al("stats_m", [P, 4, 3])
        ht = al("ht2", [P, KT, TOK])
        w = al("wmix", [P, 2, KT, CH])
    s_x, s_m, s_w = sem("x1_in"), sem("mem_in"), [sem("wmix0_in"), sem("wmix1_in")]
    t_made, t_read, x_added, s_kv = sem("mix_tiles"), sem("mix_read"), sem("x1_added"), sem("memkv_out")
    mt_made, mt_read = sem("mk_turned"), sem("mk_taken")
    kt = lambda a: a.rearrange("(kt p) n -> p kt n", p=P)
    wout = kt(I["w_out"][0])
    chunks = [wout[:, :, CH * i:CH * i + CH] for i in range(4)] + [kt(I[n][0]) for n in ("w_ck", "w_cv", "w_cq")]
    tiles = [3, 3, 3, 3, 2, 2, 4]
    first = [sum(tiles[:i]) for i in range(8)]
    mem = I["mem_prompt"][0]
    am, dm, pm, mem_turned = norm_to_features(ph, "mem", xn, [P, P], pcol("g_mem"), ht, lambda e, t: e.wait_ge(s_m, 32), (6, 7), (junk, stats_m))
    ax, dx, px, cross_turned = norm_to_features(ph, "cross", x1, [m for _, m in TILES], pcol("g_cross"), ht, lambda e, t: e.wait_ge(x_added, 12),
                                     (6, 7), (junk, stats), out=xn)

    with nc.Block() as block:
        @block.sync
        def _(sp):
            for c, src in enumerate(chunks):
                if c >= 2:
                    sp.wait_ge(t_made, first[c - 1])
                sp.dma_start(w[:, c % 2, :, :], src).then_inc(s_w[c % 2], 16)

        @block.scalar
        def _(a):
            for t, (t0, m) in enumerate(TILES):
                src = I["x_prompt"][0] if t < 2 else I["x_sample"].rearrange("b t d -> (b t) d")
                a.dma_start(x1[:m, t, :], src[t0 % SP_:t0 % SP_ + m, :]).then_inc(s_x, 16)
            for t in range(2):
                a.dma_start(xn[:, t, :], mem[P * t:P * t + P, :]).then_inc(s_m, 16)
            am(a)
            for c, dst in ((4, mk), (5, mv)):
                for t in range(2):
                    n = first[c] + t
                    a.wait_ge(t_made, n + 1)
                    a.activation(dst[:, t, :], bank[n % 4][:, :], ACT.Copy).then_inc(t_read, 1)
            a.wait_ge(t_read, 4)
            for t in range(2):
                for n, src in (("mk_p", mk), ("mv_p", mv)):
                    a.dma_start(O[n][0, 0].rearrange("s h d -> s (h d)")[P * t:P * t + P, :], src[:, t, :]).then_inc(s_kv, 16)
            for i in range(2):
                a.wait_ge(mt_made, i + 1)
                a.activation(mkt[:, 2 * i:2 * i + 2, :], bank[4 + i][:, :].rearrange("p (h s) -> p h s", h=2), ACT.Copy).then_inc(mt_read, 1)
            ax(a)
            for j in range(XH):
                n = first[6] + j
                a.wait_ge(t_made, n + 1)
                a.activation(qt_[:, j, :], bank[n % 4][:, 0:TOK], ACT.Copy).then_inc(t_read, 1)
            a.wait_ge(s_kv, 64)

        @block.vector
        def _(v):
            dm(v)
            v.wait_ge(s_x, 48)
            for c in range(4):
                for t, (t0, m) in enumerate(TILES):
                    n = 3 * c + t
                    v.wait_ge(t_made, n + 1)
                    xs = x1[:m, t, CH * c:CH * c + CH]
                    v.tensor_tensor(xs, xs, bank[n % 4][:m, :], ALU.add).then_inc(x_added, 1)
            v.wait_ge(t_made, first[6])
            dx(v)

        @block.tensor
        def _(e):
            pm(e)

            def free(n):
                if 4 <= n < 16:
                    e.wait_ge(x_added, n - 3)
                elif n >= 16:
                    e.wait_ge(t_read, n - 15)
            for c in range(7):
                if c == 6:
                    e.wait_ge(mt_read, 2)
                    px(e)
                    e.wait_ge(*cross_turned)
                if c == 4:
                    e.wait_ge(*mem_turned)
                e.wait_ge(s_w[c % 2], 16 * (c // 2 + 1))
                for t in range(tiles[c]):
                    n = first[c] + t
                    free(n)
                    if c < 6:
                        t0, m = TILES[t]
                        lhs = (lambda k: fr[:, k, t0:t0 + m]) if c < 4 else (lambda k: ht[:, k, t0:t0 + m])
                        for k in range(KT):
                            ins = e.matmul(bank[n % 4][:m, :], lhs(k), w[:, c % 2, k, :], start=(k == 0), stop=(k == KT - 1))
                    else:
                        for k in range(KT):
                            ins = e.matmul(bank[n % 4][:, 0:TOK], w[:, c % 2, k, P * t:P * t + P], ht[:, k, :], start=(k == 0), stop=(k == KT - 1))
                    ins.then_inc(t_made, 1)
                if c == 5:
                    e.wait_ge(t_read, 4)
                    for i in range(2):
                        for h in (2 * i, 2 * i + 1):
                            for t in range(2):
                                ins = e.transpose(bank[4 + i][:, (h % 2) * MEM + P * t:(h % 2) * MEM + P * t + P], mk[:, t, P * h:P * h + P], cw("ident"))
                        ins.then_inc(mt_made, 1)


def cross(ph, I, O, S):
    nc, pool_dma_sem, sem, bank, cm, cw, pcol, prm, fr = ph
    x1, mk, mv, mkt, qt_ = S["x1"], S["mk"], S["mv"], S["mkt"], S["qt"]
    with ExitStack() as tmp:
        al = lambda n, s, d=F32: tmp.enter_context(nc.sbuf_tensor(n, s, d))
        wco = al("wco", [P, XH, D])
        ot = al("ot", [P, XH, TOK])
        ckk = al("ckk", [P, 2, 2, XW])
        cvv = al("cvv", [P, 4, 2, XW])
        kts = al("kts", [P, 2, XH, MEM])
        qx = al("qx", [P, 2, XH * 40])
        lg = al("clg", [P, 2, 4, MEM])
        pt = al("cpt", [P, 2, 4, P])
        sm = al("csm", [P, 3, 4])
    s_w, s_k, s_v = sem("wco_in"), [sem("ckk_in0"), sem("ckk_in1")], sem("cvv_in")
    qk_made, lg_done, mx_done, ex_done, rc_done, nrm = [sem("c_" + n) for n in ("qk", "logits", "max", "exp", "recip", "norm")]
    pt_made, pt_read, o_made, o_read = [sem("c_" + n) for n in ("turned", "taken", "o", "o_read")]
    kt_made, kt_read, qx_zero, qx_ready, x_made, x_added = [sem("c_" + n) for n in ("k_turned", "k_taken", "q_zero", "q_spread", "x_made", "x_added")]
    UN = [("p", 0), ("p", 1), ("s", 0), ("s", 1)]
    nh = lambda u: 4 if u[0] == "p" else 1
    done = lambda n: sum(nh(u) for u in UN[:n])
    ckd = I["cache_mem_k"][0].rearrange("b (t p) h d -> b p t (h d)", p=P)
    cvd = I["cache_mem_v"][0].rearrange("b (t p) h d -> b p t (h d)", p=P)
    with nc.Block() as block:
        @block.sync
        def _(sp):
            for b in range(DB):
                if b >= 2:
                    sp.wait_ge(kt_made, 2 * (b - 1))
                sp.dma_start(ckk[:, b % 2, :, :], ckd[b]).then_inc(s_k[b % 2], 16)

        @block.scalar
        def _(a):
            a.dma_start(wco[:, :, :], I["w_co"][0].rearrange("(h p) n -> p h n", p=P)).then_inc(s_w, 16)
            for b in range(4):
                a.dma_start(cvv[:, b, :, :], cvd[b]).then_inc(s_v, 16)
            nk = 0
            for n, u in enumerate(UN):
                if u[0] == "s":
                    for b in range(4 * u[1], 4 * u[1] + 4):
                        for i in range(2):
                            a.wait_ge(kt_made, 2 * b + i + 1)
                            if b >= 2:
                                a.wait_ge(qk_made, 4 + b - 1)
                            a.activation(kts[:, b % 2, 2 * i:2 * i + 2, :], bank[2 + i][:, :].rearrange("p (h s) -> p h s", h=2), ACT.Copy).then_inc(kt_read, 1)
                a.wait_ge(mx_done, n + 1)
                for j in range(nh(u)):
                    a.activation(lg[:, n % 2, j, :], lg[:, n % 2, j, :], ACT.Exp, bias=sm[:, 0, j:j + 1], accum_out=sm[:, 1, j:j + 1]).then_inc(ex_done, 1)
                for i in range(2 if u[0] == "p" else 1):
                    a.wait_ge(pt_made, 2 * min(n, 2) + max(n - 2, 0) + i + 1)
                    w = 4 if u[0] == "p" else 2
                    a.activation(pt[:, i, 0:w, :], bank[4 + i][:, 0:w * P].rearrange("p (j q) -> p j q", j=w), ACT.Copy).then_inc(pt_read, 1)
                a.wait_ge(o_made, n + 1)
                if u[0] == "p":
                    a.activation(ot[:, :, P * u[1]:P * u[1] + P], bank[6][:, :].rearrange("p (h q) -> p h q", h=XH), ACT.Copy).then_inc(o_read, 1)
                else:
                    g0 = SP_ + 32 * u[1]
                    a.activation(ot[:, :, g0:g0 + 32].rearrange("p h (b q) -> p b h q", q=T),
                                 bank[6][:, 0:P].rearrange("p (b h q) -> p b h q", b=4, h=XH), ACT.Copy).then_inc(o_read, 1)
                if n == 2:
                    for b in range(4, 8):
                        a.dma_start(cvv[:, b - 4, :, :], cvd[b]).then_inc(s_v, 16)

        @block.tensor
        def _(e):
            for n, u in enumerate(UN):
                if u[0] == "p":
                    if n:
                        e.wait_ge(lg_done, n)
                    tok = slice(P * u[1], P * u[1] + P)
                    for h in range(XH):
                        ins = e.matmul(bank[h // 2][:, (h % 2) * MEM:(h % 2 + 1) * MEM], qt_[:, h, tok], mkt[:, h, :], start=True, stop=True)
                        if h % 2:
                            ins.then_inc(qk_made, 1)
                else:
                    if u[1] == 0:
                        e.wait_ge(lg_done, 2)
                    else:
                        e.wait_ge(lg_done, 3)
                    for b in range(4 * u[1], 4 * u[1] + 4):
                        e.wait_ge(s_k[b % 2], 16 * (b // 2 + 1))
                        for i in range(2):
                            if b:
                                e.wait_ge(kt_read, 2 * (b - 1) + i + 1)
                            for h in (2 * i, 2 * i + 1):
                                for t in range(2):
                                    ins = e.transpose(bank[2 + i][:, (h % 2) * MEM + P * t:(h % 2) * MEM + P * t + P], ckk[:, b % 2, t, P * h:P * h + P], cw("ident"))
                            ins.then_inc(kt_made, 1)
                        e.wait_ge(kt_read, 2 * b + 2)
                        e.wait_ge(qx_ready, b + 1)
                        r = 32 * (b % 4)
                        for h in range(XH):
                            ins = e.matmul(bank[0][r:r + 32, 0:MEM], qx[:, b % 2, 32 * h:32 * h + 32], kts[:, b % 2, h, :], start=(h == 0), stop=(h == XH - 1))
                        ins.then_inc(qk_made, 1)
                e.wait_ge(nrm, n + 1)
                for i in range(2 if u[0] == "p" else 1):
                    if n:
                        e.wait_ge(pt_read, 2 * min(n, 2) + max(n - 2, 0))
                    if u[0] == "p":
                        for h in (2 * i, 2 * i + 1):
                            for t in range(2):
                                ins = e.transpose(bank[4 + i][:, (2 * (h % 2) + t) * P:(2 * (h % 2) + t + 1) * P], lg[:, n % 2, h, P * t:P * t + P], cw("ident"))
                    else:
                        for t in range(2):
                            ins = e.transpose(bank[4][:, t * P:(t + 1) * P], lg[:, n % 2, 0, P * t:P * t + P], cw("ident"))
                    ins.then_inc(pt_made, 1)
                e.wait_ge(pt_read, 2 * min(n + 1, 2) + max(n - 1, 0))
                if n:
                    e.wait_ge(o_read, n)
                if u[0] == "p":
                    for h in range(XH):
                        for t in range(2):
                            ins = e.matmul(bank[6][:, P * h:P * h + P], mv[:, t, P * h:P * h + P], pt[:, h // 2, 2 * (h % 2) + t, :], start=(t == 0), stop=(t == 1))
                else:
                    e.wait_ge(s_v, 64 * (u[1] + 1))
                    for b in range(4):
                        for h in range(XH):
                            c = 32 * b + T * h
                            for t in range(2):
                                ins = e.matmul(bank[6][:, c:c + T], cvv[:, b, t, P * h:P * h + P], pt[:, 0, t, c:c + T], start=(t == 0), stop=(t == 1))
                ins.then_inc(o_made, 1)
            e.wait_ge(s_w, 16)
            e.wait_ge(o_read, 4)
            for t, (t0, m) in enumerate(TILES):
                for c in range(4):
                    n = 4 * t + c
                    if n >= 4:
                        e.wait_ge(x_added, n - 3)
                    for h in range(XH):
                        ins = e.matmul(bank[n % 4][:m, :], ot[:, h, t0:t0 + m], wco[:, h, CH * c:CH * c + CH], start=(h == 0), stop=(h == XH - 1))
                    ins.then_inc(x_made, 1)

        @block.vector
        def _(v):
            v.memset(qx[:, :, :], 0.0).then_inc(qx_zero, 1)
            v.wait_ge(qx_zero, 1)
            for n, u in enumerate(UN):
                if u[0] == "p":
                    v.wait_ge(qk_made, 2 * n + 2)
                    for i in range(2):
                        ins = v.tensor_scalar(lg[:, n % 2, 2 * i:2 * i + 2, :], bank[i][:, :].rearrange("p (h s) -> p h s", h=2), P ** -0.5, None, ALU.mult)
                    ins.then_inc(lg_done, 1)
                else:
                    for b in range(4 * u[1], 4 * u[1] + 4):
                        if b >= 2:
                            v.wait_ge(qk_made, 4 + b - 1)
                        v.tensor_copy(qx[:, b % 2, :].rearrange("p (h x) -> p h x", x=40)[:, :, 0:T], qt_[:, :, SP_ + T * b:SP_ + T * b + T]).then_inc(qx_ready, 1)
                    v.wait_ge(qk_made, 4 + 4 * (u[1] + 1))
                    v.tensor_scalar(lg[:, n % 2, 0, :], bank[0][:, 0:MEM], P ** -0.5, None, ALU.mult).then_inc(lg_done, 1)
                v.wait_ge(lg_done, n + 1)
                w = nh(u)
                v.tensor_reduce(sm[:, 0, 0:w], lg[:, n % 2, 0:w, :], AXX, ALU.max, negate=True).then_inc(mx_done, 1)
                v.wait_ge(ex_done, done(n + 1))
                v.reciprocal(sm[:, 2, 0:w], sm[:, 1, 0:w]).then_inc(rc_done, 1)
                v.wait_ge(rc_done, n + 1)
                v.tensor_tensor(lg[:, n % 2, 0:w, :], lg[:, n % 2, 0:w, :], sm[:, 2, 0:w].unsqueeze(2).to_broadcast([P, w, MEM]), ALU.mult).then_inc(nrm, 1)
            for t, (t0, m) in enumerate(TILES):
                for c in range(4):
                    n = 4 * t + c
                    v.wait_ge(x_made, n + 1)
                    xs = x1[:m, t, CH * c:CH * c + CH]
                    v.tensor_tensor(xs, xs, bank[n % 4][:m, :], ALU.add).then_inc(x_added, 1)


def route(ph, I, S):
    nc, pool_dma_sem, sem, bank, cm, cw, pcol, prm, fr = ph
    x1, hn, cmo, gates, slot, rounds = S["x1"], S["hn"], S["cmo"], S["gates"], S["slot"], S["rounds"]
    with ExitStack() as tmp:
        al = lambda n, s, d=F32: tmp.enter_context(nc.sbuf_tensor(n, s, d))
        junk = al("junk3", [P, D])
        stats = al("stats3", [P, 4, 3])
        ht = al("ht3", [P, KT, TOK])
        wr = al("wr", [P, KT, NG + NE])
        br = al("br", [P, NG + NE])
        lo = al("rlog", [P, 3, NG + NE])
        gm = al("gm", [P, 3])
        eg = al("eg", [P, 3, NG])
        cg = al("cg", [P, 3, NG])
        xg = al("xge", [P, 3, NG])
        pg = al("pg", [P, 3])
        m8 = al("rm8", [P, 3, 8])
        gt = al("rgt", [P, 3, NE])
        eq = al("req", [P, 3, NE])
        cum = al("rcum", [P, 3, NE])
        ex = al("rex", [P, 3, NE])
        ws = al("rws", [P, 3])
        need = al("rneed", [P, 1])
        mc = al("mc", [P, 1])
        rf = al("rf", [P, 2])
    s_in, r_made, exps, subs, sel_done, rk_made, rch = [sem("r_" + n) for n in ("in", "logits", "exps", "differences", "selected", "ranks", "chain")]
    an, dn, pn, turned = norm_to_features(ph, "ffn", x1, [m for _, m in TILES], pcol("g_ffn"), ht, lambda e, t: None, (6, 7), (junk, stats), out=hn)
    ones = cmw(cmo, "ones")
    with nc.Block() as block:
        @block.sync
        def _(sp):
            sp.dma_start(cmo[:, :], S["c_moe"]).then_inc(s_in, 16)
            sp.dma_start(wr[:, :, 0:NG], I["w_rg"][0].rearrange("(kt p) n -> p kt n", p=P)).then_inc(s_in, 16)
            sp.dma_start(wr[:, :, NG:], I["w_re"][0].rearrange("(kt p) n -> p kt n", p=P)).then_inc(s_in, 16)
            sp.dma_start(br[:, 0:NG], I["b_rg"][0].partition_broadcast(P)).then_inc(s_in, 16)
            sp.dma_start(br[:, NG:], I["b_re"][0].partition_broadcast(P)).then_inc(s_in, 16)

        @block.scalar
        def _(a):
            an(a)
            a.wait_ge(subs, 1)
            a.activation(xg[:, :, :], xg[:, :, :], ACT.Exp).then_inc(exps, 1)
            a.wait_ge(subs, 2)
            a.activation(ex[:, :, :], ex[:, :, :], ACT.Exp).then_inc(exps, 1)

        @block.tensor
        def _(e):
            pn(e)
            e.wait_ge(*turned)
            e.wait_ge(s_in, 80)
            for t, (t0, m) in enumerate(TILES):
                for k in range(KT):
                    ins = e.matmul(bank[t][:m, 0:NG + NE], ht[:, k, t0:t0 + m], wr[:, k, :], start=(k == 0), stop=(k == KT - 1))
                ins.then_inc(r_made, 1)
            e.wait_ge(sel_done, 1)
            for t in range(3):
                for j in range(t + 1):
                    e.matmul(bank[3][:, NE * t:NE * t + NE], ones if j < t else cmw(cmo, "upto"), gt[:, j, :], start=(j == 0), stop=(j == t))
            for j in range(3):
                ins = e.matmul(bank[3][:, NE * 3:NE * 4], ones, gt[:, j, :], start=(j == 0), stop=(j == 2))
            ins.then_inc(rk_made, 1)

        @block.vector
        def _(v):
            d = chain_of(v, rch)
            d(v.memset(lo[:, :, :], 0.0))
            dn(v)
            v.wait_ge(s_in, 80)
            for t, (t0, m) in enumerate(TILES):
                v.wait_ge(r_made, t + 1)
                d(v.tensor_tensor(lo[:m, t, :], bank[t][:m, 0:NG + NE], br[:m, :], ALU.add))
            gl, el = lo[:, :, 0:NG], lo[:, :, NG:]
            b3 = lambda z, n: z.unsqueeze(2).to_broadcast([P, 3, n])
            d(v.tensor_reduce(gm[:, :], gl, AXX, ALU.max))
            v.tensor_tensor(xg[:, :, :], gl, b3(gm[:, :], NG), ALU.subtract).then_inc(subs, 1)
            d(v.tensor_tensor(eg[:, :, :], gl, b3(gm[:, :], NG), ALU.is_equal))
            for t in range(3):
                d(v.tensor_tensor_scan(cg[:, t, :], ones[:, 0:NG], eg[:, t, :], 0.0, ALU.mult, ALU.add))
            d(v.scalar_tensor_tensor(eg[:, :, :], cg[:, :, :], 1.0, eg[:, :, :], ALU.is_le, ALU.mult))
            d(v.tensor_scalar(eg[:, :, :], eg[:, :, :], -1.0, -NEG, ALU.add, ALU.mult))
            d(v.tensor_tensor(el.rearrange("p t (g x) -> p t g x", g=NG), el.rearrange("p t (g x) -> p t g x", g=NG),
                              eg[:, :, :].unsqueeze(3).to_broadcast([P, 3, NG, EPG]), ALU.add))
            for t in range(3):
                top_mask(v, d, el[:, t, :], None, m8[:, t, :], gt[:, t, :], eq[:, t, :], cum[:, t, :], ones[:, 0:NE], need, 2, None, NE, P)
            v.wait_ge(subs, 1)
            v.tensor_tensor(ex[:, :, :], el, m8[:, :, 0:1].to_broadcast([P, 3, NE]), ALU.subtract).then_inc(subs, 1)
            v.memset(gt[64:P, 2, :], 0.0).then_inc(sel_done, 1)
            v.wait_ge(exps, 2)
            d(v.tensor_reduce(pg[:, :], xg[:, :, :], AXX, ALU.add))
            d(v.tensor_tensor(ex[:, :, :], ex[:, :, :], gt[:, :, :], ALU.mult))
            d(v.memset(ex[64:P, 2, :], 1.0))
            d(v.tensor_reduce(ws[:, :], ex[:, :, :], AXX, ALU.add))
            d(v.tensor_tensor(ws[:, :], ws[:, :], pg[:, :], ALU.mult))
            d(v.reciprocal(ws[:, :], ws[:, :]))
            d(v.tensor_tensor(gates[:, :, :], ex[:, :, :], b3(ws[:, :], NE), ALU.mult))
            v.wait_ge(rk_made, 1)
            d(v.tensor_tensor(slot[:, :, :], bank[3][:, 0:3 * NE].rearrange("p (t e) -> p t e", t=3), gt[:, :, :], ALU.mult))
            d(v.tensor_scalar(slot[:, :, :], slot[:, :, :], -1.0, None, ALU.add))
            d(v.tensor_reduce(mc[:, :], bank[3][:, 3 * NE:4 * NE], AXX, ALU.max))
            d(v.memset(rf[:, 0:1], 1.0))
            for r in range(1, -(-TOK // SLOTS)):
                d(v.tensor_scalar(rf[:, 1:2], mc[:, :], float(SLOTS * r), None, ALU.is_gt))
                d(v.tensor_tensor(rf[:, 0:1], rf[:, 0:1], rf[:, 1:2], ALU.add))
            d(v.tensor_copy(rounds[:, :], rf[:, 0:1]))


def experts(ph, I, S):
    nc, pool_dma_sem, sem, bank, cm, cw, pcol, prm, fr = ph
    x1, hn, cmo, gates, slot, rounds = S["x1"], S["hn"], S["cmo"], S["gates"], S["slot"], S["rounds"]
    with ExitStack() as tmp:
        w = tmp.enter_context(nc.sbuf_tensor("wexp", [P, RING, 2, 4 * DE], F32))
    flat = fr[:, :, :].rearrange("p a b -> p (a b)")
    at = [0]

    def view(n):
        at[0] += n
        return flat[:, at[0] - n:at[0]]
    xg = view(KT * P).rearrange("p (k s) -> p k s", k=KT)
    ys = view(D)
    oh = view(3 * P).rearrange("p (t s) -> p t s", t=3)
    og = view(3 * P).rearrange("p (t s) -> p t s", t=3)
    sg = view(TOK)
    u1, u2 = view(DE), view(DE)
    ut = view(DE).rearrange("p (f s) -> p f s", f=4)
    s_w = [sem(f"wexp_in{i}") for i in range(RING)]
    w_used, oh_ready, xg_made, xg_read, h_made, silu_done, u_done = [sem("m_" + n) for n in (
        "w_used", "onehots", "gathered", "gathered_read", "hidden", "silu", "u")]
    ut_made, ut_read, sg_made, sg_read, y_made, y_read, sc_made, sc_read, slot_ready = [sem("m_" + n) for n in (
        "u_turned", "u_taken", "onehots_turned", "onehots_taken", "y_made", "y_read", "scattered", "added", "slots_ready")]
    UNITS = 12
    w13 = [I[n][0].rearrange("(g a) (kt p) n -> g p a kt n", a=2, p=P) for n in ("w_e1", "w_e3")]
    w2 = I["w_e2"][0].rearrange("(g a) (f p) n -> g p a f n", a=2, p=P)
    half = lambda z, a: z[SLOTS * a:SLOTS * a + SLOTS]
    PAIRS = NE // 2

    def number_of_rounds(eng):
        return eng.value_load(rounds[0:1, 0:1], min_val=1, max_val=-(-TOK // SLOTS))

    with nc.Block() as block:
        @block.sync
        def _(sp):
            with sp.Fori(0, number_of_rounds(sp)) as r:
                with sp.Fori(0, PAIRS) as p:
                    g = r * PAIRS + p
                    for u in range(UNITS):
                        sp.wait_ge(w_used, g * UNITS + (u + 1))
                        for a_ in range(2):
                            if u < 8:
                                src = w13[u // 4][bass.DynSlice(p, 1), :, a_, 4 * (u % 4):4 * (u % 4) + 4, :].squeeze(0)
                                dst = w[:, u % RING, a_, :].rearrange("p (k n) -> p k n", k=4)
                            else:
                                src = w2[bass.DynSlice(p, 1), :, a_, u - 8, :].squeeze(0)
                                dst = w[:, u % RING, a_, :]
                            sp.dma_start(dst, src).then_inc(s_w[u % RING], 16)

        @block.vector
        def _(v):
            v.sem_inc(sc_read, 1)
            v.sem_inc(slot_ready, 1)
            with v.Fori(0, number_of_rounds(v)) as r:
                with v.Fori(0, PAIRS) as p:
                    g = r * PAIRS + p
                    v.wait_ge(slot_ready, r + 1)
                    mine = lambda z: z[:, :, bass.DynSlice(2 * p, 2)].unsqueeze(3).to_broadcast([P, 3, 2, SLOTS])
                    cut = lambda z: z.rearrange("p t (e s) -> p t e s", e=2)
                    v.tensor_tensor(cut(oh), cmw(cmo, "iota_slots").unsqueeze(1).unsqueeze(1).to_broadcast([P, 3, 2, SLOTS]), mine(slot), ALU.is_equal).then_inc(oh_ready, 1)
                    v.wait_ge(oh_ready, 2 * g + 1)
                    v.tensor_tensor(cut(og), cut(oh), mine(gates), ALU.mult).then_inc(oh_ready, 1)
                    for q in range(4):
                        v.wait_ge(xg_made, 4 * g + (q + 1))
                        v.tensor_tensor(xg[:, 4 * q:4 * q + 4, :], bank[6 + q % 2][:, :].rearrange("p (k s) -> p k s", k=4),
                                        pcol("g_ffn")[:, 4 * q:4 * q + 4].unsqueeze(2).to_broadcast([P, 4, P]), ALU.mult).then_inc(xg_read, 1)
                    v.wait_ge(silu_done, g + 1)
                    v.wait_ge(h_made, 2 * g + 2)
                    v.tensor_tensor(u2, u1, bank[1][:, :], ALU.mult).then_inc(u_done, 1)
                    for i in range(12):
                        t, c = divmod(i, 4)
                        m = TILES[t][1]
                        v.wait_ge(sc_made, 12 * g + (i + 1))
                        xs = x1[:m, t, CH * c:CH * c + CH]
                        v.tensor_tensor(xs, xs, bank[6 + i % 2][:m, :], ALU.add).then_inc(sc_read, 1)
                v.tensor_scalar(slot[:, :, :], slot[:, :, :], -float(SLOTS), None, ALU.add).then_inc(slot_ready, 1)

        @block.scalar
        def _(a):
            with a.Fori(0, number_of_rounds(a)) as r:
                with a.Fori(0, PAIRS) as p:
                    g = r * PAIRS + p
                    a.wait_ge(h_made, 2 * g + 1)
                    a.activation(u1, bank[0][:, :], ACT.Silu).then_inc(silu_done, 1)
                    a.wait_ge(sg_made, g + 1)
                    a.activation(sg, bank[1][:, 0:TOK], ACT.Copy).then_inc(sg_read, 1)
                    a.wait_ge(ut_made, g + 1)
                    a.activation(ut, bank[0][:, :].rearrange("p (f s) -> p f s", f=4), ACT.Copy).then_inc(ut_read, 1)
                    a.wait_ge(y_made, g + 1)
                    for c in range(4):
                        a.activation(ys[:, CH * c:CH * c + CH], bank[2 + c][:, :], ACT.Copy).then_inc(y_read, 1)

        @block.tensor
        def _(e):
            e.sem_inc(w_used, RING)
            with e.Fori(0, number_of_rounds(e)) as r:
                with e.Fori(0, PAIRS) as p:
                    g = r * PAIRS + p
                    e.wait_ge(oh_ready, 2 * g + 1)
                    e.wait_ge(sc_read, 12 * g + 1)
                    for q in range(4):
                        if q >= 2:
                            e.wait_ge(xg_read, 4 * g + (q - 1))
                        for k in range(4 * q, 4 * q + 4):
                            for t, (t0, m) in enumerate(TILES):
                                ins = e.matmul(bank[6 + q % 2][:, (k % 4) * P:(k % 4 + 1) * P], hn[:m, t, k * P:(k + 1) * P], oh[:m, t, :],
                                               start=(t == 0), stop=(t == 2))
                        ins.then_inc(xg_made, 1)
                    e.wait_ge(xg_read, 4 * g + 4)
                    for u in range(8):
                        e.wait_ge(s_w[u % RING], 64 * g + 32 * (u // RING + 1))
                        for k in range(4):
                            for a_ in range(2):
                                kk = 4 * (u % 4) + k
                                ins = e.matmul(half(bank[u // 4], a_), xg[:, kk, SLOTS * a_:SLOTS * a_ + SLOTS],
                                               w[:, u % RING, a_, DE * k:DE * k + DE], start=(kk == 0), stop=(kk == KT - 1))
                            if k == 3:
                                ins.then_inc(w_used, 1)
                        if u % 4 == 3:
                            e.wait_ge(w_used, g * UNITS + (u + 1 + RING))
                            e.sem_inc(h_made, 1)
                    e.wait_ge(u_done, g + 1)
                    for t, (t0, m) in enumerate(TILES):
                        ins = e.transpose(bank[1][:, t0:t0 + m], og[:m, t, :], cw("ident")[:m, :m])
                    ins.then_inc(sg_made, 1)
                    for f in range(4):
                        ins = e.transpose(bank[0][:, f * P:(f + 1) * P], u2[:, f * P:(f + 1) * P], cw("ident"))
                    ins.then_inc(ut_made, 1)
                    e.wait_ge(ut_read, g + 1)
                    for f in range(4):
                        u = 8 + f
                        e.wait_ge(s_w[u % RING], 64 * g + 32 * (u // RING + 1))
                        for c in range(4):
                            for a_ in range(2):
                                ins = e.matmul(half(bank[2 + c], a_), ut[:, f, SLOTS * a_:SLOTS * a_ + SLOTS],
                                               w[:, u % RING, a_, CH * c:CH * c + CH], start=(f == 0), stop=(f == 3))
                        ins.then_inc(w_used, 1)
                    e.wait_ge(w_used, g * UNITS + (UNITS + RING))
                    e.sem_inc(y_made, 1)
                    e.wait_ge(sg_read, g + 1)
                    e.wait_ge(y_read, 4 * g + 4)
                    for i in range(12):
                        t, c = divmod(i, 4)
                        t0, m = TILES[t]
                        if i >= 2:
                            e.wait_ge(sc_read, 12 * g + i)
                        e.matmul(bank[6 + i % 2][:m, :], sg[:, t0:t0 + m], ys[:, CH * c:CH * c + CH], start=True, stop=True).then_inc(sc_made, 1)


def finish(ph, I, O, S):
    nc, pool_dma_sem, sem, bank, cm, cw, pcol, prm, fr = ph
    x1 = S["x1"]
    with ExitStack() as tmp:
        al = lambda n, s, d=F32: tmp.enter_context(nc.sbuf_tensor(n, s, d))
        junk = al("junk4", [P, D])
        st_ = al("stats4", [P, 4, 3])
        gf = al("gf", [P, D])
    s_g, sq, ms, rt, rc, fo, s_o = [sem("f_" + n) for n in ("gain_in", "squares", "mean", "root", "recip", "out", "stored")]
    with nc.Block() as block:
        @block.sync
        def _(sp):
            sp.dma_start(gf[:, :], I["g_final"].partition_broadcast(P)).then_inc(s_g, 16)
            for t, (t0, m) in enumerate(TILES):
                sp.wait_ge(fo, t + 1)
                dst = O["y_p"][0] if t < 2 else O["y_s"].rearrange("b t d -> (b t) d")
                sp.dma_start(dst[t0 % SP_:t0 % SP_ + m, :], x1[:m, t, :]).then_inc(s_o, 16)
            sp.wait_ge(s_o, 48)

        @block.scalar
        def _(a):
            for t, (t0, m) in enumerate(TILES):
                if t:
                    a.wait_ge(sq, t)
                a.activation(junk[:m, :], x1[:m, t, :], ACT.Square, accum_out=st_[:m, 0, t:t + 1]).then_inc(sq, 1)
            for t, (t0, m) in enumerate(TILES):
                a.wait_ge(ms, t + 1)
                a.activation(st_[:m, 2, t:t + 1], st_[:m, 1, t:t + 1], ACT.Sqrt).then_inc(rt, 1)

        @block.vector
        def _(v):
            for t, (t0, m) in enumerate(TILES):
                v.wait_ge(sq, t + 1)
                v.tensor_scalar(st_[:m, 1, t:t + 1], st_[:m, 0, t:t + 1], 1.0 / D, EPS, ALU.mult, ALU.add).then_inc(ms, 1)
            v.wait_ge(s_g, 16)
            for t, (t0, m) in enumerate(TILES):
                v.wait_ge(rt, t + 1)
                v.reciprocal(st_[:m, 3, t:t + 1], st_[:m, 2, t:t + 1]).then_inc(rc, 1)
                v.wait_ge(rc, t + 1)
                v.scalar_tensor_tensor(x1[:m, t, :], x1[:m, t, :], st_[:m, 3, t:t + 1], gf[:m, :], ALU.mult, ALU.mult).then_inc(fo, 1)


_INS = ["x_prompt", "x_sample", "mem_prompt", "cache_k", "cache_v", "cache_idx_k", "page_table", "state_wkv",
        "state_shift", "cache_mem_k", "cache_mem_v", "g_mix", "w_in", "mu_shift", "rw_w0", "rw_w2", "rw_a0", "rw_a2",
        "rw_g2", "rw_kk", "rw_ka", "rw_rk", "rw_ln_g", "rw_ln_b", "w_out", "g_cross", "g_mem", "w_cq", "w_ck", "w_cv",
        "w_co", "g_ffn", "w_rg", "b_rg", "w_re", "b_re", "w_e1", "w_e3", "w_e2", "rel_bias", "g_final"]
_OUTS = [("y_p", (1, 256, 2048)), ("y_s", (8, 8, 2048)), ("k_p", (1, 1, 256, 16, 64)), ("v_p", (1, 1, 256, 16, 64)),
         ("ik_p", (1, 1, 256, 64)), ("wkv_p", (1, 1, 16, 64, 64)), ("shift_p", (1, 1, 3328)),
         ("mk_p", (1, 1, 256, 4, 128)), ("mv_p", (1, 1, 256, 4, 128)), ("k_s", (1, 8, 8, 16, 64)),
         ("v_s", (1, 8, 8, 16, 64)), ("ik_s", (1, 8, 8, 64)), ("wkv_s", (1, 8, 16, 64, 64)), ("shift_s", (1, 8, 3328))]


def kernel(**inputs):
    import numpy as _np
    import concourse.bacc as _bacc
    from concourse import mybir as _mybir
    from concourse.bass_utils import run_bass_kernel_spmd as _run

    nc = _bacc.Bacc("TRN2", target_bir_lowering=False, num_devices=1)
    arrays, ins, cons, outs = {}, {}, {}, {}
    for name in _INS:
        a = _np.ascontiguousarray(inputs[name])
        arrays[f"in_{name}"] = a
        ins[name] = nc.dram_tensor(f"in_{name}", a.shape, _mybir.dt.from_np(a.dtype), kind="ExternalInput").ap()
    for name, a in CONSTS.items():
        arrays[name] = a
        cons[name] = nc.dram_tensor(name, a.shape, _mybir.dt.from_np(a.dtype), kind="ExternalInput").ap()
    for name, shape in _OUTS:
        outs[name] = nc.dram_tensor(f"out_{name}", shape, F32, kind="ExternalOutput").ap()
    build(nc, ins, outs, cons)
    r = _run(nc, [arrays], core_ids=[0])
    return tuple(r.results[0][f"out_{name}"] for name, _ in _OUTS)
```

```python
from contextlib import ExitStack

import numpy as np

import concourse.bass as bass
from concourse import mybir

F32 = mybir.dt.float32
I32 = mybir.dt.int32
ALU = mybir.AluOpType
ACT = mybir.ActivationFunctionType
AXX = mybir.AxisListType.X

P = 128
D = 2048
KT = D // P
SP_, SS = 256, 64
TOK = SP_ + SS
DB, T = 8, 8
TILES = [(0, 128), (128, 128), (256, 64)]
HD = 64
NH = 16
HP = NH // 2
RWT = 26
RWP = RWT * P
ATC = 4176
ATT = 33
AT = NH * HD
IDXW = NH ** -0.5 * HD ** -0.5
CH = 512
CP, CS = 16, 8
PAST, PAGE, NPG = 1024, 128, 8
KEYS = PAST + SS
NEG = -1.0e30
XW, XH, MEM = 512, 4, 256
NE, NG, EPG, DE = 32, 4, 8, 512
EPS = 1e-6
SLOTS = 64
RING = 6
GN_EPS = 64e-5
TOPK_P, TOPK_S = 64, 256
REV = 1536

PRM_ORDER = [("mu_shift", 26), ("g_mix", 16), ("rw_w0", 8), ("rw_a0", 8), ("rw_kk", 8), ("rw_ka", 8), ("rw_rk", 8),
             ("rw_ln_g", 8), ("rw_ln_b", 8), ("g_cross", 16), ("PAD", 14), ("g_ffn", 16), ("g_mem", 16)]
PRM = {}
_at = 0
for _n, _k in PRM_ORDER:
    PRM[_n] = (_at, _k)
    _at += _k
PRM_GROUPS = (P - PRM.pop("PAD")[1], _at - P)


def consts():
    p = np.arange(P)
    out = {}
    ident = np.eye(P, dtype=np.float32)
    bones = (p[:, None] // HD == p[None, :] // HD).astype(np.float32)

    def chunk_masks(m, c):
        s, t = np.arange(m)[:, None], np.arange(m)[None, :]
        same = s // c == t // c
        return np.stack([same & (s < t), same & (s <= t)], 1), same & (t < s)

    ab16, lo16 = chunk_masks(128, CP)
    ab8, lo8 = chunk_masks(64, CS)
    scan = np.ones(TOK)
    scan[0:SP_:CP] = 0
    scan[SP_::CS] = 0
    em16 = (p[:, None] % 64) // CP == np.arange(4)[None, :]
    em8 = (p[:, None] % 32) // CS == np.arange(4)[None, :]
    pad = lambda a: np.concatenate([a.reshape(a.shape[0], -1), np.zeros((P - a.shape[0], a[0].size))], 0)
    cols = [("ident", ident), ("bones", bones), ("ab16", ab16), ("lo16", lo16), ("ab8", pad(ab8)), ("lo8", pad(lo8)),
            ("scan", np.broadcast_to(scan, (P, TOK))), ("em16", em16), ("em8", em8)]
    where, at, parts = {}, 0, []
    for n, a in cols:
        a = a.reshape(P, -1).astype(np.float32)
        where[n] = (at, a.shape[1])
        at += a.shape[1]
        parts.append(a)
    out["c_main"] = np.ascontiguousarray(np.concatenate(parts, 1))

    q = np.arange(2 * P)
    cn = np.where(np.arange(SP_)[None, :] <= q[:, None], 0, NEG).reshape(2, P, SP_).transpose(1, 0, 2)
    bq = np.arange(SS)
    cns = np.where((bq[:, None] // T == bq[None, :] // T) & (bq[None, :] % T <= bq[:, None] % T), 0, NEG)
    hq = np.arange(P)
    rep = np.stack([(bq[:, None] // T == b) & (bq[:, None] % T == hq[None, :] % T) for b in range(DB)], 1)
    reph = np.zeros((P, P))
    reph[64:80] = np.arange(NH)[:, None] == hq[None, :] // T
    dqq = hq[:, None] % T == bq[None, :] % T
    at, parts = 0, []
    for n, a in [("cn", cn), ("cns", pad(cns)), ("rep", pad(rep)), ("reph", reph), ("dqq", dqq), ("iota", p[:, None])]:
        a = a.reshape(P, -1).astype(np.float32)
        where[n] = (at, a.shape[1])
        at += a.shape[1]
        parts.append(a)
    out["c_dsa"] = np.ascontiguousarray(np.concatenate(parts, 1))
    at, parts = 0, []
    for n, a in [("ones", np.ones((P, P))), ("upto", p[:, None] <= p[None, :]), ("iota_slots", np.broadcast_to(np.arange(SLOTS), (P, SLOTS)))]:
        a = a.reshape(P, -1).astype(np.float32)
        where[n] = (at, a.shape[1])
        at += a.shape[1]
        parts.append(a)
    out["c_moe"] = np.ascontiguousarray(np.concatenate(parts, 1))
    dist = np.maximum(PAST + T - 1 - np.arange(REV), 0)
    far = 16 + (np.log(np.maximum(dist, 1).astype(np.float32) / np.float32(16)) / np.float32(np.log(8.0)) * np.float32(16)).astype(np.int32)
    bucket = np.where(dist < 16, dist, np.minimum(far, 31))
    out["c_bkt"] = (np.arange(32)[:, None] == bucket[None, :]).astype(np.float32)
    return out, where


CONSTS, CW = consts()


def cmw(cmo, n):
    return cmo[:, CW[n][0]:CW[n][0] + CW[n][1]]


def cdw(cd, n):
    return cd[:, CW[n][0]:CW[n][0] + CW[n][1]]


def build(nc, I, O, C):
    st = ExitStack()
    with st:
        def keep(name, shape, dt=F32):
            return st.enter_context(nc.sbuf_tensor(name, shape, dt))

        sems = Semaphores(nc, st)
        sem, pool_dma_sem = sems.new, sems.of_pool_dma
        bank = [st.enter_context(nc.psum_tensor(f"bank{i}", [P, 512], F32)) for i in range(8)]
        cm = keep("cm", [P, CONSTS["c_main"].shape[1]])
        cw = lambda n: cm[:, CW[n][0]:CW[n][0] + CW[n][1]]
        prm = keep("prm", [P, 2, P])
        pcol = lambda n: prm[:, PRM[n][0] // P, PRM[n][0] % P:PRM[n][0] % P + PRM[n][1]]
        fr = keep("fr", [P, RWT, TOK])
        ph = (nc, pool_dma_sem, sem, bank, cm, cw, pcol, prm, fr)
        fat_d = nc.dram_tensor("fat_d", (P, ATT, TOK), F32, kind="Internal").ap()
        project(ph, I, C, fat_d)
        sems.clear()
        with ExitStack() as tmp:
            al = lambda n, s, d=F32: tmp.enter_context(nc.sbuf_tensor(n, s, d))
            R = {"t": [al(f"t{i}", [P, HP, TOK])[:, :, :] for i in range(1, 7)] + [al("ar", [P, 2, HP, TOK])]}
            R["al"] = al
            rwkv_prepare(ph, I, O, R)
            sems.clear()
            rwkv_core(ph, I, O, R)
            sems.clear()
            rwkv_finish(ph, I, O, R)
            sems.clear()
        rev_d = nc.dram_tensor("rev_d", (NH, REV), F32, kind="Internal").ap()
        tp_d = nc.dram_tensor("tp_d", (NH, P, 3 * P), F32, kind="Internal").ap()
        bs_d = nc.dram_tensor("bs_d", (NH, T, KEYS), F32, kind="Internal").ap()
        with ExitStack() as tmp:
            al = lambda n, s, d=F32: tmp.enter_context(nc.sbuf_tensor(n, s, d))
            S = {"ik2": al("ik2", [P, TOK]), "vt": al("vt", [P, 3, AT]), "ikw": al("ikw", [P, 3, 80]),
                 "cd": al("cd", [P, CONSTS["c_dsa"].shape[1]]), "nm": al("nm", [P, 2, SP_]),
                 "iqs": al("iqs", [P, DB, HP, 2, T]), "wts": al("wts", [P, 576]), "qs": al("qs", [P, 2, 1152]),
                 "qn": al("qn", [P, HP, SS]), "kn": al("kn", [P, HP, SS])}
            with ExitStack() as tmp2:
                S["fa"] = tmp2.enter_context(nc.sbuf_tensor("fa2", [P, ATT, TOK], F32))
                dsa_prepare(ph, I, O, C, fat_d, rev_d, tp_d, bs_d, S)
                sems.clear()
                dsa_prompt(ph, I, O, tp_d, S)
                sems.clear()
            dsa_sample(ph, I, O, bs_d, S)
            sems.clear()
        x1 = keep("x1", [P, 3, D])
        with ExitStack() as tmp:
            al = lambda n, s, d=F32: tmp.enter_context(nc.sbuf_tensor(n, s, d))
            S = {"x1": x1, "mk": al("mk", [P, 2, XW]), "mv": al("mv", [P, 2, XW]), "mkt": al("mkt", [P, XH, MEM]), "qt": al("qt", [P, XH, TOK])}
            mix_out(ph, I, O, S)
            sems.clear()
            cross(ph, I, O, S)
            sems.clear()
        with ExitStack() as tmp:
            al = lambda n, s, d=F32: tmp.enter_context(nc.sbuf_tensor(n, s, d))
            S = {"x1": x1, "hn": al("hn", [P, 3, D]), "cmo": al("cmo", [P, CONSTS["c_moe"].shape[1]]), "c_moe": C["c_moe"],
                 "gates": al("gates", [P, 3, NE]), "slot": al("slot", [P, 3, NE]), "rounds": al("rounds", [P, 1], I32)}
            route(ph, I, S)
            sems.clear()
            experts(ph, I, S)
            sems.clear()
            finish(ph, I, O, S)


class Semaphores:

    def __init__(self, nc, kept):
        self.kept = kept
        self.nc, self.live, self.stack = nc, [], ExitStack()

    def new(self, name):
        self.live.append(self.stack.enter_context(self.nc.semaphore(name)))
        return self.live[-1]

    def of_pool_dma(self, name):
        return self.kept.enter_context(self.nc.semaphore(name))

    def clear(self):
        with self.nc.Block() as block:
            @block.sync
            def _(sp):
                for s in self.live:
                    sp.sem_clear(s)
        self.stack.close()
        self.live, self.stack = [], ExitStack()


def chain_of(eng, sem):
    n = [0]

    def step(ins):
        n[0] += 1
        ins.then_inc(sem, 1)
        eng.wait_ge(sem, n[0])
    return step


def norm_to_features(ph, tag, x, sizes, gain, ht, wait_x, tb, scratch, out=None):
    nc, pool_dma_sem, sem, bank, cm, cw, pcol, prm, fr = ph
    junk, stats = scratch
    out = x if out is None else out
    ssq, msq, rtd, rst, hrm, tpm, tpr = [sem(f"{tag}_{n}") for n in
                                         ("squares", "mean", "root", "recip", "scaled", "turned", "taken")]
    n = len(sizes)

    def act(a):
        for t, m in enumerate(sizes):
            wait_x(a, t)
            if t:
                a.wait_ge(ssq, t)
            a.activation(junk[:m, :], x[:m, t, :], ACT.Square, accum_out=stats[:m, 0, t:t + 1]).then_inc(ssq, 1)
        for t, m in enumerate(sizes):
            a.wait_ge(msq, t + 1)
            a.activation(stats[:m, 2, t:t + 1], stats[:m, 1, t:t + 1], ACT.Sqrt).then_inc(rtd, 1)
        for t, m in enumerate(sizes):
            a.wait_ge(rst, t + 1)
            a.activation(out[:m, t, :], x[:m, t, :], ACT.Copy, scale=stats[:m, 3, t:t + 1]).then_inc(hrm, 1)

    def dve(v):
        for t, m in enumerate(sizes):
            v.wait_ge(ssq, t + 1)
            v.tensor_scalar(stats[:m, 1, t:t + 1], stats[:m, 0, t:t + 1], 1.0 / D, EPS, ALU.mult, ALU.add).then_inc(msq, 1)
        for t, m in enumerate(sizes):
            v.wait_ge(rtd, t + 1)
            v.reciprocal(stats[:m, 3, t:t + 1], stats[:m, 2, t:t + 1]).then_inc(rst, 1)
        for t, m in enumerate(sizes):
            for q in range(KT // 4):
                v.wait_ge(tpm, 4 * t + q + 1)
                v.tensor_tensor(ht[:, 4 * q:4 * q + 4, 128 * t:128 * t + m],
                                bank[tb[q % 2]][:, 0:4 * m].rearrange("p (a m) -> p a m", a=4),
                                gain[:, 4 * q:4 * q + 4].unsqueeze(2).to_broadcast([P, 4, m]), ALU.mult).then_inc(tpr, 1)

    def pe(e):
        for t, m in enumerate(sizes):
            e.wait_ge(hrm, t + 1)
            for q in range(KT // 4):
                g = 4 * t + q
                if g >= 2:
                    e.wait_ge(tpr, g - 1)
                for a in range(4):
                    k = 4 * q + a
                    ins = e.transpose(bank[tb[q % 2]][:, a * m:(a + 1) * m], out[:m, t, k * P:(k + 1) * P],
                                      cw("ident")[:m, :m])
                ins.then_inc(tpm, 1)
    return act, dve, pe, (tpr, 4 * n)


def project(ph, I, C, fat_d):
    nc, pool_dma_sem, sem, bank, cm, cw, pcol, prm, fr = ph
    with ExitStack() as tmp:
        al = lambda n, s, d=F32: tmp.enter_context(nc.sbuf_tensor(n, s, d))
        fa = al("fa", [P, ATT, TOK])
        x = al("x", [P, 3, D])
        junk = al("junk", [P, D])
        stats = al("stats", [P, 4, 3])
        ht = al("ht", [P, KT, TOK])
        w = al("w", [P, 2, KT, CH])
        prin = al("prin", [P, 2, P])
    s_c, s_x, s_prin = sem("consts_in"), sem("x_in"), sem("params_in")
    s_prt, s_prm = sem("params_turned"), sem("params_ready")
    s_w = [sem("win0_in"), sem("win1_in")]
    f_made, f_read, s_sp = sem("f_made"), sem("f_read"), sem("fat_out")
    win = I["w_in"][0].rearrange("(kt p) n -> p kt n", p=P)
    gain = pcol("g_mix")
    act_n, dve_n, pe_n, (tpr, nt) = norm_to_features(
        ph, "mix", x, [m for _, m in TILES], gain, ht, lambda e, t: e.wait_ge(s_x, 48), (6, 7), (junk, stats))
    n_rw = RWP // CH

    with nc.Block() as block:
        @block.sync
        def _(sp):
            def load(buf, col, width):
                sp.dma_start(w[:, buf, :, 0:width], win[:, :, col:col + width] if isinstance(col, int)
                             else win[:, :, bass.DynSlice(col, width)]).then_inc(s_w[buf], 16)
            sp.dma_start(cm[:, :], C["c_main"]).then_inc(s_c, 16)
            for t, (t0, m) in enumerate(TILES):
                src = I["x_prompt"][0] if t < 2 else I["x_sample"].rearrange("b t d -> (b t) d")
                sp.dma_start(x[:m, t, :], src[t0 % SP_:t0 % SP_ + m, :]).then_inc(s_x, 16)
            load(0, 0, CH)
            load(1, CH, CH)
            with sp.Fori(1, n_rw // 2) as i:
                for b in range(2):
                    sp.wait_ge(f_made, 8 * i + 4 * b - 4)
                    load(b, (2 * i + b) * CH, CH)
            sp.wait_ge(f_made, 4 * (n_rw - 1))
            load(0, n_rw * CH, CH // 2)
            for c in range(2):
                sp.wait_ge(f_made, 24 if c == 0 else 26)
                load((c + 1) % 2, RWP + c * CH, CH)
            with sp.Fori(1, 4) as i:
                for b in range(2):
                    sp.wait_ge(f_made, 22 + 8 * i + 4 * b)
                    load((b + 1) % 2, RWP + (2 * i + b) * CH, CH)
            sp.wait_ge(f_made, 26 + 4 * 7)
            load(1, RWP + 8 * CH, 80)
            sp.wait_ge(f_read, 59)
            sp.dma_start(fat_d[:, 0:ATT - 1, :], fa[:, 0:ATT - 1, :]).then_inc(s_sp, 16)
            sp.dma_start(fat_d[0:80, ATT - 1, :], fa[0:80, ATT - 1, :]).then_inc(s_sp, 16)
            sp.wait_ge(s_sp, 32)

        @block.scalar
        def _(a):
            for name, (r0, k) in PRM.items():
                src = (I[name][0] if name != "rw_rk" else I[name][0].rearrange("h d -> (h d)")).rearrange("(r p) -> r p", p=P)
                a.dma_start(prin[r0 % P:r0 % P + k, r0 // P, :], src).then_inc(s_prin, 16)
            act_n(a)

            def take(n, dst, width, b):
                a.wait_ge(f_made, n + 1)
                a.activation(dst, bank[b][:width, 0:TOK], ACT.Copy).then_inc(f_read, 1)
            with a.Fori(0, n_rw) as i:
                for j in range(4):
                    take(4 * i + j, fr[:, bass.DynSlice(4 * i + j, 1), :], P, j)
            for j in range(2):
                take(24 + j, fr[:, 24 + j, :], P, j)
            with a.Fori(0, 8) as i:
                for j in range(4):
                    take(26 + 4 * i + j, fa[:, bass.DynSlice(4 * i + j, 1), :], P, (j + 2) % 4)
            take(58, fa[:80, 32, :], 80, 2)

        @block.vector
        def _(v):
            for g, r in enumerate(PRM_GROUPS):
                v.wait_ge(s_prt, 2)
                v.tensor_copy(prm[:, g, 0:r], bank[5][:, g * P:g * P + r]).then_inc(s_prm, 1)
            v.wait_ge(s_prm, 2)
            dve_n(v)

        @block.tensor
        def _(e):
            e.wait_ge(s_c, 16)
            e.wait_ge(s_prin, 16 * len(PRM))
            for g, r in enumerate(PRM_GROUPS):
                e.transpose(bank[5][:, g * P:g * P + r], prin[:r, g, :], cw("ident")[:r, :r]).then_inc(s_prt, 1)
            pe_n(e)
            e.wait_ge(tpr, nt)

            def chunk(buf, landed, n0, widths, b0, first=False):
                e.wait_ge(s_w[buf], landed)
                for j, width in enumerate(widths):
                    if not first:
                        e.wait_ge(f_read, n0 + j - 3)
                    out = bank[(b0 + j) % 4][:width, 0:TOK]
                    for k in range(KT):
                        ins = e.matmul(out, w[:, buf, k, j * P:j * P + width], ht[:, k, :], start=(k == 0), stop=(k == KT - 1))
                    ins.then_inc(f_made, 1)
            full = [P] * 4
            chunk(0, 16, 0, full, 0, first=True)
            chunk(1, 16, 4, full, 0)
            with e.Fori(1, n_rw // 2) as i:
                for b in range(2):
                    chunk(b, 16 * i + 16, 8 * i + 4 * b, full, 0)
            chunk(0, 64, 24, [P] * 2, 0)
            with e.Fori(0, 4) as i:
                for b in range(2):
                    chunk((b + 1) % 2, (16 * i + 64) if b == 0 else (16 * i + 80), 26 + 8 * i + 4 * b, full, 2)
            chunk(1, 16 * 8, 58, [80], 2)



class Tick:

    def __init__(self, sem):
        self.sem, self.n = sem, 0

    def on(self, ins):
        self.n += 1
        ins.then_inc(self.sem, 1)
        return self

    def own(self, eng):
        eng.wait_ge(self.sem, self.n)


def rwkv_prepare(ph, I, O, R):
    nc, pool_dma_sem, sem, bank, cm, cw, pcol, prm, fr = ph
    t1, t2, t3, t4, t5, t6, ar = R["t"]
    with ExitStack() as tmp:
        al = lambda n, s, d=F32: tmp.enter_context(nc.sbuf_tensor(n, s, d))
        w2a2 = al("w2a2", [P, NH * HD])
        g2 = al("g2", [P, NH * HD])
        ssin = al("ssin", [104, 2, P])
        ss = al("ss", [P, DB, RWT])
        sho = al("sho", [P, 9, RWT])
        shw = al("shw", [104, 3, P])
    s_in, s_ss = sem("lora_in"), sem("state_shift_in")
    ss_turned, sho_ready, sho_turned, sho_sb, s_sho = [sem(n) for n in (
        "ss_turned", "shift_rows_ready", "shift_rows_turned", "shift_rows_copied", "shift_rows_out")]
    dch = sem("prep_dve_chain")
    shifted, squashed, sq_ready, bp_ready, le_ready, bon_done, r_free = [sem(n) for n in (
        "shifted", "lora_squashed", "kk_squares", "bonus_products", "log_decay_ready", "bonus_done", "r_free")]
    exps = sem("decay_exps")
    z_made, z_read = sem("z_made"), sem("z_read")
    rr, kk, vv = fr[:, 0:8, :], fr[:, 8:16, :], fr[:, 16:24, :]
    bc = lambda name, n=8: pcol(name)[:, 0:n].unsqueeze(2).to_broadcast([P, n, TOK])
    SHG = [(0, 26), (26, 104), (130, 104)]

    with nc.Block() as block:
        @block.sync
        def _(sp):
            sp.dma_start(w2a2[0:64, :], I["rw_w2"][0]).then_inc(s_in, 16)
            sp.dma_start(w2a2[64:P, :], I["rw_a2"][0]).then_inc(s_in, 16)
            sp.dma_start(g2[:, :], I["rw_g2"][0]).then_inc(s_in, 16)
            src = I["state_shift"][0].rearrange("b (c p) -> (b c) p", p=P)
            for g in range(2):
                sp.dma_start(ssin[:, g, :], src[104 * g:104 * g + 104, :]).then_inc(s_ss, 16)
            sp.wait_ge(sho_sb, 3)
            sp.dma_start(O["shift_p"][0, 0].rearrange("(c p) -> c p", p=P), shw[0:26, 0, :]).then_inc(s_sho, 16)
            dst = O["shift_s"][0].rearrange("b (c p) -> (b c) p", p=P)
            for g in range(2):
                sp.dma_start(dst[104 * g:104 * g + 104, :], shw[:, 1 + g, :]).then_inc(s_sho, 16)
            sp.wait_ge(s_sho, 48)

        @block.vector
        def _(v):
            d = chain_of(v, dch)
            v.tensor_copy(sho[:, :, :], fr[:, :, SP_ - 1:TOK:8].rearrange("p c i -> p i c")).then_inc(sho_ready, 1)
            v.wait_ge(sho_ready, 1)
            v.wait_ge(ss_turned, 2)
            d(v.tensor_copy(ss[:, :, :], bank[4][:, 0:208].rearrange("p (b c) -> p b c", b=DB)))
            for c0 in (0, 8, 16, 24):
                n = min(8, RWT - c0)
                f, dd = fr[:, c0:c0 + n, :], t1[:, 0:n, :]
                fs_, ds = f[:, :, SP_:].rearrange("p c (b t) -> p c b t", t=T), dd[:, :, SP_:].rearrange("p c (b t) -> p c b t", t=T)
                v.tensor_tensor(dd[:, :, 1:SP_], f[:, :, 0:SP_ - 1], f[:, :, 1:SP_], ALU.subtract)
                v.tensor_scalar(dd[:, :, 0], f[:, :, 0], -1.0, None, ALU.mult)
                v.tensor_tensor(ds[:, :, :, 1:T], fs_[:, :, :, 0:T - 1], fs_[:, :, :, 1:T], ALU.subtract)
                d(v.tensor_tensor(ds[:, :, :, 0], ss[:, :, c0:c0 + n].rearrange("p b c -> p c b"), fs_[:, :, :, 0], ALU.subtract))
                d(v.tensor_tensor(dd, dd, pcol("mu_shift")[:, c0:c0 + n].unsqueeze(2).to_broadcast([P, n, TOK]), ALU.mult))
                ins = v.tensor_tensor(f, f, dd, ALU.add)
                if c0 == 24:
                    ins.then_inc(shifted, 1)
                    v.wait_ge(shifted, 1)
                else:
                    d(ins)
            d(v.tensor_tensor(t4, kk, bc("rw_kk"), ALU.mult))
            v.tensor_tensor(t3, t4, t4, ALU.mult).then_inc(sq_ready, 1)
            v.wait_ge(z_read, 24)
            d(v.tensor_scalar(t6, t6, 1e-12, None, ALU.max))
            d(v.reciprocal(t6, t6))
            d(v.tensor_tensor(t4, t4, t6, ALU.mult))
            d(v.tensor_scalar(t1, t1, -float(np.exp(-0.5)), None, ALU.mult))
            d(v.tensor_scalar(t5, t2, -1.0, None, ALU.add))
            d(v.tensor_tensor(t5, t5, bc("rw_ka"), ALU.mult))
            d(v.scalar_tensor_tensor(kk, t5, 1.0, kk, ALU.add, ALU.mult))
            d(v.tensor_tensor(t5, rr, kk, ALU.mult))
            v.tensor_tensor(t5, t5, bc("rw_rk"), ALU.mult).then_inc(bp_ready, 1)
            for j in range(HP):
                ins = v.tensor_tensor_scan(t3[:, j, :], cw("scan"), t1[:, j, :], 0.0, ALU.mult, ALU.add)
            d(ins)
            v.tensor_tensor(t1, t3, t1, ALU.subtract).then_inc(le_ready, 1)
            v.wait_ge(z_read, 32)
            v.wait_ge(bp_ready, 1)
            v.tensor_tensor(t5, t6, vv, ALU.mult).then_inc(bon_done, 1)
            v.wait_ge(exps, 3)
            d(v.scalar_tensor_tensor(ar[:, 0, :, :], t4, -1.0, t1, ALU.mult, ALU.mult))
            v.tensor_tensor(ar[:, 1, :, :], rr, t6, ALU.mult).then_inc(r_free, 1)
            d(v.tensor_tensor(t4, t4, t2, ALU.mult))
            d(v.tensor_tensor(t4, t4, t3, ALU.mult))
            d(v.tensor_tensor(kk, kk, t3, ALU.mult))
            for src, dst in ((t4, t1), (kk, t2)):
                for a, b, c in ((0, SP_, CP), (SP_, TOK, CS)):
                    n = (b - a) // c
                    cut = lambda z: z[:, :, a:b].rearrange("p h (n c) -> p h n c", c=c)
                    end = t6[:, :, a + c - 1:b:c].unsqueeze(3).to_broadcast([P, HP, n, c])
                    d(v.tensor_tensor(cut(dst), cut(src), end, ALU.mult))

        @block.scalar
        def _(a):
            a.wait_ge(shifted, 1)
            a.activation(fr[0:64, 24, :], fr[0:64, 24, :], ACT.Tanh).then_inc(squashed, 1)
            a.activation(fr[:, 25, :], fr[:, 25, :], ACT.Sigmoid).then_inc(squashed, 1)

            def take(n, dst, func, bias=0.0):
                a.wait_ge(z_made, n + 1)
                a.activation(dst, bank[n % 4][:, 0:TOK], func, **({} if func == ACT.Copy else {"bias": bias})).then_inc(z_read, 1)
            for j in range(8):
                take(j, t1[:, j, :], ACT.Sigmoid, pcol("rw_w0")[:, j:j + 1])
            for j in range(8):
                take(8 + j, t2[:, j, :], ACT.Sigmoid, pcol("rw_a0")[:, j:j + 1])
            for j in range(8):
                take(16 + j, t6[:, j, :], ACT.Sqrt)
            for j in range(8):
                take(24 + j, t6[:, j, :], ACT.Copy)
            for g, (r0, k) in enumerate(SHG):
                a.wait_ge(sho_turned, 3)
                a.activation(shw[:k, g, :], bank[5][:k, g * P:(g + 1) * P], ACT.Copy).then_inc(sho_sb, 1)
            a.wait_ge(le_ready, 1)
            a.activation(t1, t1, ACT.Exp).then_inc(exps, 1)
            a.wait_ge(bon_done, 1)
            a.activation(t6, t3, ACT.Exp).then_inc(exps, 1)
            a.wait_ge(exps, 2)
            a.activation(t3, t3, ACT.Exp, scale=-1.0).then_inc(exps, 1)
            for j in range(8):
                take(32 + j, fr[:, j, :], ACT.Copy)

        @block.tensor
        def _(e):
            e.wait_ge(s_ss, 32)
            for g in range(2):
                e.transpose(bank[4][:, 104 * g:104 * g + 104], ssin[:, g, :], cw("ident")[:104, :104]).then_inc(ss_turned, 1)
            e.wait_ge(sho_ready, 1)
            flat = sho[:, :, :].rearrange("p i c -> p (i c)")
            for g, (r0, k) in enumerate(SHG):
                e.transpose(bank[5][:k, g * P:(g + 1) * P], flat[:, r0:r0 + k], cw("ident")).then_inc(sho_turned, 1)
            e.wait_ge(s_in, 48)
            e.wait_ge(squashed, 2)
            n = 0
            for kind in ("decay", "iclr", "norm", "bonus", "gate"):
                if kind == "norm":
                    e.wait_ge(sq_ready, 1)
                if kind == "bonus":
                    e.wait_ge(bp_ready, 1)
                if kind == "gate":
                    e.wait_ge(r_free, 1)
                for j in range(8):
                    c = slice(j * P, (j + 1) * P)
                    lhs, rhs = {"decay": (w2a2[0:64, c], fr[0:64, 24, :]), "iclr": (w2a2[64:P, c], fr[64:P, 24, :]),
                                "norm": (cw("bones"), t3[:, j, :]), "bonus": (cw("bones"), t5[:, j, :]),
                                "gate": (g2[:, c], fr[:, 25, :])}[kind]
                    if n >= 4:
                        e.wait_ge(z_read, n - 3)
                    e.matmul(bank[n % 4][:, 0:TOK], lhs, rhs, start=True, stop=True).then_inc(z_made, 1)
                    n += 1


def rwkv_core(ph, I, O, R):
    nc, pool_dma_sem, sem, bank, cm, cw, pcol, prm, fr = ph
    t1, t2, t3, t4, t5, t6, ar = R["t"]
    yt = t3
    kk, vv = fr[:, 8:16, :], fr[:, 16:24, :]
    with ExitStack() as tmp:
        al = lambda n, s, d=F32: tmp.enter_context(nc.sbuf_tensor(n, s, d))
        mts = al("mt", [P, 2, 4, 8, HD])
        nns = al("nn", [P, 2, 4, 8, HD])
        qys = al("qy", [P, 2, 2, 4, P])
        tm = al("tm", [P, 2, 4, P])
        ab = al("ab", [P, 4, 2, P])
        ak = al("ak", [P, 4, 2, P])
        a1 = al("a1", [P, 4, P])
        pw = al("pw", [P, 2, 2, 4, P])
        xx = al("xx", [P, 4, P])
        bx = al("bx", [P, 2, 4, P])
        vx = al("vx", [P, 2, 4, P])
        wx = al("wx", [P, 4, 4, HD])
        sta = al("sta", [P, 4, HD])
        stb = al("stb", [P, 4, HD])
        stt = al("stt", [P, 4, HD])
        si = al("si", [HD, 2, 8, HD])
        so = al("so", [HD, 2, 4, P])
    tm_made, tm_read, ab_made, ab_read = sem("tm_made"), sem("tm_read"), sem("ab_made"), sem("ab_read")
    akv_made, x_begun, xm_made, x_added = sem("akv_made"), sem("x_begun"), sem("xm_made"), sem("x_added")
    sq_made, sq_read, bv_spread, w_spread = sem("sq_made"), sem("sq_read"), sem("bv_spread"), sem("w_spread")
    map_made, map_read, add_read, qy_read = sem("map_made"), sem("map_read"), sem("add_read"), sem("qy_read")
    qy_made, add_made = sem("qy_made"), sem("add_made")
    st_ready, ser_made, y_read, si_turned = sem("state_ready"), sem("step_made"), sem("y_read"), sem("si_turned")
    si_in = [sem("si_in0"), sem("si_in1")]
    so_turned, so_read = sem("so_turned"), sem("so_read")
    so_out = [pool_dma_sem(f"so_out{i}") for i in range(2)]
    cch = sem("core_dve_chain")
    nit = 4
    E = 4
    MAPB, ADDB = (2, 3), (4, 5)
    QYB, CHB = 6, 7
    SQB = [(2, 3), (4, 5), (6,)]
    ident = cw("ident")
    GROUPS = [(hg, ti) for hg in range(2) for ti in (2, 0, 1)]
    NGR = len(GROUPS)
    EXPORTS = [(hg, b) for hg in range(2) for b in list(range(DB)) + [None]]

    def quads():
        for gi, (hg, ti) in enumerate(GROUPS):
            t0, m = TILES[ti]
            for q in range(2):
                yield 2 * gi + q, gi, hg, ti, t0, m, q, 4 * hg + 2 * q

    def parts(gi, place):
        if gi == 0:
            return
        hg, ti = GROUPS[gi - 1]
        c, odd = divmod(place, 2)
        if ti == 2:
            if odd:
                yield "step", gi - 1, c
            else:
                if c:
                    yield "export", gi - 1, c - 1
                yield "load", gi - 1, c
        elif odd:
            yield "step", gi - 1, c
        if place == 15 and ti:
            yield "export", gi - 1, c

    with nc.Block() as block:
        @block.sync
        def _(sp):
            n = 0
            for hg in range(2):
                for b in range(DB):
                    if n >= 2:
                        sp.wait_ge(si_turned, n - 1)
                    sp.dma_start(si[:, n % 2, :, :], I["state_wkv"][0, b, 8 * hg:8 * hg + 8].rearrange("h i j -> i h j")).then_inc(si_in[n % 2], 16)
                    n += 1

        @block.gpsimd
        def _(g):
            n = [0]

            def send(gi, places):
                for place in places:
                    for part, cg, c in parts(gi, place):
                        if part != "export":
                            continue
                        hg, b = EXPORTS[n[0]]
                        n[0] += 1
                        g.wait_ge(so_read, n[0])
                        dst = (O["wkv_p"][0, 0] if b is None else O["wkv_s"][0, b])[8 * hg:8 * hg + 8]
                        g.dma_start(dst.rearrange("h i j -> i h j"), so[:, (n[0] - 1) % 2, :, :].rearrange("i a (p j) -> i (a p) j", p=2)).then_inc(so_out[(n[0] - 1) % 2], 16)
            for k, gi, hg, ti, t0, m, q, hp in quads():
                em = cw("em16" if ti < 2 else "em8")[:m, 0:E].unsqueeze(2)
                g.wait_ge(tm_read, 2 * k + 2)
                if k:
                    g.wait_ge(add_made, k)
                for dst, col in ((bx, 1), (vx, 3)):
                    for p_ in range(2):
                        g.tensor_tensor(dst[:m, p_, 0:E, :], tm[:m, p_, col, :].unsqueeze(1).to_broadcast([m, E, P]),
                                        em.to_broadcast([m, E, P]), ALU.mult).then_inc(bv_spread, 1)
                send(gi, range(8 * q, 8 * q + 8))
            send(NGR, range(16))
            for i in range(2):
                g.wait_ge(so_out[i], 16 * (len(EXPORTS) // 2))

        @block.scalar
        def _(a):
            ns = 0
            n = [0]

            def chain(gi, place):
                for part, cg, c in parts(gi, place):
                    if part == "export":
                        a.wait_ge(so_turned, n[0] + 1)
                        if n[0] >= 2:
                            a.wait_ge(so_out[n[0] % 2], 16 * (n[0] // 2))
                        a.activation(so[:, n[0] % 2, :, :], bank[CHB][:HD, :].rearrange("i (a x) -> i a x", a=4), ACT.Copy).then_inc(so_read, 1)
                        n[0] += 1
            for k, gi, hg, ti, t0, m, q, hp in quads():
                for p_ in range(2):
                    a.wait_ge(tm_made, 2 * k + p_ + 1)
                    if k:
                        a.wait_ge(qy_made, k)
                    a.activation(tm[:m, p_, :, :], bank[p_][:m, :].rearrange("t (c x) -> t c x", c=4), ACT.Copy).then_inc(tm_read, 1)
                a.wait_ge(tm_read, 2 * k + 2)
                a.activation(xx[:m, :, 0:HD], tm[:m, :, 0, :].rearrange("t a (p j) -> t a p j", p=2), ACT.Copy).then_inc(x_begun, 1)
                chain(gi, 8 * q)
                a.wait_ge(akv_made, k + 1)
                a.activation(xx[:m, :, HD:P], bank[0][:m, 0:4 * HD].rearrange("t (h j) -> t h j", h=4), ACT.Copy).then_inc(x_begun, 1)
                for it in range(nit - 1):
                    chain(gi, 8 * q + it + 1)
                    for half in range(2 if it < nit - 2 else 1):
                        a.wait_ge(sq_made, ns + 1)
                        a.activation(pw[:m, it % 2, half, :, 0:m], bank[SQB[it][half]][:m, 0:4 * m].rearrange("t (h s) -> t h s", h=4),
                                     ACT.Copy).then_inc(sq_read, 1)
                        ns += 1
                for place in (4, 5):
                    chain(gi, 8 * q + place)
                a.wait_ge(map_made, k + 1)
                for g in range(2):
                    ins = a.activation(mts[:, gi % 2, 2 * q:2 * q + 2, E * g:E * (g + 1), :],
                                       bank[MAPB[g]][:, :].rearrange("p (a c j) -> p a c j", a=2, c=E), ACT.Copy)
                ins.then_inc(map_read, 1)
                for place in (6, 7):
                    chain(gi, 8 * q + place)
            for place in range(16):
                chain(NGR, place)

        @block.vector
        def _(v):
            d = chain_of(v, cch)
            n = {"step": 0, "ready": 0, "load": 0, "export": 0}

            def chain(gi, place):
                for part, cg, c in parts(gi, place):
                    hg, ti = GROUPS[cg]
                    t0, _ = TILES[ti]
                    C = CP if ti < 2 else CS
                    buf = cg % 2
                    if part == "export":
                        n["export"] += 1
                        continue
                    if part == "load" or (ti == 0 and c == 0):
                        if n["export"]:
                            v.wait_ge(so_turned, n["export"])
                        if part == "load":
                            n["load"] += 1
                            v.wait_ge(si_turned, n["load"])
                            v.tensor_copy(sta[:, :, :], bank[CHB][:, 4 * CP:4 * CP + 4 * HD].rearrange("p (a i) -> p a i", a=4)).then_inc(st_ready, 1)
                        else:
                            v.memset(sta[:, :, :], 0.0).then_inc(st_ready, 1)
                        n["ready"] += 1
                        v.wait_ge(st_ready, n["ready"])
                    if part == "load":
                        continue
                    end = t6[:, 4 * hg:4 * hg + 4, t0 + C * (c + 1) - 1].unsqueeze(2).to_broadcast([P, 4, HD])
                    d(v.tensor_tensor(stt[:, :, :], sta[:, :, :], end, ALU.mult))
                    d(v.tensor_tensor(stt[:, :, :], stt[:, :, :], nns[:, buf, :, c, :], ALU.add))
                    n["step"] += 1
                    v.wait_ge(ser_made, n["step"])
                    dst = sta if ti < 2 else stb
                    if ti == 2 and n["export"]:
                        v.wait_ge(so_turned, n["export"])
                    v.tensor_tensor(dst[:, :, :], stt[:, :, :], bank[CHB][:, 4 * CP:4 * CP + 4 * HD].rearrange("p (a i) -> p a i", a=4), ALU.add).then_inc(st_ready, 1)
                    v.tensor_tensor(yt[:, 4 * hg:4 * hg + 4, t0 + C * c:t0 + C * (c + 1)],
                                    bank[CHB][:, 0:4 * C].rearrange("p (a t) -> p a t", a=4),
                                    qys[:, buf, 1, :, C * c:C * (c + 1)], ALU.add).then_inc(y_read, 1)
                    n["ready"] += 1
                    v.wait_ge(st_ready, n["ready"])
            for k, gi, hg, ti, t0, m, q, hp in quads():
                two = cw("ab16" if ti < 2 else "ab8")[:m, :].rearrange("s (a t) -> s a t", a=2)
                low = cw("lo16" if ti < 2 else "lo8")[:m, :]
                for i in range(4):
                    v.wait_ge(ab_made, 6 * k + i + 1)
                    dst = (ab, ak)[i // 2]
                    v.tensor_tensor(dst[:m, i % 2::2, :, 0:m],
                                    bank[2 + i][:m, 0:4 * m].rearrange("s (h a t) -> s h a t", h=2, a=2),
                                    two.unsqueeze(1).to_broadcast([m, 2, 2, m]), ALU.mult).then_inc(ab_read, 1)
                for i in range(2):
                    v.wait_ge(ab_made, 6 * k + 5 + i)
                    v.tensor_tensor(a1[:m, i::2, 0:m], bank[(6, 1)[i]][:m, 0:2 * m].rearrange("s (h t) -> s h t", h=2),
                                    low.unsqueeze(1).to_broadcast([m, 2, m]), ALU.mult).then_inc(ab_read, 1)
                chain(gi, 8 * q)
                v.wait_ge(x_begun, 2 * k + 2)
                for it in range(nit):
                    v.wait_ge(xm_made, 4 * k + it + 1)
                    v.tensor_tensor(xx[:m, :, :], xx[:m, :, :], bank[it % 2][:m, :].rearrange("t (h x) -> t h x", h=4), ALU.add).then_inc(x_added, 1)
                    chain(gi, 8 * q + it + 1)
                    v.wait_ge(x_added, 4 * k + it + 1)
                em = cw("em16" if ti < 2 else "em8")[:m, 0:E].unsqueeze(2).to_broadcast([m, E, HD])
                for h in range(4):
                    v.tensor_tensor(wx[:m, h, 0:E, :], xx[:m, h, HD:P].unsqueeze(1).to_broadcast([m, E, HD]), em, ALU.mult).then_inc(w_spread, 1)
                chain(gi, 8 * q + 5)
                v.wait_ge(add_made, k + 1)
                for g in range(2):
                    ins = v.tensor_copy(nns[:, gi % 2, 2 * q:2 * q + 2, E * g:E * (g + 1), :],
                                        bank[ADDB[g]][:, :].rearrange("p (a c j) -> p a c j", a=2, c=E))
                ins.then_inc(add_read, 1)
                chain(gi, 8 * q + 6)
                v.wait_ge(qy_made, k + 1)
                v.tensor_tensor(qys[:, gi % 2, 0, 2 * q:2 * q + 2, 0:m], bank[QYB][:, 0:2 * m].rearrange("p (a t) -> p a t", a=2),
                                ar[:, 1, hp:hp + 2, t0:t0 + m], ALU.add).then_inc(qy_read, 1)
                v.tensor_copy(qys[:, gi % 2, 1, 2 * q:2 * q + 2, 0:m], bank[QYB][:, 2 * m:4 * m].rearrange("p (a t) -> p a t", a=2)).then_inc(qy_read, 1)
                chain(gi, 8 * q + 7)
                v.wait_ge(add_read, k + 1)
                v.wait_ge(qy_read, 2 * k + 2)
            for place in range(16):
                chain(NGR, place)

        @block.tensor
        def _(e):
            n = {"step": 0, "ready": 0, "load": 0, "export": 0}
            half = lambda z, h: z[HD * (h % 2):HD * (h % 2) + HD]

            def chain(gi, place):
                for part, cg, c in parts(gi, place):
                    hg, ti = GROUPS[cg]
                    C = CP if ti < 2 else CS
                    buf = cg % 2
                    if part == "step" and ti == 0 and c == 0:
                        n["ready"] += 1
                    if part == "step" and c == 0:
                        e.wait_ge(map_read, 2 * cg + 2)
                        e.wait_ge(qy_read, 4 * cg + 4)
                    if n["ready"]:
                        e.wait_ge(st_ready, n["ready"])
                    if n["step"]:
                        e.wait_ge(y_read, n["step"])
                    if n["export"]:
                        e.wait_ge(so_read, n["export"])
                    if part == "load":
                        nb = n["load"]
                        e.wait_ge(si_in[nb % 2], 16 * (nb // 2 + 1))
                        for p_ in range(4):
                            ins = e.transpose(bank[CHB][:, 4 * CP + p_ * HD:4 * CP + (p_ + 1) * HD],
                                              si[:, nb % 2, 2 * p_:2 * p_ + 2, :].rearrange("i h j -> i (h j)"), ident[:HD, :HD])
                        ins.then_inc(si_turned, 1)
                        n["load"] += 1
                        n["ready"] += 1
                    elif part == "step":
                        for p_ in range(4):
                            for h in (0, 1):
                                e.matmul(half(bank[CHB][:, 4 * CP + p_ * HD:4 * CP + (p_ + 1) * HD], h), half(mts[:, buf, p_, c, :], h),
                                         half(sta[:, p_, :], h), start=True, stop=True)
                        for p_ in range(4):
                            for h in (0, 1):
                                ins = e.matmul(half(bank[CHB][:, p_ * C:(p_ + 1) * C], h), half(sta[:, p_, :], h),
                                               half(qys[:, buf, 0, p_, C * c:C * (c + 1)], h), start=True, stop=True)
                        ins.then_inc(ser_made, 1)
                        n["step"] += 1
                        n["ready"] += 1
                    else:
                        src = stb if ti == 2 else sta
                        for p_ in range(4):
                            ins = e.transpose(bank[CHB][:HD, p_ * P:(p_ + 1) * P], src[:, p_, :], ident)
                        ins.then_inc(so_turned, 1)
                        n["export"] += 1
            for k, gi, hg, ti, t0, m, q, hp in quads():
                tok = slice(t0, t0 + m)
                for p_ in range(2):
                    for i, src in enumerate((ar[:, 0], t1, t2, vv)):
                        ins = e.transpose(bank[p_][:m, i * P:(i + 1) * P], src[:, hp + p_, tok], ident)
                    ins.then_inc(tm_made, 1)
                if k:
                    e.wait_ge(map_read, k)
                    e.wait_ge(add_read, k)
                for i, src in enumerate((t4, kk)):
                    for h in range(4):
                        ins = e.matmul(bank[2 + 2 * i + h % 2][:m, (h // 2) * 2 * m:(h // 2 + 1) * 2 * m], half(src[:, hp + h // 2, tok], h),
                                       half(ar[:, :, hp + h // 2, tok], h), start=True, stop=True)
                        if h >= 2:
                            ins.then_inc(ab_made, 1)
                if k:
                    e.wait_ge(qy_read, 2 * k)
                e.wait_ge(tm_read, 2 * k + 2)
                for h in range(4):
                    ins = e.matmul(bank[(6, 1)[h % 2]][:m, (h // 2) * m:(h // 2 + 1) * m], half(ar[:, 0, hp + h // 2, tok], h), half(t4[:, hp + h // 2, tok], h),
                                   start=True, stop=True)
                    if h >= 2:
                        ins.then_inc(ab_made, 1)
                chain(gi, 8 * q)
                vh = lambda h: tm[:m, h // 2, 3, HD * (h % 2):HD * (h % 2) + HD]
                e.wait_ge(ab_read, 6 * k + 4)
                for h in range(4):
                    ins = e.matmul(bank[0][:m, h * HD:(h + 1) * HD], ak[:m, h, 0, 0:m], vh(h), start=True, stop=True)
                ins.then_inc(akv_made, 1)
                e.wait_ge(ab_read, 6 * k + 6)
                e.wait_ge(x_begun, 2 * k + 2)
                for it in range(nit):
                    if it:
                        e.wait_ge(x_added, 4 * k + it)
                        e.wait_ge(sq_read, 5 * k + (2, 4, 5)[it - 1])
                    up = (lambda h: ab[:m, h, 0, 0:m]) if it == 0 else (lambda h: pw[:m, (it - 1) % 2, 0, h, 0:m])
                    lo = (lambda h: a1[:m, h, 0:m]) if it == 0 else (lambda h: pw[:m, (it - 1) % 2, 1, h, 0:m])
                    for h in range(4):
                        ins = e.matmul(bank[it % 2][:m, h * P:(h + 1) * P], up(h), xx[:m, h, :], start=True, stop=True)
                    ins.then_inc(xm_made, 1)
                    if it < nit - 1:
                        for h in range(4):
                            ins = e.matmul(bank[SQB[it][0]][:m, h * m:(h + 1) * m], lo(h), up(h), start=True, stop=True)
                        ins.then_inc(sq_made, 1)
                    if it < nit - 2:
                        for h in range(4):
                            ins = e.matmul(bank[SQB[it][1]][:m, h * m:(h + 1) * m], up(h), lo(h), start=True, stop=True)
                        ins.then_inc(sq_made, 1)
                    chain(gi, 8 * q + it + 1)
                e.wait_ge(x_added, 4 * k + 4)
                e.wait_ge(bv_spread, 4 * k + 4)
                R = m // 2
                w = E * HD
                for h0 in (0, 2):
                    for g, h in ((g, h) for g in range(2) for h in (h0, h0 + 1)):
                        r = slice(R * g, R * g + R)
                        c = slice(HD * (h % 2), HD * (h % 2) + HD)
                        ins = e.matmul(half(bank[MAPB[g]][:, (h // 2) * w:(h // 2 + 1) * w], h), xx[r, h, 0:HD],
                                       bx[r, h // 2, 0:E, c], start=True, stop=True)
                ins.then_inc(map_made, 1)
                chain(gi, 8 * q + 5)
                e.wait_ge(w_spread, 4 * k + 4)
                for h0 in (0, 2):
                    for i in range(2):
                        for g, h in ((g, h) for g in range(2) for h in (h0, h0 + 1)):
                            r = slice(R * g, R * g + R)
                            c = slice(HD * (h % 2), HD * (h % 2) + HD)
                            out = half(bank[ADDB[g]][:, (h // 2) * w:(h // 2 + 1) * w], h)
                            ins = e.matmul(out, tm[r, h // 2, 1 + i, c], (wx[r, h, 0:E, :], vx[r, h // 2, 0:E, c])[i], start=(i == 0), stop=(i == 1))
                ins.then_inc(add_made, 1)
                chain(gi, 8 * q + 6)
                for h0 in (0, 2):
                    for i in range(3):
                        for h in (h0, h0 + 1):
                            out = half(bank[QYB][:, (2 * (i > 0) + h // 2) * m:(2 * (i > 0) + h // 2 + 1) * m], h)
                            lhs, rhs = ((xx[:m, h, 0:HD], ab), (xx[:m, h, HD:P], ab), (vh(h), ak))[i]
                            ins = e.matmul(out, lhs, rhs[:m, h, 1, 0:m], start=(i < 2), stop=(i != 1))
                ins.then_inc(qy_made, 1)
                chain(gi, 8 * q + 7)
            for place in range(16):
                chain(NGR, place)


def rwkv_finish(ph, I, O, R):
    nc, pool_dma_sem, sem, bank, cm, cw, pcol, prm, fr = ph
    t1, t2, t3, t4, t5, t6, ar = R["t"]
    s_made, s_read, sq, fch, fdone = sem("gn_sums"), sem("gn_read"), sem("gn_squares"), sem("gn_chain"), sem("gn_sqrt")
    epsb = R["al"]("gneps", [P, 1])
    bc = lambda name: pcol(name)[:, 0:8].unsqueeze(2).to_broadcast([P, 8, TOK])
    with nc.Block() as block:
        @block.tensor
        def _(e):
            n = 0
            for src in (t3, t1):
                if src is t1:
                    e.wait_ge(sq, 1)
                for j in range(8):
                    if n >= 4:
                        e.wait_ge(s_read, n - 3)
                    e.matmul(bank[n % 4][:, 0:TOK], cw("bones"), src[:, j, :], start=True, stop=True).then_inc(s_made, 1)
                    n += 1

        @block.scalar
        def _(a):
            for n in range(8):
                a.wait_ge(s_made, n + 1)
                a.activation(t2[:, n, :], bank[n % 4][:, 0:TOK], ACT.Copy, scale=-1.0 / HD).then_inc(s_read, 1)
            a.wait_ge(fdone, 1)
            for n in range(8, 16):
                a.wait_ge(s_made, n + 1)
                a.activation(t4[:, n - 8, :], bank[n % 4][:, 0:TOK], ACT.Sqrt, scale=1.0 / HD, bias=epsb[:, 0:1]).then_inc(s_read, 1)

        @block.vector
        def _(v):
            d = chain_of(v, fch)
            v.memset(epsb[:, :], GN_EPS).then_inc(fdone, 1)
            v.wait_ge(s_read, 8)
            d(v.tensor_tensor(t3, t3, t2, ALU.add))
            v.tensor_tensor(t1, t3, t3, ALU.mult).then_inc(sq, 1)
            v.wait_ge(s_read, 16)
            d(v.reciprocal(t4, t4))
            d(v.tensor_tensor(t3, t3, t4, ALU.mult))
            d(v.tensor_tensor(t3, t3, bc("rw_ln_g"), ALU.mult))
            d(v.tensor_tensor(t3, t3, bc("rw_ln_b"), ALU.add))
            d(v.tensor_tensor(t3, t3, t5, ALU.add))
            d(v.tensor_tensor(fr[:, 0:8, :], fr[:, 0:8, :], t3, ALU.mult))




def dsa_prepare(ph, I, O, C, fat_d, rev_d, tp_d, bs_d, S):
    nc, pool_dma_sem, sem, bank, cm, cw, pcol, prm, fr = ph
    fa, ik2, vt, ikw, nm, cd = S["fa"], S["ik2"], S["vt"], S["ikw"], S["nm"], S["cd"]
    with ExitStack() as tmp:
        al = lambda n, s, d=F32: tmp.enter_context(nc.sbuf_tensor(n, s, d))
        ktok = al("ktok", [P, 3, AT])
        rb = al("rb", [32, NH])
        bk = al("bk", [32, REV])
        rv = al("rv", [NH, REV])
        rl = al("rl", [P, 2, SP_])
        acc = al("acc", [P, 2, SP_])
        wk = al("wk", [P, 2, SP_])
        m8 = al("m8", [P, 8])
        gt = al("gt", [P, SP_])
        eq = al("eq", [P, SP_])
        cum = al("cum", [P, SP_])
        ones = al("ones", [P, SP_])
        need = al("need", [P, 1])
        wsc = al("wsc", [P, 2, NH])
    s_fa, s_c = sem("fa_in"), sem("dsa_consts_in")
    kt_made, kt_read, s_kv = sem("kv_turned"), sem("kv_read"), sem("kv_out")
    rv_made, rv_read, s_rv = sem("rev_made"), sem("rev_read"), sem("rev_out")
    dot_made, relu_done, acc_done, dch, wt_made = sem("dots_made"), sem("relu_done"), sem("acc_done"), sem("sel_chain"), sem("wt_made")
    groups = []
    for t, (t0, m) in enumerate(TILES):
        groups += [(t, t0, m, 8 + 4 * i, ktok, 4 * i) for i in range(2)] + [(t, t0, m, 16 + 4 * i, vt, 4 * i) for i in range(2)]
        groups.append((t, t0, m, None, ikw, 0))
    NG_ = len(groups)
    units = [(qt, h) for qt in range(2) for h in range(NH)]
    with nc.Block() as block:
        @block.sync
        def _(sp):
            sp.dma_start(cd[:, :], C["c_dsa"]).then_inc(s_c, 16)
            sp.dma_start(bk[:, :], C["c_bkt"]).then_inc(s_c, 16)
            sp.dma_start(rb[:, :], I["rel_bias"]).then_inc(s_c, 16)
            sp.dma_start(fa[:, 0:32, :], fat_d[:, 0:32, :]).then_inc(s_fa, 16)
            sp.dma_start(fa[0:80, 32, :], fat_d[0:80, 32, :]).then_inc(s_fa, 16)
            for i in range(2):
                sp.dma_start(ik2[64 * i:64 * i + 64, :], fat_d[0:64, 32, :]).then_inc(s_fa, 16)
            for g, (t, t0, m, c, dst, o) in enumerate(groups):
                if g % 5 == 4:
                    sp.wait_ge(kt_read, g + 1)
                    for src, n, w in ((ktok, "k", AT), (vt, "v", AT), (ikw, "ik", HD)):
                        o_ = O[n + "_p"][0, 0] if t < 2 else O[n + "_s"][0]
                        if n != "ik":
                            o_ = o_.rearrange("s h d -> s (h d)") if t < 2 else o_.rearrange("b s h d -> (b s) (h d)")
                        elif t == 2:
                            o_ = o_.rearrange("b s d -> (b s) d")
                        sp.dma_start(o_[t0 % SP_:t0 % SP_ + m, :], src[:m, t, 0:w]).then_inc(s_kv, 16)
            sp.wait_ge(rv_read, 3)
            sp.dma_start(rev_d, rv[:, :]).then_inc(s_rv, 16)
            sp.wait_ge(s_rv, 16)
            sp.dma_start(tp_d, bass.AP(rev_d.tensor, PAST + T - 1 - P, [[REV, NH], [-1, P], [1, 3 * P]])).then_inc(s_rv, 16)
            L = PAST + T - 1
            sp.dma_start(bs_d[:, :, 0:PAST], bass.AP(rev_d.tensor, T - 1, [[REV, NH], [-1, T], [1, PAST]])).then_inc(s_rv, 16)
            for b in range(DB):
                sp.dma_start(bs_d[:, :, PAST + T * b:PAST + T * b + T], bass.AP(rev_d.tensor, L, [[REV, NH], [-1, T], [1, T]])).then_inc(s_rv, 16)
            sp.wait_ge(s_rv, 16 * (3 + DB))
            sp.wait_ge(s_kv, 16 * 9)

        @block.tensor
        def _(e):
            e.wait_ge(s_fa, 64)
            e.wait_ge(s_c, 48)
            for i in range(3):
                e.matmul(bank[5 + i][:NH, :], rb[:, :], bk[:, 512 * i:512 * i + 512], start=True, stop=True).then_inc(rv_made, 1)
            for g, (t, t0, m, c, dst, o) in enumerate(groups):
                if g >= 2:
                    e.wait_ge(kt_read, g - 1)
                if c is None:
                    ins = e.transpose(bank[g % 2][:m, 0:80], fa[:80, 32, t0:t0 + m], cw("ident")[:80, :80])
                else:
                    for i in range(4):
                        ins = e.transpose(bank[g % 2][:m, i * P:(i + 1) * P], fa[:, c + i, t0:t0 + m], cw("ident"))
                ins.then_inc(kt_made, 1)
            e.wait_ge(rv_read, 1)
            e.matmul(bank[5][:, 0:SS], cdw(cd, "reph")[64:80, :], fa[64:80, 32, SP_:], start=True, stop=True).then_inc(wt_made, 1)
            e.wait_ge(kt_read, NG_)
            for n, (qt, h) in enumerate(units):
                nk = P * (qt + 1)
                r = slice(HD * (h % 2), HD * (h % 2) + HD)
                if n >= 4:
                    e.wait_ge(relu_done, n - 3)
                e.matmul(bank[n % 4][:, 0:nk], fa[r, 24 + h // 2, P * qt:P * qt + P], ik2[r, 0:nk], start=True, stop=True).then_inc(dot_made, 1)

        @block.scalar
        def _(a):
            for i in range(3):
                a.wait_ge(rv_made, i + 1)
                a.activation(rv[:, 512 * i:512 * i + 512], bank[5 + i][:NH, :], ACT.Copy).then_inc(rv_read, 1)
            for g, (t, t0, m, c, dst, o) in enumerate(groups):
                a.wait_ge(kt_made, g + 1)
                w = 80 if c is None else 512
                a.activation(dst[:m, t, o * P:o * P + w], bank[g % 2][:m, 0:w], ACT.Copy).then_inc(kt_read, 1)
            for n, (qt, h) in enumerate(units):
                nk = P * (qt + 1)
                a.wait_ge(dot_made, n + 1)
                if n >= 2:
                    a.wait_ge(acc_done, n - 1)
                a.activation(rl[:, n % 2, 0:nk], bank[n % 4][:, 0:nk], ACT.Relu).then_inc(relu_done, 1)

        @block.vector
        def _(v):
            d = chain_of(v, dch)
            d(v.memset(ones[:, :], 1.0))
            for z in (S["iqs"][:, :, :, :, :], S["wts"][:, :], S["qs"][:, :, :]):
                d(v.memset(z, 0.0))
            d(v.memset(acc[:, :, :], 0.0))
            v.wait_ge(s_fa, 64)
            v.wait_ge(s_c, 48)
            for p_ in range(2):
                r = slice(HD * p_, HD * p_ + HD)
                d(v.tensor_copy(S["iqs"][r, :, :, p_, :], fa[r, 24:32, SP_:].rearrange("p h (b q) -> p b h q", q=T)))
            d(v.tensor_copy(S["qn"][:, :, :], fa[:, 0:8, SP_:]))
            d(v.tensor_copy(S["kn"][:, :, :], fa[:, 8:16, SP_:]))
            v.wait_ge(wt_made, 1)
            d(v.tensor_tensor(S["wts"][:, :].rearrange("p (b x) -> p b x", x=72)[:, :, 0:T], bank[5][:, 0:SS].rearrange("p (b q) -> p b q", q=T),
                              cdw(cd, "dqq").rearrange("p (b q) -> p b q", q=T), ALU.mult))
            v.wait_ge(kt_read, NG_)
            d(v.tensor_scalar(wsc[:, :, :], ikw[:, 0:2, HD:HD + NH], IDXW, None, ALU.mult))
            for n, (qt, h) in enumerate(units):
                nk = P * (qt + 1)
                v.wait_ge(relu_done, n + 1)
                v.scalar_tensor_tensor(acc[:, qt, 0:nk], rl[:, n % 2, 0:nk], wsc[:, qt, h:h + 1], acc[:, qt, 0:nk], ALU.mult, ALU.add).then_inc(acc_done, 1)
                v.wait_ge(acc_done, n + 1)
            for qt in range(2):
                nk = P * (qt + 1)
                cn = cdw(cd, "cn")[:, SP_ * qt:SP_ * qt + nk]
                sc = acc[:, qt, 0:nk]
                d(v.tensor_tensor(sc, sc, cn, ALU.add))
                top_mask(v, d, sc, wk, m8, gt[:, 0:nk], eq[:, 0:nk], cum[:, 0:nk], ones[:, 0:nk], need, TOPK_P, nm[:, qt, 0:nk], nk, P)
                d(v.tensor_tensor(nm[:, qt, 0:nk], nm[:, qt, 0:nk], cn, ALU.min))


def top_mask(v, d, sc, wk, m8, gt, eq, cum, ones, need, topk, out, nk, rows):
    src = sc
    turns = -(-topk // 8)
    for r in range(turns):
        d(v.max(m8[:rows, :], src))
        if r < turns - 1:
            dst = wk[:rows, r % 2, 0:nk]
            d(v.match_replace(dst, m8[:rows, :], src, NEG * 3))
            src = dst
    last = (topk - 1) % 8
    least = m8[:rows, last:last + 1]
    d(v.tensor_scalar(gt, sc, least, None, ALU.is_gt))
    d(v.tensor_scalar(eq, sc, least, None, ALU.is_equal))
    d(v.tensor_reduce(need[:rows, :], gt, AXX, ALU.add))
    d(v.tensor_scalar(need[:rows, :], need[:rows, :], -1.0, float(topk), ALU.mult, ALU.add))
    d(v.tensor_tensor_scan(cum, ones, eq, 0.0, ALU.mult, ALU.add))
    d(v.scalar_tensor_tensor(eq, cum, need[:rows, :], eq, ALU.is_le, ALU.mult))
    d(v.tensor_tensor(gt, gt, eq, ALU.add))
    if out is not None:
        d(v.tensor_scalar(out, gt, -1.0, -NEG, ALU.add, ALU.mult))


def dsa_prompt(ph, I, O, tp_d, S):
    nc, pool_dma_sem, sem, bank, cm, cw, pcol, prm, fr = ph
    fa, vt, nm = S["fa"], S["vt"], S["nm"]
    with ExitStack() as tmp:
        al = lambda n, s, d=F32: tmp.enter_context(nc.sbuf_tensor(n, s, d))
        bp = al("bp", [P, 2, 2, SP_])
        lg = al("lg", [P, 2, 2, SP_])
        pt = al("pt", [P, 2, 4, P])
        sm = al("sm", [P, 3, 2, 2])
    s_bp = [sem("bias_in0"), sem("bias_in1")]
    bm_done, qk_made, lg_done, mx_done, ex_done, rc_done = [sem("p_" + n) for n in ("bm", "qk", "logits", "max", "exp", "recip")]
    nrm, pt_made, pt_read, o_made, o_read, dch = [sem("p_" + n) for n in ("norm", "turned", "taken", "o", "o_read", "chain")]
    units = [(qt, hp) for qt in range(2) for hp in range(HP)]
    def take(a, n):
        qt, hp = units[n]
        a.wait_ge(pt_made, n + 1)
        a.activation(pt[:, n % 2, :, :].rearrange("p (h j) q -> p h j q", h=2)[:, :, 0:qt + 1, :],
                     bank[4 + n % 2][:, :].rearrange("p (h j q) -> p h j q", h=2, j=2)[:, :, 0:qt + 1, :], ACT.Copy).then_inc(pt_read, 1)
        a.wait_ge(o_made, n + 1)
        a.activation(fr[:, 8 + hp, P * qt:P * qt + P], bank[6 + n % 2][:, 0:P], ACT.Copy).then_inc(o_read, 1)

    with nc.Block() as block:
        @block.sync
        def _(sp):
            for n, (qt, hp) in enumerate(units):
                nk = P * (qt + 1)
                if n >= 2:
                    sp.wait_ge(lg_done, 2 * (n - 1))
                src = tp_d[2 * hp:2 * hp + 2, :, P * (1 - qt):P * (1 - qt) + nk].rearrange("h p s -> p h s")
                sp.dma_start(bp[:, n % 2, :, 0:nk], src).then_inc(s_bp[n % 2], 16)

        @block.gpsimd
        def _(g):
            for n, (qt, hp) in enumerate(units):
                nk = P * (qt + 1)
                g.wait_ge(s_bp[n % 2], 16 * (n // 2 + 1))
                g.tensor_tensor(bp[:, n % 2, :, 0:nk], bp[:, n % 2, :, 0:nk], nm[:, qt, 0:nk].unsqueeze(1).to_broadcast([P, 2, nk]), ALU.add).then_inc(bm_done, 1)

        @block.tensor
        def _(e):
            def qk(n):
                qt, hp = units[n]
                nk = P * (qt + 1)
                if n >= 2:
                    e.wait_ge(lg_done, 2 * (n - 1))
                for p_ in range(2):
                    r = slice(HD * p_, HD * p_ + HD)
                    e.matmul(bank[2 * (n % 2) + p_][:, 0:nk], fa[r, hp, P * qt:P * qt + P], fa[r, 8 + hp, 0:nk], start=True, stop=True).then_inc(qk_made, 1)
            qk(0)
            for n, (qt, hp) in enumerate(units):
                if n + 1 < len(units):
                    qk(n + 1)
                e.wait_ge(nrm, n + 1)
                if n >= 2:
                    e.wait_ge(pt_read, n - 1)
                for p_ in range(2):
                    for j in range(qt + 1):
                        ins = e.transpose(bank[4 + n % 2][:, (2 * p_ + j) * P:(2 * p_ + j + 1) * P], lg[:, n % 2, p_, j * P:(j + 1) * P], cw("ident"))
                ins.then_inc(pt_made, 1)
                e.wait_ge(pt_read, n + 1)
                if n >= 2:
                    e.wait_ge(o_read, n - 1)
                for p_ in range(2):
                    for j in range(qt + 1):
                        ins = e.matmul(bank[6 + n % 2][HD * p_:HD * p_ + HD, 0:P], vt[:, j, hp * P + HD * p_:hp * P + HD * p_ + HD],
                                       pt[:, n % 2, 2 * p_ + j, :], start=(j == 0), stop=(j == qt))
                ins.then_inc(o_made, 1)

        @block.scalar
        def _(a):
            for n, (qt, hp) in enumerate(units):
                nk = P * (qt + 1)
                a.wait_ge(mx_done, n + 1)
                for p_ in range(2):
                    a.activation(lg[:, n % 2, p_, 0:nk], lg[:, n % 2, p_, 0:nk], ACT.Exp, bias=sm[:, 0, n % 2, p_:p_ + 1],
                                 accum_out=sm[:, 1, n % 2, p_:p_ + 1]).then_inc(ex_done, 1)
                if n:
                    take(a, n - 1)
            take(a, len(units) - 1)

        @block.vector
        def _(v):
            for n, (qt, hp) in enumerate(units):
                nk = P * (qt + 1)
                v.wait_ge(bm_done, n + 1)
                if n >= 2:
                    v.wait_ge(pt_made, n - 1)
                for p_ in range(2):
                    v.wait_ge(qk_made, 2 * n + p_ + 1)
                    v.scalar_tensor_tensor(lg[:, n % 2, p_, 0:nk], bank[2 * (n % 2) + p_][:, 0:nk], HD ** -0.5, bp[:, n % 2, p_, 0:nk],
                                           ALU.mult, ALU.add).then_inc(lg_done, 1)
                v.wait_ge(lg_done, 2 * n + 2)
                v.tensor_reduce(sm[:, 0, n % 2, :], lg[:, n % 2, :, 0:nk], AXX, ALU.max, negate=True).then_inc(mx_done, 1)
                v.wait_ge(ex_done, 2 * n + 2)
                v.reciprocal(sm[:, 2, n % 2, :], sm[:, 1, n % 2, :]).then_inc(rc_done, 1)
                v.wait_ge(rc_done, n + 1)
                v.tensor_tensor(lg[:, n % 2, :, 0:nk], lg[:, n % 2, :, 0:nk], sm[:, 2, n % 2, :].unsqueeze(2).to_broadcast([P, 2, nk]), ALU.mult).then_inc(nrm, 1)


def dsa_sample(ph, I, O, bs_d, S):
    nc, pool_dma_sem, sem, bank, cm, cw, pcol, prm, fr = ph
    ik2, vt, cd, iqs, wts, qs, qn, kn = [S[n] for n in ("ik2", "vt", "cd", "iqs", "wts", "qs", "qn", "kn")]
    with ExitStack() as tmp:
        al = lambda n, s, d=F32: tmp.enter_context(nc.sbuf_tensor(n, s, d))
        pti = al("pti", [1, DB * NPG], I32)
        kp = al("kp", [P, NPG, AT])
        vp = al("vp", [P, NPG, AT])
        ki = al("ki", [P, 2, NPG, HD])
        kd = al("kd", [P, NPG, 2, HD])
        kit = al("kit", [P, 2, 512])
        rl = al("srl", [P, KEYS])
        sc = al("ssc", [SS, KEYS])
        nms = al("nms", [SS, KEYS])
        m8 = al("sm8", [SS, 8])
        need = al("sneed", [SS, 1])
        ktr = al("ktr", [P, HP, 512])
        bs = al("bs", [P, KEYS])
        om = al("som", [P, 2 * P])
        lg = al("slg", [P, KEYS])
        pt = al("spt", [P, 9, P])
        sm = al("ssm", [P, 4])
    gt, eq, cum, ones = rl[0:SS, :], lg[0:SS, :], pt[0:SS, :, :].rearrange("p a b -> p (a b)")[:, 0:KEYS], ktr[0:SS, :, :].rearrange("p a b -> p (a b)")[:, 0:KEYS]
    wk = ktr[0:SS, :, :].rearrange("p a b -> p (a b)")[:, KEYS:3 * KEYS].rearrange("p (a b) -> p a b", a=2)
    s_pt, s_bs = sem("page_table_in"), sem("sample_bias_in")
    s_ki = [sem(f"ki_in{i}") for i in range(2)]
    kd_done, kit_made, kit_read, dot_made, relu_done, sc_made = [sem("s_" + n) for n in ("dup", "ki_turned", "ki_taken", "dots", "relu", "scores")]
    sch = sem("s_sel_chain")
    s_k = [sem(f"k_pages_in{i}") for i in range(2)]
    s_v = sem("v_pages_in")
    ck = I["cache_k"][0].rearrange("n p h d -> n p (h d)")
    cv = I["cache_v"][0].rearrange("n p h d -> n p (h d)")
    ci = I["cache_idx_k"][0]
    N_POOL = ci.shape[0]
    cols = [(0, 512), (512, 1024), (1024, KEYS)]

    def load_page(sp, dst, src, i):
        page = sp.value_load(pti[0:1, i:i + 1], min_val=0, max_val=N_POOL - 1)
        return sp.dma_start(dst, src[bass.DynSlice(page, 1), :, :].squeeze(0))

    with nc.Block() as block:
        @block.sync
        def _(sp):
            sp.dma_start(pti[:, :], I["page_table"].rearrange("b n -> (b n)").unsqueeze(0)).then_inc(s_pt, 16)
            sp.dma_start(bs[:, :], bs_d.rearrange("h q s -> (h q) s")).then_inc(s_bs, 16)
            sp.wait_ge(s_pt, 16)
            for b in range(DB):
                if b >= 2:
                    sp.wait_ge(kd_done, b - 1)
                for n in range(NPG):
                    load_page(sp, ki[:, b % 2, n, :], ci, NPG * b + n).then_inc(s_ki[b % 2], 16)
            for n in range(NPG):
                load_page(sp, kp[:, n, :], ck, n).then_inc(s_k[n // 4], 16)
            for n in range(NPG):
                load_page(sp, vp[:, n, :], cv, n).then_inc(s_v, 16)
            sp.wait_ge(s_bs, 16)

        @block.scalar
        def _(a):
            for b in range(DB):
                for i in range(2):
                    a.wait_ge(kit_made, 2 * b + i + 1)
                    if b:
                        a.wait_ge(dot_made, 3 * (b - 1) + i + 1)
                    a.activation(kit[:, i, :], bank[i][:, :], ACT.Copy).then_inc(kit_read, 1)
                for i, (c0, c1) in enumerate(cols):
                    a.wait_ge(dot_made, 3 * b + i + 1)
                    if b:
                        a.wait_ge(sc_made, b)
                    a.activation(rl[:, c0:c1], bank[2 + i][:, 0:c1 - c0], ACT.Relu).then_inc(relu_done, 1)

        @block.tensor
        def _(e):
            for b in range(DB):
                e.wait_ge(kd_done, b + 1)
                for i in range(2):
                    if b:
                        e.wait_ge(kit_read, 2 * (b - 1) + i + 1)
                    for n in range(4):
                        ins = e.transpose(bank[i][:, n * P:(n + 1) * P], kd[:, 4 * i + n, :, :].rearrange("p a d -> p (a d)"), cw("ident"))
                    ins.then_inc(kit_made, 1)
                for i, (c0, c1) in enumerate(cols):
                    if i < 2:
                        e.wait_ge(kit_read, 2 * b + i + 1)
                    if b:
                        e.wait_ge(relu_done, 3 * (b - 1) + i + 1)
                    rhs = kit[:, i, :] if i < 2 else ik2[:, SP_:]
                    e.matmul(bank[2 + i][:, 0:c1 - c0], iqs[:, b, :, :, :].rearrange("p h a q -> p (h a q)"), rhs, start=True, stop=True).then_inc(dot_made, 1)
                for i, (c0, c1) in enumerate(cols):
                    e.wait_ge(relu_done, 3 * b + i + 1)
                    ins = e.matmul(bank[5 + i][:SS, 0:c1 - c0], wts[:, SS * b:SS * b + SS], rl[:, c0:c1], start=(b == 0), stop=(b == DB - 1))
                ins.then_inc(sc_made, 1)

        @block.vector
        def _(v):
            d = chain_of(v, sch)
            for b in range(DB):
                v.wait_ge(s_ki[b % 2], 16 * NPG * (b // 2 + 1))
                if b:
                    v.wait_ge(kit_made, 2 * b)
                src = ki[:, b % 2, :, :]
                v.tensor_copy(kd[:, :, :, :], src.unsqueeze(2).to_broadcast([P, NPG, 2, HD])).then_inc(kd_done, 1)
            v.wait_ge(sc_made, DB)
            for i, (c0, c1) in enumerate(cols):
                if i < 2:
                    d(v.tensor_scalar(sc[:, c0:c1], bank[5 + i][:SS, 0:c1 - c0], IDXW, None, ALU.mult))
                else:
                    d(v.scalar_tensor_tensor(sc[:, c0:c1], bank[5 + i][:SS, 0:c1 - c0], IDXW, cdw(cd, "cns")[0:SS, :], ALU.mult, ALU.add))
            d(v.memset(ones, 1.0))
            top_mask(v, d, sc[:, :], wk, m8, gt, eq, cum, ones, need, TOPK_S, nms[:, :], KEYS, SS)
            d(v.tensor_tensor(nms[:, PAST:], nms[:, PAST:], cdw(cd, "cns")[0:SS, :], ALU.min))

    ktr_made, ktr_read, qs_ready, qk_grp, qk_made = [sem("a_" + n) for n in ("k_turned", "k_taken", "q_spread", "qk_group", "logits_made")]
    lg_done, mx_done, ex_done, rc_done, nrm = [sem("a_" + n) for n in ("logits", "max", "exp", "recip", "norm")]
    pt_made, pt_read, o_made, o_taken, o_turned, o_read = [sem("a_" + n) for n in ("p_turned", "p_taken", "o_made", "o_taken", "o_turned", "o_read")]
    HPS = (0, 2, 4, 6, 1, 3, 5, 7)
    GROUP_AFTER = {5: 0, 9: 1, 13: 2}
    with nc.Block() as block:
        @block.sync
        def _(sp):
            def keys(b):
                for i in range(2):
                    sp.wait_ge(ktr_made, 16 * (b - 1) + 8 * i + 8)
                    for n in range(4):
                        load_page(sp, kp[:, 4 * i + n, :], ck, NPG * b + 4 * i + n).then_inc(s_k[i], 16)

            keys(1)
            for b in range(1, DB):
                if b + 1 < DB:
                    keys(b + 1)
                sp.wait_ge(o_made, b)
                for n in range(NPG):
                    load_page(sp, vp[:, n, :], cv, NPG * b + n).then_inc(s_v, 16)

        @block.tensor
        def _(e):
            def logits(b):
                e.wait_ge(qs_ready, 2 * b + 2)

                def group(x):
                    i, lo = divmod(x, 2)
                    if lo == 0:
                        if b:
                            e.wait_ge(lg_done, 3 * (b - 1) + i + 1)
                        e.matmul(bank[2 + i][:, :], cdw(cd, "rep")[0:SS, P * b:P * b + P], nms[:, 512 * i:512 * i + 512], start=True, stop=False)
                    e.wait_ge(ktr_read, 16 * b + 4 * x + 4)
                    for y in range(4):
                        hp, j = HPS[4 * lo + y], slice(32 * y, 32 * y + 32)
                        ins = e.matmul(bank[2 + i][j, :], qs[:, b % 2, hp * P + 32 * y:hp * P + 32 * y + 32], ktr[:, 4 * lo + y, :],
                                       start=False, stop=(lo == 1))
                    ins.then_inc(qk_grp, 1)
                    if lo == 1:
                        e.wait_ge(qk_grp, 4 * b + x + 1)
                        e.sem_inc(qk_made, 1)
                for turn in range(16):
                    i, y = divmod(turn, 8)
                    g = 16 * b + turn
                    hp = HPS[y]
                    if y == 0:
                        e.wait_ge(s_k[i], 64 * (b + 1))
                    if g >= 2:
                        e.wait_ge(ktr_read, g - 1)
                    for n in range(4):
                        ins = e.transpose(bank[g % 2][:, n * P:(n + 1) * P], kp[:, 4 * i + n, hp * P:(hp + 1) * P], cw("ident"))
                    ins.then_inc(ktr_made, 1)
                    if turn in GROUP_AFTER:
                        group(GROUP_AFTER[turn])
                if b:
                    e.wait_ge(lg_done, 3 * b)
                e.matmul(bank[4][:, 0:SS], cdw(cd, "rep")[0:SS, P * b:P * b + P], nms[:, PAST:], start=True, stop=False)
                for y, hp in enumerate(HPS):
                    j = 32 * (y % 4)
                    e.matmul(bank[4][j:j + 32, 0:SS], qs[:, b % 2, hp * P + j:hp * P + j + 32], kn[:, hp, :], start=False, stop=(y >= 4))
                group(3)
                e.sem_inc(qk_made, 1)

            logits(0)
            for b in range(DB):
                if b + 1 < DB:
                    logits(b + 1)
                e.wait_ge(nrm, b + 1)
                for c in range(3):
                    if 3 * b + c >= 2:
                        e.wait_ge(pt_read, 3 * b + c - 1)
                    for n in range(4 * c, min(4 * c + 4, 9)):
                        w = P if n < 8 else SS
                        ins = e.transpose(bank[5 + (3 * b + c) % 2][:w, (n % 4) * P:(n % 4 + 1) * P], lg[:, n * P:n * P + w], cw("ident"))
                    ins.then_inc(pt_made, 1)
                e.wait_ge(pt_read, 3 * b + 3)
                e.wait_ge(s_v, 16 * NPG * (b + 1))
                if b:
                    e.wait_ge(o_read, 4 * b)
                for n in range(9):
                    w = P if n < 8 else SS
                    for j in range(4):
                        rhs = vp[:, n, 2 * P * j:2 * P * j + 2 * P] if n < 8 else vt[0:SS, 2, 2 * P * j:2 * P * j + 2 * P]
                        ins = e.matmul(bank[7][32 * j:32 * j + 32, 0:2 * P], pt[:w, n, 32 * j:32 * j + 32], rhs, start=(n == 0), stop=(n == 8))
                ins.then_inc(o_made, 1)
                e.wait_ge(o_taken, b + 1)
                for c in range(2):
                    ins = e.transpose(bank[7][:, (2 + c) * P:(3 + c) * P], om[:, c * P:(c + 1) * P], cw("ident"))
                ins.then_inc(o_turned, 1)

        @block.scalar
        def _(a):
            def take_keys(b):
                for g in range(16 * b, 16 * b + 16):
                    a.wait_ge(ktr_made, g + 1)
                    if g % 4 == 0 and g >= 8:
                        a.wait_ge(qk_grp, g // 4 - 1)
                    a.activation(ktr[:, g % 8, :], bank[g % 2][:, :], ACT.Copy).then_inc(ktr_read, 1)

            def exponent(b):
                a.wait_ge(mx_done, b + 1)
                a.activation(lg[:, :], lg[:, :], ACT.Exp, bias=sm[:, 0:1], accum_out=sm[:, 1:2]).then_inc(ex_done, 1)
            take_keys(0)
            exponent(0)
            for b in range(DB):
                if b + 1 < DB:
                    take_keys(b + 1)
                for c in range(3):
                    a.wait_ge(pt_made, 3 * b + c + 1)
                    n, w = (4, P) if c < 2 else (1, SS)
                    a.activation(pt[:w, 4 * c:4 * c + n, :], bank[5 + (3 * b + c) % 2][:w, 0:n * P].rearrange("p (n q) -> p n q", n=n), ACT.Copy).then_inc(pt_read, 1)
                a.wait_ge(o_made, b + 1)
                a.activation(om[:, :], bank[7][:, 0:2 * P], ACT.Copy).then_inc(o_taken, 1)
                a.wait_ge(o_turned, b + 1)
                for p_ in range(2):
                    for c in range(2):
                        r = slice(HD * p_, HD * p_ + HD)
                        a.activation(fr[r, 8 + c:16:2, SP_ + T * b:SP_ + T * b + T],
                                     bank[7][r, (2 + c) * P:(3 + c) * P].rearrange("p (j x q) -> p j x q", x=4, q=T)[:, :, 2 * c + p_, :], ACT.Copy).then_inc(o_read, 1)
                if b + 1 < DB:
                    exponent(b + 1)

        @block.vector
        def _(v):
            def spread(b):
                if b >= 2:
                    v.wait_ge(qk_made, 3 * (b - 1))
                for p_ in range(2):
                    r = slice(HD * p_, HD * p_ + HD)
                    v.tensor_copy(qs[r, b % 2, :].rearrange("p (h x) -> p h x", x=144)[:, :, T * p_:T * p_ + T], qn[r, :, T * b:T * b + T]).then_inc(qs_ready, 1)
            spread(0)
            spread(1)
            for b in range(DB):
                if b:
                    v.wait_ge(pt_made, 3 * b)
                for i, (c0, c1) in enumerate(cols):
                    v.wait_ge(qk_made, 3 * b + i + 1)
                    v.scalar_tensor_tensor(lg[:, c0:c1], bank[2 + i][:, 0:c1 - c0], HD ** -0.5, bs[:, c0:c1], ALU.mult, ALU.add).then_inc(lg_done, 1)
                v.wait_ge(lg_done, 3 * b + 3)
                v.tensor_reduce(sm[:, 0:1], lg[:, :], AXX, ALU.max, negate=True).then_inc(mx_done, 1)
                if b + 2 < DB:
                    spread(b + 2)
                v.wait_ge(ex_done, b + 1)
                v.reciprocal(sm[:, 2:3], sm[:, 1:2]).then_inc(rc_done, 1)
                v.wait_ge(rc_done, b + 1)
                v.tensor_scalar(lg[:, :], lg[:, :], sm[:, 2:3], None, ALU.mult).then_inc(nrm, 1)


def mix_out(ph, I, O, S):
    nc, pool_dma_sem, sem, bank, cm, cw, pcol, prm, fr = ph
    x1, mk, mv, mkt, qt_ = S["x1"], S["mk"], S["mv"], S["mkt"], S["qt"]
    with ExitStack() as tmp:
        al = lambda n, s, d=F32: tmp.enter_context(nc.sbuf_tensor(n, s, d))
        xn = al("xn", [P, 3, D])
        junk = al("junk2", [P, D])
        stats = al("stats2", [P, 4, 3])
        stats_m = al("stats_m", [P, 4, 3])
        ht = al("ht2", [P, KT, TOK])
        w = al("wmix", [P, 2, KT, CH])
    s_x, s_m, s_w = sem("x1_in"), sem("mem_in"), [sem("wmix0_in"), sem("wmix1_in")]
    t_made, t_read, x_added, s_kv = sem("mix_tiles"), sem("mix_read"), sem("x1_added"), sem("memkv_out")
    mt_made, mt_read = sem("mk_turned"), sem("mk_taken")
    kt = lambda a: a.rearrange("(kt p) n -> p kt n", p=P)
    wout = kt(I["w_out"][0])
    chunks = [wout[:, :, CH * i:CH * i + CH] for i in range(4)] + [kt(I[n][0]) for n in ("w_ck", "w_cv", "w_cq")]
    tiles = [3, 3, 3, 3, 2, 2, 4]
    first = [sum(tiles[:i]) for i in range(8)]
    mem = I["mem_prompt"][0]
    am, dm, pm, mem_turned = norm_to_features(ph, "mem", xn, [P, P], pcol("g_mem"), ht, lambda e, t: e.wait_ge(s_m, 32), (6, 7), (junk, stats_m))
    ax, dx, px, cross_turned = norm_to_features(ph, "cross", x1, [m for _, m in TILES], pcol("g_cross"), ht, lambda e, t: e.wait_ge(x_added, 12),
                                     (6, 7), (junk, stats), out=xn)

    with nc.Block() as block:
        @block.sync
        def _(sp):
            for c, src in enumerate(chunks):
                if c >= 2:
                    sp.wait_ge(t_made, first[c - 1])
                sp.dma_start(w[:, c % 2, :, :], src).then_inc(s_w[c % 2], 16)

        @block.scalar
        def _(a):
            for t, (t0, m) in enumerate(TILES):
                src = I["x_prompt"][0] if t < 2 else I["x_sample"].rearrange("b t d -> (b t) d")
                a.dma_start(x1[:m, t, :], src[t0 % SP_:t0 % SP_ + m, :]).then_inc(s_x, 16)
            for t in range(2):
                a.dma_start(xn[:, t, :], mem[P * t:P * t + P, :]).then_inc(s_m, 16)
            am(a)
            for c, dst in ((4, mk), (5, mv)):
                for t in range(2):
                    n = first[c] + t
                    a.wait_ge(t_made, n + 1)
                    a.activation(dst[:, t, :], bank[n % 4][:, :], ACT.Copy).then_inc(t_read, 1)
            a.wait_ge(t_read, 4)
            for t in range(2):
                for n, src in (("mk_p", mk), ("mv_p", mv)):
                    a.dma_start(O[n][0, 0].rearrange("s h d -> s (h d)")[P * t:P * t + P, :], src[:, t, :]).then_inc(s_kv, 16)
            for i in range(2):
                a.wait_ge(mt_made, i + 1)
                a.activation(mkt[:, 2 * i:2 * i + 2, :], bank[4 + i][:, :].rearrange("p (h s) -> p h s", h=2), ACT.Copy).then_inc(mt_read, 1)
            ax(a)
            for j in range(XH):
                n = first[6] + j
                a.wait_ge(t_made, n + 1)
                a.activation(qt_[:, j, :], bank[n % 4][:, 0:TOK], ACT.Copy).then_inc(t_read, 1)
            a.wait_ge(s_kv, 64)

        @block.vector
        def _(v):
            dm(v)
            v.wait_ge(s_x, 48)
            for c in range(4):
                for t, (t0, m) in enumerate(TILES):
                    n = 3 * c + t
                    v.wait_ge(t_made, n + 1)
                    xs = x1[:m, t, CH * c:CH * c + CH]
                    v.tensor_tensor(xs, xs, bank[n % 4][:m, :], ALU.add).then_inc(x_added, 1)
            v.wait_ge(t_made, first[6])
            dx(v)

        @block.tensor
        def _(e):
            pm(e)

            def free(n):
                if 4 <= n < 16:
                    e.wait_ge(x_added, n - 3)
                elif n >= 16:
                    e.wait_ge(t_read, n - 15)
            for c in range(7):
                if c == 6:
                    e.wait_ge(mt_read, 2)
                    px(e)
                    e.wait_ge(*cross_turned)
                if c == 4:
                    e.wait_ge(*mem_turned)
                e.wait_ge(s_w[c % 2], 16 * (c // 2 + 1))
                for t in range(tiles[c]):
                    n = first[c] + t
                    free(n)
                    if c < 6:
                        t0, m = TILES[t]
                        lhs = (lambda k: fr[:, k, t0:t0 + m]) if c < 4 else (lambda k: ht[:, k, t0:t0 + m])
                        for k in range(KT):
                            ins = e.matmul(bank[n % 4][:m, :], lhs(k), w[:, c % 2, k, :], start=(k == 0), stop=(k == KT - 1))
                    else:
                        for k in range(KT):
                            ins = e.matmul(bank[n % 4][:, 0:TOK], w[:, c % 2, k, P * t:P * t + P], ht[:, k, :], start=(k == 0), stop=(k == KT - 1))
                    ins.then_inc(t_made, 1)
                if c == 5:
                    e.wait_ge(t_read, 4)
                    for i in range(2):
                        for h in (2 * i, 2 * i + 1):
                            for t in range(2):
                                ins = e.transpose(bank[4 + i][:, (h % 2) * MEM + P * t:(h % 2) * MEM + P * t + P], mk[:, t, P * h:P * h + P], cw("ident"))
                        ins.then_inc(mt_made, 1)


def cross(ph, I, O, S):
    nc, pool_dma_sem, sem, bank, cm, cw, pcol, prm, fr = ph
    x1, mk, mv, mkt, qt_ = S["x1"], S["mk"], S["mv"], S["mkt"], S["qt"]
    with ExitStack() as tmp:
        al = lambda n, s, d=F32: tmp.enter_context(nc.sbuf_tensor(n, s, d))
        wco = al("wco", [P, XH, D])
        ot = al("ot", [P, XH, TOK])
        ckk = al("ckk", [P, 2, 2, XW])
        cvv = al("cvv", [P, 4, 2, XW])
        kts = al("kts", [P, 2, XH, MEM])
        qx = al("qx", [P, 2, XH * 40])
        lg = al("clg", [P, 2, 4, MEM])
        pt = al("cpt", [P, 2, 4, P])
        sm = al("csm", [P, 3, 4])
    s_w, s_k, s_v = sem("wco_in"), [sem("ckk_in0"), sem("ckk_in1")], sem("cvv_in")
    qk_made, lg_done, mx_done, ex_done, rc_done, nrm = [sem("c_" + n) for n in ("qk", "logits", "max", "exp", "recip", "norm")]
    pt_made, pt_read, o_made, o_read = [sem("c_" + n) for n in ("turned", "taken", "o", "o_read")]
    kt_made, kt_read, qx_zero, qx_ready, x_made, x_added = [sem("c_" + n) for n in ("k_turned", "k_taken", "q_zero", "q_spread", "x_made", "x_added")]
    UN = [("p", 0), ("p", 1), ("s", 0), ("s", 1)]
    nh = lambda u: 4 if u[0] == "p" else 1
    done = lambda n: sum(nh(u) for u in UN[:n])
    ckd = I["cache_mem_k"][0].rearrange("b (t p) h d -> b p t (h d)", p=P)
    cvd = I["cache_mem_v"][0].rearrange("b (t p) h d -> b p t (h d)", p=P)
    with nc.Block() as block:
        @block.sync
        def _(sp):
            for b in range(DB):
                if b >= 2:
                    sp.wait_ge(kt_made, 2 * (b - 1))
                sp.dma_start(ckk[:, b % 2, :, :], ckd[b]).then_inc(s_k[b % 2], 16)

        @block.scalar
        def _(a):
            a.dma_start(wco[:, :, :], I["w_co"][0].rearrange("(h p) n -> p h n", p=P)).then_inc(s_w, 16)
            for b in range(4):
                a.dma_start(cvv[:, b, :, :], cvd[b]).then_inc(s_v, 16)
            nk = 0
            for n, u in enumerate(UN):
                if u[0] == "s":
                    for b in range(4 * u[1], 4 * u[1] + 4):
                        for i in range(2):
                            a.wait_ge(kt_made, 2 * b + i + 1)
                            if b >= 2:
                                a.wait_ge(qk_made, 4 + b - 1)
                            a.activation(kts[:, b % 2, 2 * i:2 * i + 2, :], bank[2 + i][:, :].rearrange("p (h s) -> p h s", h=2), ACT.Copy).then_inc(kt_read, 1)
                a.wait_ge(mx_done, n + 1)
                for j in range(nh(u)):
                    a.activation(lg[:, n % 2, j, :], lg[:, n % 2, j, :], ACT.Exp, bias=sm[:, 0, j:j + 1], accum_out=sm[:, 1, j:j + 1]).then_inc(ex_done, 1)
                for i in range(2 if u[0] == "p" else 1):
                    a.wait_ge(pt_made, 2 * min(n, 2) + max(n - 2, 0) + i + 1)
                    w = 4 if u[0] == "p" else 2
                    a.activation(pt[:, i, 0:w, :], bank[4 + i][:, 0:w * P].rearrange("p (j q) -> p j q", j=w), ACT.Copy).then_inc(pt_read, 1)
                a.wait_ge(o_made, n + 1)
                if u[0] == "p":
                    a.activation(ot[:, :, P * u[1]:P * u[1] + P], bank[6][:, :].rearrange("p (h q) -> p h q", h=XH), ACT.Copy).then_inc(o_read, 1)
                else:
                    g0 = SP_ + 32 * u[1]
                    a.activation(ot[:, :, g0:g0 + 32].rearrange("p h (b q) -> p b h q", q=T),
                                 bank[6][:, 0:P].rearrange("p (b h q) -> p b h q", b=4, h=XH), ACT.Copy).then_inc(o_read, 1)
                if n == 2:
                    for b in range(4, 8):
                        a.dma_start(cvv[:, b - 4, :, :], cvd[b]).then_inc(s_v, 16)

        @block.tensor
        def _(e):
            for n, u in enumerate(UN):
                if u[0] == "p":
                    if n:
                        e.wait_ge(lg_done, n)
                    tok = slice(P * u[1], P * u[1] + P)
                    for h in range(XH):
                        ins = e.matmul(bank[h // 2][:, (h % 2) * MEM:(h % 2 + 1) * MEM], qt_[:, h, tok], mkt[:, h, :], start=True, stop=True)
                        if h % 2:
                            ins.then_inc(qk_made, 1)
                else:
                    if u[1] == 0:
                        e.wait_ge(lg_done, 2)
                    else:
                        e.wait_ge(lg_done, 3)
                    for b in range(4 * u[1], 4 * u[1] + 4):
                        e.wait_ge(s_k[b % 2], 16 * (b // 2 + 1))
                        for i in range(2):
                            if b:
                                e.wait_ge(kt_read, 2 * (b - 1) + i + 1)
                            for h in (2 * i, 2 * i + 1):
                                for t in range(2):
                                    ins = e.transpose(bank[2 + i][:, (h % 2) * MEM + P * t:(h % 2) * MEM + P * t + P], ckk[:, b % 2, t, P * h:P * h + P], cw("ident"))
                            ins.then_inc(kt_made, 1)
                        e.wait_ge(kt_read, 2 * b + 2)
                        e.wait_ge(qx_ready, b + 1)
                        r = 32 * (b % 4)
                        for h in range(XH):
                            ins = e.matmul(bank[0][r:r + 32, 0:MEM], qx[:, b % 2, 32 * h:32 * h + 32], kts[:, b % 2, h, :], start=(h == 0), stop=(h == XH - 1))
                        ins.then_inc(qk_made, 1)
                e.wait_ge(nrm, n + 1)
                for i in range(2 if u[0] == "p" else 1):
                    if n:
                        e.wait_ge(pt_read, 2 * min(n, 2) + max(n - 2, 0))
                    if u[0] == "p":
                        for h in (2 * i, 2 * i + 1):
                            for t in range(2):
                                ins = e.transpose(bank[4 + i][:, (2 * (h % 2) + t) * P:(2 * (h % 2) + t + 1) * P], lg[:, n % 2, h, P * t:P * t + P], cw("ident"))
                    else:
                        for t in range(2):
                            ins = e.transpose(bank[4][:, t * P:(t + 1) * P], lg[:, n % 2, 0, P * t:P * t + P], cw("ident"))
                    ins.then_inc(pt_made, 1)
                e.wait_ge(pt_read, 2 * min(n + 1, 2) + max(n - 1, 0))
                if n:
                    e.wait_ge(o_read, n)
                if u[0] == "p":
                    for h in range(XH):
                        for t in range(2):
                            ins = e.matmul(bank[6][:, P * h:P * h + P], mv[:, t, P * h:P * h + P], pt[:, h // 2, 2 * (h % 2) + t, :], start=(t == 0), stop=(t == 1))
                else:
                    e.wait_ge(s_v, 64 * (u[1] + 1))
                    for b in range(4):
                        for h in range(XH):
                            c = 32 * b + T * h
                            for t in range(2):
                                ins = e.matmul(bank[6][:, c:c + T], cvv[:, b, t, P * h:P * h + P], pt[:, 0, t, c:c + T], start=(t == 0), stop=(t == 1))
                ins.then_inc(o_made, 1)
            e.wait_ge(s_w, 16)
            e.wait_ge(o_read, 4)
            for t, (t0, m) in enumerate(TILES):
                for c in range(4):
                    n = 4 * t + c
                    if n >= 4:
                        e.wait_ge(x_added, n - 3)
                    for h in range(XH):
                        ins = e.matmul(bank[n % 4][:m, :], ot[:, h, t0:t0 + m], wco[:, h, CH * c:CH * c + CH], start=(h == 0), stop=(h == XH - 1))
                    ins.then_inc(x_made, 1)

        @block.vector
        def _(v):
            v.memset(qx[:, :, :], 0.0).then_inc(qx_zero, 1)
            v.wait_ge(qx_zero, 1)
            for n, u in enumerate(UN):
                if u[0] == "p":
                    v.wait_ge(qk_made, 2 * n + 2)
                    for i in range(2):
                        ins = v.tensor_scalar(lg[:, n % 2, 2 * i:2 * i + 2, :], bank[i][:, :].rearrange("p (h s) -> p h s", h=2), P ** -0.5, None, ALU.mult)
                    ins.then_inc(lg_done, 1)
                else:
                    for b in range(4 * u[1], 4 * u[1] + 4):
                        if b >= 2:
                            v.wait_ge(qk_made, 4 + b - 1)
                        v.tensor_copy(qx[:, b % 2, :].rearrange("p (h x) -> p h x", x=40)[:, :, 0:T], qt_[:, :, SP_ + T * b:SP_ + T * b + T]).then_inc(qx_ready, 1)
                    v.wait_ge(qk_made, 4 + 4 * (u[1] + 1))
                    v.tensor_scalar(lg[:, n % 2, 0, :], bank[0][:, 0:MEM], P ** -0.5, None, ALU.mult).then_inc(lg_done, 1)
                v.wait_ge(lg_done, n + 1)
                w = nh(u)
                v.tensor_reduce(sm[:, 0, 0:w], lg[:, n % 2, 0:w, :], AXX, ALU.max, negate=True).then_inc(mx_done, 1)
                v.wait_ge(ex_done, done(n + 1))
                v.reciprocal(sm[:, 2, 0:w], sm[:, 1, 0:w]).then_inc(rc_done, 1)
                v.wait_ge(rc_done, n + 1)
                v.tensor_tensor(lg[:, n % 2, 0:w, :], lg[:, n % 2, 0:w, :], sm[:, 2, 0:w].unsqueeze(2).to_broadcast([P, w, MEM]), ALU.mult).then_inc(nrm, 1)
            for t, (t0, m) in enumerate(TILES):
                for c in range(4):
                    n = 4 * t + c
                    v.wait_ge(x_made, n + 1)
                    xs = x1[:m, t, CH * c:CH * c + CH]
                    v.tensor_tensor(xs, xs, bank[n % 4][:m, :], ALU.add).then_inc(x_added, 1)


def route(ph, I, S):
    nc, pool_dma_sem, sem, bank, cm, cw, pcol, prm, fr = ph
    x1, hn, cmo, gates, slot, rounds = S["x1"], S["hn"], S["cmo"], S["gates"], S["slot"], S["rounds"]
    with ExitStack() as tmp:
        al = lambda n, s, d=F32: tmp.enter_context(nc.sbuf_tensor(n, s, d))
        junk = al("junk3", [P, D])
        stats = al("stats3", [P, 4, 3])
        ht = al("ht3", [P, KT, TOK])
        wr = al("wr", [P, KT, NG + NE])
        br = al("br", [P, NG + NE])
        lo = al("rlog", [P, 3, NG + NE])
        gm = al("gm", [P, 3])
        eg = al("eg", [P, 3, NG])
        cg = al("cg", [P, 3, NG])
        xg = al("xge", [P, 3, NG])
        pg = al("pg", [P, 3])
        m8 = al("rm8", [P, 3, 8])
        gt = al("rgt", [P, 3, NE])
        eq = al("req", [P, 3, NE])
        cum = al("rcum", [P, 3, NE])
        ex = al("rex", [P, 3, NE])
        ws = al("rws", [P, 3])
        need = al("rneed", [P, 1])
        mc = al("mc", [P, 1])
        rf = al("rf", [P, 2])
    s_in, r_made, exps, subs, sel_done, rk_made, rch = [sem("r_" + n) for n in ("in", "logits", "exps", "differences", "selected", "ranks", "chain")]
    an, dn, pn, turned = norm_to_features(ph, "ffn", x1, [m for _, m in TILES], pcol("g_ffn"), ht, lambda e, t: None, (6, 7), (junk, stats), out=hn)
    ones = cmw(cmo, "ones")
    with nc.Block() as block:
        @block.sync
        def _(sp):
            sp.dma_start(cmo[:, :], S["c_moe"]).then_inc(s_in, 16)
            sp.dma_start(wr[:, :, 0:NG], I["w_rg"][0].rearrange("(kt p) n -> p kt n", p=P)).then_inc(s_in, 16)
            sp.dma_start(wr[:, :, NG:], I["w_re"][0].rearrange("(kt p) n -> p kt n", p=P)).then_inc(s_in, 16)
            sp.dma_start(br[:, 0:NG], I["b_rg"][0].partition_broadcast(P)).then_inc(s_in, 16)
            sp.dma_start(br[:, NG:], I["b_re"][0].partition_broadcast(P)).then_inc(s_in, 16)

        @block.scalar
        def _(a):
            an(a)
            a.wait_ge(subs, 1)
            a.activation(xg[:, :, :], xg[:, :, :], ACT.Exp).then_inc(exps, 1)
            a.wait_ge(subs, 2)
            a.activation(ex[:, :, :], ex[:, :, :], ACT.Exp).then_inc(exps, 1)

        @block.tensor
        def _(e):
            pn(e)
            e.wait_ge(*turned)
            e.wait_ge(s_in, 80)
            for t, (t0, m) in enumerate(TILES):
                for k in range(KT):
                    ins = e.matmul(bank[t][:m, 0:NG + NE], ht[:, k, t0:t0 + m], wr[:, k, :], start=(k == 0), stop=(k == KT - 1))
                ins.then_inc(r_made, 1)
            e.wait_ge(sel_done, 1)
            for t in range(3):
                for j in range(t + 1):
                    e.matmul(bank[3][:, NE * t:NE * t + NE], ones if j < t else cmw(cmo, "upto"), gt[:, j, :], start=(j == 0), stop=(j == t))
            for j in range(3):
                ins = e.matmul(bank[3][:, NE * 3:NE * 4], ones, gt[:, j, :], start=(j == 0), stop=(j == 2))
            ins.then_inc(rk_made, 1)

        @block.vector
        def _(v):
            d = chain_of(v, rch)
            d(v.memset(lo[:, :, :], 0.0))
            dn(v)
            v.wait_ge(s_in, 80)
            for t, (t0, m) in enumerate(TILES):
                v.wait_ge(r_made, t + 1)
                d(v.tensor_tensor(lo[:m, t, :], bank[t][:m, 0:NG + NE], br[:m, :], ALU.add))
            gl, el = lo[:, :, 0:NG], lo[:, :, NG:]
            b3 = lambda z, n: z.unsqueeze(2).to_broadcast([P, 3, n])
            d(v.tensor_reduce(gm[:, :], gl, AXX, ALU.max))
            v.tensor_tensor(xg[:, :, :], gl, b3(gm[:, :], NG), ALU.subtract).then_inc(subs, 1)
            d(v.tensor_tensor(eg[:, :, :], gl, b3(gm[:, :], NG), ALU.is_equal))
            for t in range(3):
                d(v.tensor_tensor_scan(cg[:, t, :], ones[:, 0:NG], eg[:, t, :], 0.0, ALU.mult, ALU.add))
            d(v.scalar_tensor_tensor(eg[:, :, :], cg[:, :, :], 1.0, eg[:, :, :], ALU.is_le, ALU.mult))
            d(v.tensor_scalar(eg[:, :, :], eg[:, :, :], -1.0, -NEG, ALU.add, ALU.mult))
            d(v.tensor_tensor(el.rearrange("p t (g x) -> p t g x", g=NG), el.rearrange("p t (g x) -> p t g x", g=NG),
                              eg[:, :, :].unsqueeze(3).to_broadcast([P, 3, NG, EPG]), ALU.add))
            for t in range(3):
                top_mask(v, d, el[:, t, :], None, m8[:, t, :], gt[:, t, :], eq[:, t, :], cum[:, t, :], ones[:, 0:NE], need, 2, None, NE, P)
            v.wait_ge(subs, 1)
            v.tensor_tensor(ex[:, :, :], el, m8[:, :, 0:1].to_broadcast([P, 3, NE]), ALU.subtract).then_inc(subs, 1)
            v.memset(gt[64:P, 2, :], 0.0).then_inc(sel_done, 1)
            v.wait_ge(exps, 2)
            d(v.tensor_reduce(pg[:, :], xg[:, :, :], AXX, ALU.add))
            d(v.tensor_tensor(ex[:, :, :], ex[:, :, :], gt[:, :, :], ALU.mult))
            d(v.memset(ex[64:P, 2, :], 1.0))
            d(v.tensor_reduce(ws[:, :], ex[:, :, :], AXX, ALU.add))
            d(v.tensor_tensor(ws[:, :], ws[:, :], pg[:, :], ALU.mult))
            d(v.reciprocal(ws[:, :], ws[:, :]))
            d(v.tensor_tensor(gates[:, :, :], ex[:, :, :], b3(ws[:, :], NE), ALU.mult))
            v.wait_ge(rk_made, 1)
            d(v.tensor_tensor(slot[:, :, :], bank[3][:, 0:3 * NE].rearrange("p (t e) -> p t e", t=3), gt[:, :, :], ALU.mult))
            d(v.tensor_scalar(slot[:, :, :], slot[:, :, :], -1.0, None, ALU.add))
            d(v.tensor_reduce(mc[:, :], bank[3][:, 3 * NE:4 * NE], AXX, ALU.max))
            d(v.memset(rf[:, 0:1], 1.0))
            for r in range(1, -(-TOK // SLOTS)):
                d(v.tensor_scalar(rf[:, 1:2], mc[:, :], float(SLOTS * r), None, ALU.is_gt))
                d(v.tensor_tensor(rf[:, 0:1], rf[:, 0:1], rf[:, 1:2], ALU.add))
            d(v.tensor_copy(rounds[:, :], rf[:, 0:1]))


def experts(ph, I, S):
    nc, pool_dma_sem, sem, bank, cm, cw, pcol, prm, fr = ph
    x1, hn, cmo, gates, slot, rounds = S["x1"], S["hn"], S["cmo"], S["gates"], S["slot"], S["rounds"]
    with ExitStack() as tmp:
        w = tmp.enter_context(nc.sbuf_tensor("wexp", [P, RING, 2, 4 * DE], F32))
    flat = fr[:, :, :].rearrange("p a b -> p (a b)")
    at = [0]

    def view(n):
        at[0] += n
        return flat[:, at[0] - n:at[0]]
    xg = view(KT * P).rearrange("p (k s) -> p k s", k=KT)
    ys = view(D)
    oh = view(3 * P).rearrange("p (t s) -> p t s", t=3)
    og = view(3 * P).rearrange("p (t s) -> p t s", t=3)
    sg = view(TOK)
    u1, u2 = view(DE), view(DE)
    ut = view(DE).rearrange("p (f s) -> p f s", f=4)
    s_w = [sem(f"wexp_in{i}") for i in range(RING)]
    w_used, oh_ready, xg_made, xg_read, h_made, silu_done, u_done = [sem("m_" + n) for n in (
        "w_used", "onehots", "gathered", "gathered_read", "hidden", "silu", "u")]
    ut_made, ut_read, sg_made, sg_read, y_made, y_read, sc_made, sc_read, slot_ready = [sem("m_" + n) for n in (
        "u_turned", "u_taken", "onehots_turned", "onehots_taken", "y_made", "y_read", "scattered", "added", "slots_ready")]
    UNITS = 12
    w13 = [I[n][0].rearrange("(g a) (kt p) n -> g p a kt n", a=2, p=P) for n in ("w_e1", "w_e3")]
    w2 = I["w_e2"][0].rearrange("(g a) (f p) n -> g p a f n", a=2, p=P)
    half = lambda z, a: z[SLOTS * a:SLOTS * a + SLOTS]
    PAIRS = NE // 2

    def number_of_rounds(eng):
        return eng.value_load(rounds[0:1, 0:1], min_val=1, max_val=-(-TOK // SLOTS))

    with nc.Block() as block:
        @block.sync
        def _(sp):
            with sp.Fori(0, number_of_rounds(sp)) as r:
                with sp.Fori(0, PAIRS) as p:
                    g = r * PAIRS + p
                    for u in range(UNITS):
                        sp.wait_ge(w_used, g * UNITS + (u + 1))
                        for a_ in range(2):
                            if u < 8:
                                src = w13[u // 4][bass.DynSlice(p, 1), :, a_, 4 * (u % 4):4 * (u % 4) + 4, :].squeeze(0)
                                dst = w[:, u % RING, a_, :].rearrange("p (k n) -> p k n", k=4)
                            else:
                                src = w2[bass.DynSlice(p, 1), :, a_, u - 8, :].squeeze(0)
                                dst = w[:, u % RING, a_, :]
                            sp.dma_start(dst, src).then_inc(s_w[u % RING], 16)

        @block.vector
        def _(v):
            v.sem_inc(sc_read, 1)
            v.sem_inc(slot_ready, 1)
            with v.Fori(0, number_of_rounds(v)) as r:
                with v.Fori(0, PAIRS) as p:
                    g = r * PAIRS + p
                    v.wait_ge(slot_ready, r + 1)
                    mine = lambda z: z[:, :, bass.DynSlice(2 * p, 2)].unsqueeze(3).to_broadcast([P, 3, 2, SLOTS])
                    cut = lambda z: z.rearrange("p t (e s) -> p t e s", e=2)
                    v.tensor_tensor(cut(oh), cmw(cmo, "iota_slots").unsqueeze(1).unsqueeze(1).to_broadcast([P, 3, 2, SLOTS]), mine(slot), ALU.is_equal).then_inc(oh_ready, 1)
                    v.wait_ge(oh_ready, 2 * g + 1)
                    v.tensor_tensor(cut(og), cut(oh), mine(gates), ALU.mult).then_inc(oh_ready, 1)
                    for q in range(4):
                        v.wait_ge(xg_made, 4 * g + (q + 1))
                        v.tensor_tensor(xg[:, 4 * q:4 * q + 4, :], bank[6 + q % 2][:, :].rearrange("p (k s) -> p k s", k=4),
                                        pcol("g_ffn")[:, 4 * q:4 * q + 4].unsqueeze(2).to_broadcast([P, 4, P]), ALU.mult).then_inc(xg_read, 1)
                    v.wait_ge(silu_done, g + 1)
                    v.wait_ge(h_made, 2 * g + 2)
                    v.tensor_tensor(u2, u1, bank[1][:, :], ALU.mult).then_inc(u_done, 1)
                    for i in range(12):
                        t, c = divmod(i, 4)
                        m = TILES[t][1]
                        v.wait_ge(sc_made, 12 * g + (i + 1))
                        xs = x1[:m, t, CH * c:CH * c + CH]
                        v.tensor_tensor(xs, xs, bank[6 + i % 2][:m, :], ALU.add).then_inc(sc_read, 1)
                v.tensor_scalar(slot[:, :, :], slot[:, :, :], -float(SLOTS), None, ALU.add).then_inc(slot_ready, 1)

        @block.scalar
        def _(a):
            with a.Fori(0, number_of_rounds(a)) as r:
                with a.Fori(0, PAIRS) as p:
                    g = r * PAIRS + p
                    a.wait_ge(h_made, 2 * g + 1)
                    a.activation(u1, bank[0][:, :], ACT.Silu).then_inc(silu_done, 1)
                    a.wait_ge(sg_made, g + 1)
                    a.activation(sg, bank[1][:, 0:TOK], ACT.Copy).then_inc(sg_read, 1)
                    a.wait_ge(ut_made, g + 1)
                    a.activation(ut, bank[0][:, :].rearrange("p (f s) -> p f s", f=4), ACT.Copy).then_inc(ut_read, 1)
                    a.wait_ge(y_made, g + 1)
                    for c in range(4):
                        a.activation(ys[:, CH * c:CH * c + CH], bank[2 + c][:, :], ACT.Copy).then_inc(y_read, 1)

        @block.tensor
        def _(e):
            e.sem_inc(w_used, RING)
            with e.Fori(0, number_of_rounds(e)) as r:
                with e.Fori(0, PAIRS) as p:
                    g = r * PAIRS + p
                    e.wait_ge(oh_ready, 2 * g + 1)
                    e.wait_ge(sc_read, 12 * g + 1)
                    for q in range(4):
                        if q >= 2:
                            e.wait_ge(xg_read, 4 * g + (q - 1))
                        for k in range(4 * q, 4 * q + 4):
                            for t, (t0, m) in enumerate(TILES):
                                ins = e.matmul(bank[6 + q % 2][:, (k % 4) * P:(k % 4 + 1) * P], hn[:m, t, k * P:(k + 1) * P], oh[:m, t, :],
                                               start=(t == 0), stop=(t == 2))
                        ins.then_inc(xg_made, 1)
                    e.wait_ge(xg_read, 4 * g + 4)
                    for u in range(8):
                        e.wait_ge(s_w[u % RING], 64 * g + 32 * (u // RING + 1))
                        for k in range(4):
                            for a_ in range(2):
                                kk = 4 * (u % 4) + k
                                ins = e.matmul(half(bank[u // 4], a_), xg[:, kk, SLOTS * a_:SLOTS * a_ + SLOTS],
                                               w[:, u % RING, a_, DE * k:DE * k + DE], start=(kk == 0), stop=(kk == KT - 1))
                            if k == 3:
                                ins.then_inc(w_used, 1)
                        if u % 4 == 3:
                            e.wait_ge(w_used, g * UNITS + (u + 1 + RING))
                            e.sem_inc(h_made, 1)
                    e.wait_ge(u_done, g + 1)
                    for t, (t0, m) in enumerate(TILES):
                        ins = e.transpose(bank[1][:, t0:t0 + m], og[:m, t, :], cw("ident")[:m, :m])
                    ins.then_inc(sg_made, 1)
                    for f in range(4):
                        ins = e.transpose(bank[0][:, f * P:(f + 1) * P], u2[:, f * P:(f + 1) * P], cw("ident"))
                    ins.then_inc(ut_made, 1)
                    e.wait_ge(ut_read, g + 1)
                    for f in range(4):
                        u = 8 + f
                        e.wait_ge(s_w[u % RING], 64 * g + 32 * (u // RING + 1))
                        for c in range(4):
                            for a_ in range(2):
                                ins = e.matmul(half(bank[2 + c], a_), ut[:, f, SLOTS * a_:SLOTS * a_ + SLOTS],
                                               w[:, u % RING, a_, CH * c:CH * c + CH], start=(f == 0), stop=(f == 3))
                        ins.then_inc(w_used, 1)
                    e.wait_ge(w_used, g * UNITS + (UNITS + RING))
                    e.sem_inc(y_made, 1)
                    e.wait_ge(sg_read, g + 1)
                    e.wait_ge(y_read, 4 * g + 4)
                    for i in range(12):
                        t, c = divmod(i, 4)
                        t0, m = TILES[t]
                        if i >= 2:
                            e.wait_ge(sc_read, 12 * g + i)
                        e.matmul(bank[6 + i % 2][:m, :], sg[:, t0:t0 + m], ys[:, CH * c:CH * c + CH], start=True, stop=True).then_inc(sc_made, 1)


def finish(ph, I, O, S):
    nc, pool_dma_sem, sem, bank, cm, cw, pcol, prm, fr = ph
    x1 = S["x1"]
    with ExitStack() as tmp:
        al = lambda n, s, d=F32: tmp.enter_context(nc.sbuf_tensor(n, s, d))
        junk = al("junk4", [P, D])
        st_ = al("stats4", [P, 4, 3])
        gf = al("gf", [P, D])
    s_g, sq, ms, rt, rc, fo, s_o = [sem("f_" + n) for n in ("gain_in", "squares", "mean", "root", "recip", "out", "stored")]
    with nc.Block() as block:
        @block.sync
        def _(sp):
            sp.dma_start(gf[:, :], I["g_final"].partition_broadcast(P)).then_inc(s_g, 16)
            for t, (t0, m) in enumerate(TILES):
                sp.wait_ge(fo, t + 1)
                dst = O["y_p"][0] if t < 2 else O["y_s"].rearrange("b t d -> (b t) d")
                sp.dma_start(dst[t0 % SP_:t0 % SP_ + m, :], x1[:m, t, :]).then_inc(s_o, 16)
            sp.wait_ge(s_o, 48)

        @block.scalar
        def _(a):
            for t, (t0, m) in enumerate(TILES):
                if t:
                    a.wait_ge(sq, t)
                a.activation(junk[:m, :], x1[:m, t, :], ACT.Square, accum_out=st_[:m, 0, t:t + 1]).then_inc(sq, 1)
            for t, (t0, m) in enumerate(TILES):
                a.wait_ge(ms, t + 1)
                a.activation(st_[:m, 2, t:t + 1], st_[:m, 1, t:t + 1], ACT.Sqrt).then_inc(rt, 1)

        @block.vector
        def _(v):
            for t, (t0, m) in enumerate(TILES):
                v.wait_ge(sq, t + 1)
                v.tensor_scalar(st_[:m, 1, t:t + 1], st_[:m, 0, t:t + 1], 1.0 / D, EPS, ALU.mult, ALU.add).then_inc(ms, 1)
            v.wait_ge(s_g, 16)
            for t, (t0, m) in enumerate(TILES):
                v.wait_ge(rt, t + 1)
                v.reciprocal(st_[:m, 3, t:t + 1], st_[:m, 2, t:t + 1]).then_inc(rc, 1)
                v.wait_ge(rc, t + 1)
                v.scalar_tensor_tensor(x1[:m, t, :], x1[:m, t, :], st_[:m, 3, t:t + 1], gf[:m, :], ALU.mult, ALU.mult).then_inc(fo, 1)


_INS = ["x_prompt", "x_sample", "mem_prompt", "cache_k", "cache_v", "cache_idx_k", "page_table", "state_wkv",
        "state_shift", "cache_mem_k", "cache_mem_v", "g_mix", "w_in", "mu_shift", "rw_w0", "rw_w2", "rw_a0", "rw_a2",
        "rw_g2", "rw_kk", "rw_ka", "rw_rk", "rw_ln_g", "rw_ln_b", "w_out", "g_cross", "g_mem", "w_cq", "w_ck", "w_cv",
        "w_co", "g_ffn", "w_rg", "b_rg", "w_re", "b_re", "w_e1", "w_e3", "w_e2", "rel_bias", "g_final"]
_OUTS = [("y_p", (1, 256, 2048)), ("y_s", (8, 8, 2048)), ("k_p", (1, 1, 256, 16, 64)), ("v_p", (1, 1, 256, 16, 64)),
         ("ik_p", (1, 1, 256, 64)), ("wkv_p", (1, 1, 16, 64, 64)), ("shift_p", (1, 1, 3328)),
         ("mk_p", (1, 1, 256, 4, 128)), ("mv_p", (1, 1, 256, 4, 128)), ("k_s", (1, 8, 8, 16, 64)),
         ("v_s", (1, 8, 8, 16, 64)), ("ik_s", (1, 8, 8, 64)), ("wkv_s", (1, 8, 16, 64, 64)), ("shift_s", (1, 8, 3328))]


def kernel(**inputs):
    import numpy as _np
    import concourse.bacc as _bacc
    from concourse import mybir as _mybir
    from concourse.bass_utils import run_bass_kernel_spmd as _run

    nc = _bacc.Bacc("TRN2", target_bir_lowering=False, num_devices=1)
    arrays, ins, cons, outs = {}, {}, {}, {}
    for name in _INS:
        a = _np.ascontiguousarray(inputs[name])
        arrays[f"in_{name}"] = a
        ins[name] = nc.dram_tensor(f"in_{name}", a.shape, _mybir.dt.from_np(a.dtype), kind="ExternalInput").ap()
    for name, a in CONSTS.items():
        arrays[name] = a
        cons[name] = nc.dram_tensor(name, a.shape, _mybir.dt.from_np(a.dtype), kind="ExternalInput").ap()
    for name, shape in _OUTS:
        outs[name] = nc.dram_tensor(f"out_{name}", shape, F32, kind="ExternalOutput").ap()
    build(nc, ins, outs, cons)
    r = _run(nc, [arrays], core_ids=[0])
    return tuple(r.results[0][f"out_{name}"] for name, _ in _OUTS)
```

```python
from contextlib import ExitStack

import numpy as np

import concourse.bass as bass
from concourse import mybir

F32 = mybir.dt.float32
I32 = mybir.dt.int32
ALU = mybir.AluOpType
ACT = mybir.ActivationFunctionType
AXX = mybir.AxisListType.X

P = 128
D = 2048
KT = D // P
SP_, SS = 256, 64
TOK = SP_ + SS
DB, T = 8, 8
TILES = [(0, 128), (128, 128), (256, 64)]
HD = 64
NH = 16
HP = NH // 2
RWT = 26
RWP = RWT * P
ATC = 4176
ATT = 33
AT = NH * HD
IDXW = NH ** -0.5 * HD ** -0.5
CH = 512
CP, CS = 16, 8
PAST, PAGE, NPG = 1024, 128, 8
KEYS = PAST + SS
NEG = -1.0e30
XW, XH, MEM = 512, 4, 256
NE, NG, EPG, DE = 32, 4, 8, 512
EPS = 1e-6
SLOTS = 64
RING = 6
GN_EPS = 64e-5
TOPK_P, TOPK_S = 64, 256
REV = 1536

PRM_ORDER = [("mu_shift", 26), ("g_mix", 16), ("rw_w0", 8), ("rw_a0", 8), ("rw_kk", 8), ("rw_ka", 8), ("rw_rk", 8),
             ("rw_ln_g", 8), ("rw_ln_b", 8), ("g_cross", 16), ("PAD", 14), ("g_ffn", 16), ("g_mem", 16)]
PRM = {}
_at = 0
for _n, _k in PRM_ORDER:
    PRM[_n] = (_at, _k)
    _at += _k
PRM_GROUPS = (P - PRM.pop("PAD")[1], _at - P)


def consts():
    p = np.arange(P)
    out = {}
    ident = np.eye(P, dtype=np.float32)
    bones = (p[:, None] // HD == p[None, :] // HD).astype(np.float32)

    def chunk_masks(m, c):
        s, t = np.arange(m)[:, None], np.arange(m)[None, :]
        same = s // c == t // c
        return np.stack([same & (s < t), same & (s <= t)], 1), same & (t < s)

    ab16, lo16 = chunk_masks(128, CP)
    ab8, lo8 = chunk_masks(64, CS)
    scan = np.ones(TOK)
    scan[0:SP_:CP] = 0
    scan[SP_::CS] = 0
    em16 = p[:, None] // CP == np.arange(8)[None, :]
    em8 = p[:, None] // CS == np.arange(8)[None, :]
    pad = lambda a: np.concatenate([a.reshape(a.shape[0], -1), np.zeros((P - a.shape[0], a[0].size))], 0)
    cols = [("ident", ident), ("bones", bones), ("ab16", ab16), ("lo16", lo16), ("ab8", pad(ab8)), ("lo8", pad(lo8)),
            ("scan", np.broadcast_to(scan, (P, TOK))), ("em16", em16), ("em8", em8)]
    where, at, parts = {}, 0, []
    for n, a in cols:
        a = a.reshape(P, -1).astype(np.float32)
        where[n] = (at, a.shape[1])
        at += a.shape[1]
        parts.append(a)
    out["c_main"] = np.ascontiguousarray(np.concatenate(parts, 1))
    to_head = np.stack([2 * j + p[:, None] // HD == np.arange(NH)[None, :] for j in range(HP)], 1)
    out["c_heads"] = np.ascontiguousarray(np.concatenate([to_head.reshape(P, -1), pad(to_head.transpose(2, 1, 0))], 1).astype(np.float32))

    q = np.arange(2 * P)
    cn = np.where(np.arange(SP_)[None, :] <= q[:, None], 0, NEG).reshape(2, P, SP_).transpose(1, 0, 2)
    bq = np.arange(SS)
    cns = np.where((bq[:, None] // T == bq[None, :] // T) & (bq[None, :] % T <= bq[:, None] % T), 0, NEG)
    hq = np.arange(P)
    rep = np.stack([(bq[:, None] // T == b) & (bq[:, None] % T == hq[None, :] % T) for b in range(DB)], 1)
    reph = np.zeros((P, P))
    reph[64:80] = np.arange(NH)[:, None] == hq[None, :] // T
    dqq = hq[:, None] % T == bq[None, :] % T
    at, parts = 0, []
    for n, a in [("cn", cn), ("cns", pad(cns)), ("rep", pad(rep)), ("reph", reph), ("dqq", dqq), ("iota", p[:, None])]:
        a = a.reshape(P, -1).astype(np.float32)
        where[n] = (at, a.shape[1])
        at += a.shape[1]
        parts.append(a)
    out["c_dsa"] = np.ascontiguousarray(np.concatenate(parts, 1))
    at, parts = 0, []
    for n, a in [("ones", np.ones((P, P))), ("upto", p[:, None] <= p[None, :]), ("iota_slots", np.broadcast_to(np.arange(SLOTS), (P, SLOTS)))]:
        a = a.reshape(P, -1).astype(np.float32)
        where[n] = (at, a.shape[1])
        at += a.shape[1]
        parts.append(a)
    out["c_moe"] = np.ascontiguousarray(np.concatenate(parts, 1))
    dist = np.maximum(PAST + T - 1 - np.arange(REV), 0)
    far = 16 + (np.log(np.maximum(dist, 1).astype(np.float32) / np.float32(16)) / np.float32(np.log(8.0)) * np.float32(16)).astype(np.int32)
    bucket = np.where(dist < 16, dist, np.minimum(far, 31))
    out["c_bkt"] = (np.arange(32)[:, None] == bucket[None, :]).astype(np.float32)
    return out, where


CONSTS, CW = consts()


def cmw(cmo, n):
    return cmo[:, CW[n][0]:CW[n][0] + CW[n][1]]


def cdw(cd, n):
    return cd[:, CW[n][0]:CW[n][0] + CW[n][1]]


def build(nc, I, O, C):
    st = ExitStack()
    with st:
        def keep(name, shape, dt=F32):
            return st.enter_context(nc.sbuf_tensor(name, shape, dt))

        sems = Semaphores(nc, st)
        sem, pool_dma_sem = sems.new, sems.of_pool_dma
        bank = [st.enter_context(nc.psum_tensor(f"bank{i}", [P, 512], F32)) for i in range(8)]
        cm = keep("cm", [P, CONSTS["c_main"].shape[1]])
        cw = lambda n: cm[:, CW[n][0]:CW[n][0] + CW[n][1]]
        prm = keep("prm", [P, 2, P])
        pcol = lambda n: prm[:, PRM[n][0] // P, PRM[n][0] % P:PRM[n][0] % P + PRM[n][1]]
        fr = keep("fr", [P, RWT, TOK])
        ph = (nc, pool_dma_sem, sem, bank, cm, cw, pcol, prm, fr)
        fat_d = nc.dram_tensor("fat_d", (P, ATT, TOK), F32, kind="Internal").ap()
        project(ph, I, O, C, fat_d)
        sems.clear()
        with ExitStack() as tmp:
            al = lambda n, s, d=F32: tmp.enter_context(nc.sbuf_tensor(n, s, d))
            R = {"t": [al(f"t{i}", [P, HP, TOK])[:, :, :] for i in range(1, 7)] + [al("ar", [P, 2, HP, TOK])]}
            R["al"] = al
            rwkv_prepare(ph, I, O, C, R)
            sems.clear()
            rwkv_core(ph, I, O, R)
            sems.clear()
            rwkv_finish(ph, I, O, C, R)
            sems.clear()
        rev_d = nc.dram_tensor("rev_d", (NH, REV), F32, kind="Internal").ap()
        tp_d = nc.dram_tensor("tp_d", (NH, P, 3 * P), F32, kind="Internal").ap()
        bs_d = nc.dram_tensor("bs_d", (NH, T, KEYS), F32, kind="Internal").ap()
        with ExitStack() as tmp:
            al = lambda n, s, d=F32: tmp.enter_context(nc.sbuf_tensor(n, s, d))
            S = {"ik2": al("ik2", [P, TOK]), "vt": al("vt", [P, 3, AT]), "ikw": al("ikw", [P, 3, 80]),
                 "cd": al("cd", [P, CONSTS["c_dsa"].shape[1]]), "nm": al("nm", [P, 2, SP_]),
                 "iqs": al("iqs", [P, DB, HP, 2, T]), "wts": al("wts", [P, 576]), "qs": al("qs", [P, 2, 1152]),
                 "qn": al("qn", [P, HP, SS]), "kn": al("kn", [P, HP, SS])}
            S.update(pti=al("pti", [1, DB * NPG], I32), nms=al("nms", [SS, KEYS]))
            fa_space = tmp.enter_context(nc.sbuf_tensor("fa2", [P, ATT, TOK], F32))
            S["fa"] = fa_space
            S["kp"] = al("kp", [P, NPG, AT])
            S["ki"] = S["kp"][:, :, :].rearrange("p n c -> p (n c)")[:, 0:DB * NPG * HD].rearrange("p (b n d) -> p b n d", b=DB, n=NPG)
            dsa_prepare(ph, I, O, C, fat_d, rev_d, tp_d, bs_d, S)
            sems.clear()
            with ExitStack() as tmp2:
                S["sc"] = tmp2.enter_context(nc.sbuf_tensor("ssc", [SS, KEYS], F32))
                sample_scores(ph, I, S)
                sems.clear()
                dsa_prompt(ph, I, O, tp_d, S)
                sems.clear()
            sample_attention(ph, I, O, bs_d, S)
            sems.clear()
        x1 = keep("x1", [P, 3, D])
        with ExitStack() as tmp:
            al = lambda n, s, d=F32: tmp.enter_context(nc.sbuf_tensor(n, s, d))
            S = {"x1": x1, "mk": al("mk", [P, 2, XW]), "mv": al("mv", [P, 2, XW]), "mkt": al("mkt", [P, XH, MEM]), "qt": al("qt", [P, XH, TOK])}
            mix_out(ph, I, O, S)
            sems.clear()
            cross(ph, I, O, S)
            sems.clear()
        with ExitStack() as tmp:
            al = lambda n, s, d=F32: tmp.enter_context(nc.sbuf_tensor(n, s, d))
            S = {"x1": x1, "hn": al("hn", [P, 3, D]), "cmo": al("cmo", [P, CONSTS["c_moe"].shape[1]]), "c_moe": C["c_moe"],
                 "gates": al("gates", [P, 3, NE]), "slot": al("slot", [P, 3, NE]), "rounds": al("rounds", [P, 1], I32),
                 "w": al("wexp", [P, RING, 2, 4 * DE]), "s_w": [sems.lasting(f"wexp_in{i}") for i in range(RING)]}
            route(ph, I, S)
            sems.clear()
            experts(ph, I, S)
            sems.clear()
            finish(ph, I, O, S)


class Semaphores:

    def __init__(self, nc, kept):
        self.kept = kept
        self.nc, self.live, self.stack = nc, [], ExitStack()

    def new(self, name):
        self.live.append(self.stack.enter_context(self.nc.semaphore(name)))
        return self.live[-1]

    def lasting(self, name):
        return self.kept.enter_context(self.nc.semaphore(name))

    def of_pool_dma(self, name):
        return self.kept.enter_context(self.nc.semaphore(name))

    def clear(self):
        with self.nc.Block() as block:
            @block.sync
            def _(sp):
                for s in self.live:
                    sp.sem_clear(s)
        self.stack.close()
        self.live, self.stack = [], ExitStack()


def chain_of(eng, sem):
    n = [0]

    def step(ins):
        n[0] += 1
        ins.then_inc(sem, 1)
        eng.wait_ge(sem, n[0])
    return step


def norm_to_features(ph, tag, x, sizes, gain, ht, wait_x, tb, scratch, out=None):
    nc, pool_dma_sem, sem, bank, cm, cw, pcol, prm, fr = ph
    junk, stats = scratch
    out = x if out is None else out
    ssq, msq, rtd, rst, hrm, tpm, tpr = [sem(f"{tag}_{n}") for n in
                                         ("squares", "mean", "root", "recip", "scaled", "turned", "taken")]
    n = len(sizes)

    def act(a):
        for t, m in enumerate(sizes):
            wait_x(a, t)
            if t:
                a.wait_ge(ssq, t)
            a.activation(junk[:m, :], x[:m, t, :], ACT.Square, accum_out=stats[:m, 0, t:t + 1]).then_inc(ssq, 1)
        for t, m in enumerate(sizes):
            a.wait_ge(msq, t + 1)
            a.activation(stats[:m, 2, t:t + 1], stats[:m, 1, t:t + 1], ACT.Sqrt).then_inc(rtd, 1)
        for t, m in enumerate(sizes):
            a.wait_ge(rst, t + 1)
            a.activation(out[:m, t, :], x[:m, t, :], ACT.Copy, scale=stats[:m, 3, t:t + 1]).then_inc(hrm, 1)

    def dve(v):
        for t, m in enumerate(sizes):
            v.wait_ge(ssq, t + 1)
            v.tensor_scalar(stats[:m, 1, t:t + 1], stats[:m, 0, t:t + 1], 1.0 / D, EPS, ALU.mult, ALU.add).then_inc(msq, 1)
        for t, m in enumerate(sizes):
            v.wait_ge(rtd, t + 1)
            v.reciprocal(stats[:m, 3, t:t + 1], stats[:m, 2, t:t + 1]).then_inc(rst, 1)
        for t, m in enumerate(sizes):
            for q in range(KT // 4):
                v.wait_ge(tpm, 4 * t + q + 1)
                v.tensor_tensor(ht[:, 4 * q:4 * q + 4, 128 * t:128 * t + m],
                                bank[tb[q % 2]][:, 0:4 * m].rearrange("p (a m) -> p a m", a=4),
                                gain[:, 4 * q:4 * q + 4].unsqueeze(2).to_broadcast([P, 4, m]), ALU.mult).then_inc(tpr, 1)

    def pe(e):
        for t, m in enumerate(sizes):
            e.wait_ge(hrm, t + 1)
            for q in range(KT // 4):
                g = 4 * t + q
                if g >= 2:
                    e.wait_ge(tpr, g - 1)
                for a in range(4):
                    k = 4 * q + a
                    ins = e.transpose(bank[tb[q % 2]][:, a * m:(a + 1) * m], out[:m, t, k * P:(k + 1) * P],
                                      cw("ident")[:m, :m])
                ins.then_inc(tpm, 1)
    return act, dve, pe, (tpr, 4 * n)


def project(ph, I, O, C, fat_d):
    nc, pool_dma_sem, sem, bank, cm, cw, pcol, prm, fr = ph
    with ExitStack() as tmp:
        al = lambda n, s, d=F32: tmp.enter_context(nc.sbuf_tensor(n, s, d))
        fa = al("fa", [P, ATT, TOK])
        x = al("x", [P, 3, D])
        junk = al("junk", [P, D])
        stats = al("stats", [P, 4, 3])
        ht = al("ht", [P, KT, TOK])
        w = al("w", [P, 2, KT, CH])
        prin = al("prin", [P, 2, P])
        ssin = al("ssin", [104, 2, P])
        ss = al("ss", [P, DB, RWT])
        sho = al("sho", [P, 9, RWT])
        shw = al("shw", [104, 3, P])
    diff = x[:, :, :].rearrange("p t d -> p (t d)")[:, 0:HP * TOK].rearrange("p (c t) -> p c t", c=HP)
    s_ss = sem("state_shift_in")
    ss_turned, sho_ready, sho_turned, sho_sb, s_sho, shift_ch = [sem(n) for n in (
        "ss_turned", "shift_rows_ready", "shift_rows_turned", "shift_rows_copied", "shift_rows_out", "shift_chain")]
    SHG = [(0, 26), (26, 104), (130, 104)]
    s_c, s_x, s_prin = sem("consts_in"), [sem(f"x_in{t}") for t in range(3)], (pool_dma_sem("params_in_pool"), sem("params_in_act"))
    s_prt, s_prm = sem("params_turned"), sem("params_ready")
    s_w = [sem("win0_in"), sem("win1_in")]
    s_w0 = sem("win_first_half_in")
    f_made, f_read, s_sp = sem("f_made"), sem("f_read"), sem("fat_out")
    win = I["w_in"][0].rearrange("(kt p) n -> p kt n", p=P)
    gain = pcol("g_mix")
    act_n, dve_n, pe_n, (tpr, nt) = norm_to_features(
        ph, "mix", x, [m for _, m in TILES], gain, ht, lambda e, t: e.wait_ge(s_x[t], 16), (6, 7), (junk, stats))
    n_rw = RWP // CH

    def load_params(eng, names, s_):
        for name in names:
            r0, k = PRM[name]
            src = (I[name][0] if name != "rw_rk" else I[name][0].rearrange("h d -> (h d)")).rearrange("(r p) -> r p", p=P)
            eng.dma_start(prin[r0 % P:r0 % P + k, r0 // P, :], src).then_inc(s_, 16)
    names = list(PRM)
    by_pool, by_act = names[0::2], names[1::2]

    def params_in(eng):
        eng.wait_ge(s_prin[0], 16 * len(by_pool))
        eng.wait_ge(s_prin[1], 16 * len(by_act))

    with nc.Block() as block:
        @block.sync
        def _(sp):
            def load(buf, col, width):
                sp.dma_start(w[:, buf, :, 0:width], win[:, :, col:col + width] if isinstance(col, int)
                             else win[:, :, bass.DynSlice(col, width)]).then_inc(s_w[buf], 16)
            for t, (t0, m) in enumerate(TILES):
                src = I["x_prompt"][0] if t < 2 else I["x_sample"].rearrange("b t d -> (b t) d")
                sp.dma_start(x[:m, t, :], src[t0 % SP_:t0 % SP_ + m, :]).then_inc(s_x[t], 16)
                if t == 0:
                    sp.dma_start(cm[:, :], C["c_main"]).then_inc(s_c, 16)
            src = I["state_shift"][0].rearrange("b (c p) -> (b c) p", p=P)
            for g in range(2):
                sp.dma_start(ssin[:, g, :], src[104 * g:104 * g + 104, :]).then_inc(s_ss, 16)
            params_in(sp)
            sp.dma_start(w[:, 0, 0:KT // 2, :], win[:, 0:KT // 2, 0:CH]).then_inc(s_w0, 16)
            sp.dma_start(w[:, 0, KT // 2:, :], win[:, KT // 2:, 0:CH]).then_inc(s_w[0], 16)
            load(1, CH, CH)
            with sp.Fori(1, n_rw // 2) as i:
                for b in range(2):
                    sp.wait_ge(f_made, 8 * i + 4 * b - 4)
                    load(b, (2 * i + b) * CH, CH)
            sp.wait_ge(f_made, 4 * (n_rw - 1))
            load(0, n_rw * CH, CH // 2)
            for c in range(2):
                sp.wait_ge(f_made, 24 if c == 0 else 26)
                load((c + 1) % 2, RWP + c * CH, CH)
            with sp.Fori(1, 4) as i:
                for b in range(2):
                    sp.wait_ge(f_made, 22 + 8 * i + 4 * b)
                    load((b + 1) % 2, RWP + (2 * i + b) * CH, CH)
                sp.wait_ge(f_read, 26 + 8 * i)
                sp.dma_start(fat_d[:, bass.DynSlice(8 * i - 8, 8), :], fa[:, bass.DynSlice(8 * i - 8, 8), :]).then_inc(s_sp, 16)
            sp.wait_ge(f_made, 26 + 4 * 7)
            load(1, RWP + 8 * CH, 80)
            sp.wait_ge(sho_sb, 3)
            sp.dma_start(O["shift_p"][0, 0].rearrange("(c p) -> c p", p=P), shw[0:26, 0, :]).then_inc(s_sho, 16)
            dst = O["shift_s"][0].rearrange("b (c p) -> (b c) p", p=P)
            for g in range(2):
                sp.dma_start(dst[104 * g:104 * g + 104, :], shw[:, 1 + g, :]).then_inc(s_sho, 16)
            sp.wait_ge(f_read, 59)
            sp.dma_start(fat_d[:, 24:ATT - 1, :], fa[:, 24:ATT - 1, :]).then_inc(s_sp, 16)
            sp.dma_start(fat_d[0:80, ATT - 1, :], fa[0:80, ATT - 1, :]).then_inc(s_sp, 16)
            sp.wait_ge(s_sp, 16 * 5)
            sp.wait_ge(s_sho, 48)

        @block.gpsimd
        def _(g):
            load_params(g, by_pool, s_prin[0])
            g.wait_ge(s_prin[0], 16 * len(by_pool))

        @block.scalar
        def _(a):
            load_params(a, by_act, s_prin[1])
            act_n(a)

            def take(n, dst, width, b):
                a.wait_ge(f_made, n + 1)
                a.activation(dst, bank[b][:width, 0:TOK], ACT.Copy).then_inc(f_read, 1)
            with a.Fori(0, n_rw) as i:
                for j in range(4):
                    take(4 * i + j, fr[:, bass.DynSlice(4 * i + j, 1), :], P, j)
            for j in range(2):
                take(24 + j, fr[:, 24 + j, :], P, j)
            for g, (r0, k) in enumerate(SHG):
                a.wait_ge(sho_turned, 3)
                a.activation(shw[:k, g, :], bank[5][:k, g * P:(g + 1) * P], ACT.Copy).then_inc(sho_sb, 1)
            with a.Fori(0, 8) as i:
                for j in range(4):
                    take(26 + 4 * i + j, fa[:, bass.DynSlice(4 * i + j, 1), :], P, (j + 2) % 4)
            take(58, fa[:80, 32, :], 80, 2)

        @block.vector
        def _(v):
            for g, r in enumerate(PRM_GROUPS):
                v.wait_ge(s_prt, 2)
                v.tensor_copy(prm[:, g, 0:r], bank[5][:, g * P:g * P + r]).then_inc(s_prm, 1)
            v.wait_ge(s_prm, 2)
            dve_n(v)
            d = chain_of(v, shift_ch)
            v.wait_ge(f_read, RWT)
            v.tensor_copy(sho[:, :, :], fr[:, :, SP_ - 1:TOK:8].rearrange("p c i -> p i c")).then_inc(sho_ready, 1)
            v.wait_ge(sho_ready, 1)
            v.wait_ge(ss_turned, 2)
            d(v.tensor_copy(ss[:, :, :], bank[4][:, 0:208].rearrange("p (b c) -> p b c", b=DB)))
            for c0 in (0, 8, 16, 24):
                n = min(8, RWT - c0)
                f, dd = fr[:, c0:c0 + n, :], diff[:, 0:n, :]
                fs_, ds = f[:, :, SP_:].rearrange("p c (b t) -> p c b t", t=T), dd[:, :, SP_:].rearrange("p c (b t) -> p c b t", t=T)
                v.tensor_tensor(dd[:, :, 1:SP_], f[:, :, 0:SP_ - 1], f[:, :, 1:SP_], ALU.subtract)
                v.tensor_scalar(dd[:, :, 0], f[:, :, 0], -1.0, None, ALU.mult)
                v.tensor_tensor(ds[:, :, :, 1:T], fs_[:, :, :, 0:T - 1], fs_[:, :, :, 1:T], ALU.subtract)
                d(v.tensor_tensor(ds[:, :, :, 0], ss[:, :, c0:c0 + n].rearrange("p b c -> p c b"), fs_[:, :, :, 0], ALU.subtract))
                d(v.tensor_tensor(dd, dd, pcol("mu_shift")[:, c0:c0 + n].unsqueeze(2).to_broadcast([P, n, TOK]), ALU.mult))
                d(v.tensor_tensor(f, f, dd, ALU.add))

        @block.tensor
        def _(e):
            e.wait_ge(s_c, 16)
            params_in(e)
            for g, r in enumerate(PRM_GROUPS):
                e.transpose(bank[5][:, g * P:g * P + r], prin[:r, g, :], cw("ident")[:r, :r]).then_inc(s_prt, 1)
            e.wait_ge(s_ss, 32)
            for g in range(2):
                e.transpose(bank[4][:, 104 * g:104 * g + 104], ssin[:, g, :], cw("ident")[:104, :104]).then_inc(ss_turned, 1)
            pe_n(e)
            e.wait_ge(tpr, nt)

            def chunk(buf, landed, n0, widths, b0, first=False):
                e.wait_ge(*((s_w0, 16) if first else (s_w[buf], landed)))
                for j, width in enumerate(widths):
                    if not first:
                        e.wait_ge(f_read, n0 + j - 3)
                    out = bank[(b0 + j) % 4][:width, 0:TOK]
                    for k in range(KT):
                        if first and j == 0 and k == KT // 2:
                            e.wait_ge(s_w[buf], landed)
                        ins = e.matmul(out, w[:, buf, k, j * P:j * P + width], ht[:, k, :], start=(k == 0), stop=(k == KT - 1))
                    ins.then_inc(f_made, 1)
            full = [P] * 4
            chunk(0, 16, 0, full, 0, first=True)
            chunk(1, 16, 4, full, 0)
            with e.Fori(1, n_rw // 2) as i:
                for b in range(2):
                    chunk(b, 16 * i + 16, 8 * i + 4 * b, full, 0)
            chunk(0, 64, 24, [P] * 2, 0)
            e.wait_ge(sho_ready, 1)
            flat = sho[:, :, :].rearrange("p i c -> p (i c)")
            for g, (r0, k) in enumerate(SHG):
                e.transpose(bank[5][:k, g * P:(g + 1) * P], flat[:, r0:r0 + k], cw("ident")).then_inc(sho_turned, 1)
            with e.Fori(0, 4) as i:
                for b in range(2):
                    chunk((b + 1) % 2, (16 * i + 64) if b == 0 else (16 * i + 80), 26 + 8 * i + 4 * b, full, 2)
            chunk(1, 16 * 8, 58, [80], 2)



class HeadSums:

    def __init__(self, heads):
        self.to_heads = lambda j: heads[:, NH * j:NH * j + NH]
        self.to_features = lambda j: heads[0:NH, NH * HP + P * j:NH * HP + P * j + P]


def rwkv_prepare(ph, I, O, C, R):
    nc, pool_dma_sem, sem, bank, cm, cw, pcol, prm, fr = ph
    t1, t2, t3, t4, t5, t6, ar = R["t"]
    with ExitStack() as tmp:
        al = lambda n, s, d=F32: tmp.enter_context(nc.sbuf_tensor(n, s, d))
        w2a2 = al("w2a2", [P, NH * HD])
        g2 = al("g2", [P, NH * HD])
        heads = al("heads", [P, CONSTS["c_heads"].shape[1]])
        nr = al("nr", [NH, TOK])
    hs = HeadSums(heads)
    ns_made, nr_root, nr_ready, nb_made, nb_read = [sem(n) for n in ("norm_sums", "norm_root", "norm_recip", "norm_spread", "norm_spread_read")]
    s_in = sem("lora_in")
    dch = sem("prep_dve_chain")
    squashed, sq_ready, bp_ready, le_ready, bon_done, r_free = [sem(n) for n in (
        "lora_squashed", "kk_squares", "bonus_products", "log_decay_ready", "bonus_done", "r_free")]
    exps = sem("decay_exps")
    z_made, z_read = sem("z_made"), sem("z_read")
    rr, kk, vv = fr[:, 0:8, :], fr[:, 8:16, :], fr[:, 16:24, :]
    bc = lambda name, n=8: pcol(name)[:, 0:n].unsqueeze(2).to_broadcast([P, n, TOK])

    with nc.Block() as block:
        @block.sync
        def _(sp):
            sp.dma_start(w2a2[0:64, :], I["rw_w2"][0]).then_inc(s_in, 16)
            sp.dma_start(w2a2[64:P, :], I["rw_a2"][0]).then_inc(s_in, 16)
            sp.dma_start(g2[:, :], I["rw_g2"][0]).then_inc(s_in, 16)
            sp.dma_start(heads[:, :], C["c_heads"]).then_inc(s_in, 16)

        @block.vector
        def _(v):
            d = chain_of(v, dch)
            d(v.tensor_tensor(t4, kk, bc("rw_kk"), ALU.mult))
            v.tensor_tensor(t3, t4, t4, ALU.mult).then_inc(sq_ready, 1)
            v.wait_ge(nr_root, 1)
            d(v.tensor_scalar(nr[:, :], nr[:, :], 1e-12, None, ALU.max))
            v.reciprocal(nr[:, :], nr[:, :]).then_inc(nr_ready, 1)
            for j in range(HP):
                v.wait_ge(nb_made, j + 1)
                v.tensor_tensor(t4[:, j, :], t4[:, j, :], bank[4 + j % 4][:, 0:TOK], ALU.mult).then_inc(nb_read, 1)
            v.wait_ge(nb_read, HP)
            v.wait_ge(z_read, 16)
            d(v.tensor_scalar(t1, t1, -float(np.exp(-0.5)), None, ALU.mult))
            d(v.tensor_scalar(t5, t2, -1.0, None, ALU.add))
            d(v.tensor_tensor(t5, t5, bc("rw_ka"), ALU.mult))
            d(v.scalar_tensor_tensor(kk, t5, 1.0, kk, ALU.add, ALU.mult))
            d(v.tensor_tensor(t5, rr, kk, ALU.mult))
            v.tensor_tensor(t5, t5, bc("rw_rk"), ALU.mult).then_inc(bp_ready, 1)
            for j in range(HP):
                ins = v.tensor_tensor_scan(t3[:, j, :], cw("scan"), t1[:, j, :], 0.0, ALU.mult, ALU.add)
            d(ins)
            v.tensor_tensor(t1, t3, t1, ALU.subtract).then_inc(le_ready, 1)
            v.wait_ge(z_read, 24)
            v.wait_ge(bp_ready, 1)
            v.tensor_tensor(t5, t6, vv, ALU.mult).then_inc(bon_done, 1)
            v.wait_ge(exps, 3)
            d(v.scalar_tensor_tensor(ar[:, 0, :, :], t4, -1.0, t1, ALU.mult, ALU.mult))
            v.tensor_tensor(ar[:, 1, :, :], rr, t6, ALU.mult).then_inc(r_free, 1)
            d(v.tensor_tensor(t4, t4, t2, ALU.mult))
            d(v.tensor_tensor(t4, t4, t3, ALU.mult))
            d(v.tensor_tensor(kk, kk, t3, ALU.mult))
            for src, dst in ((t4, t1), (kk, t2)):
                for a, b, c in ((0, SP_, CP), (SP_, TOK, CS)):
                    n = (b - a) // c
                    cut = lambda z: z[:, :, a:b].rearrange("p h (n c) -> p h n c", c=c)
                    end = t6[:, :, a + c - 1:b:c].unsqueeze(3).to_broadcast([P, HP, n, c])
                    d(v.tensor_tensor(cut(dst), cut(src), end, ALU.mult))

        @block.scalar
        def _(a):
            a.activation(fr[0:64, 24, :], fr[0:64, 24, :], ACT.Tanh).then_inc(squashed, 1)
            a.activation(fr[:, 25, :], fr[:, 25, :], ACT.Sigmoid).then_inc(squashed, 1)

            def take(n, dst, func, bias=0.0):
                a.wait_ge(z_made, n + 1)
                a.activation(dst, bank[n % 4][:, 0:TOK], func, **({} if func == ACT.Copy else {"bias": bias})).then_inc(z_read, 1)
            for j in range(8):
                take(j, t1[:, j, :], ACT.Sigmoid, pcol("rw_w0")[:, j:j + 1])
            for j in range(8):
                take(8 + j, t2[:, j, :], ACT.Sigmoid, pcol("rw_a0")[:, j:j + 1])
            a.wait_ge(ns_made, 1)
            a.activation(nr[:, :], bank[4][0:NH, 0:TOK], ACT.Sqrt).then_inc(nr_root, 1)
            for j in range(8):
                take(16 + j, t6[:, j, :], ACT.Copy)
            a.wait_ge(le_ready, 1)
            a.activation(t1, t1, ACT.Exp).then_inc(exps, 1)
            a.wait_ge(bon_done, 1)
            a.activation(t6, t3, ACT.Exp).then_inc(exps, 1)
            a.wait_ge(exps, 2)
            a.activation(t3, t3, ACT.Exp, scale=-1.0).then_inc(exps, 1)
            for j in range(8):
                take(24 + j, fr[:, j, :], ACT.Copy)

        @block.tensor
        def _(e):
            e.wait_ge(s_in, 64)
            e.wait_ge(squashed, 2)
            n = 0
            for kind in ("decay", "iclr", "norm", "bonus", "gate"):
                if kind == "norm":
                    e.wait_ge(sq_ready, 1)
                    for j in range(HP):
                        ins = e.matmul(bank[4][0:NH, 0:TOK], hs.to_heads(j), t3[:, j, :], start=(j == 0), stop=(j == HP - 1))
                    ins.then_inc(ns_made, 1)
                    e.wait_ge(nr_ready, 1)
                    for j in range(HP):
                        if j >= 4:
                            e.wait_ge(nb_read, j - 3)
                        e.matmul(bank[4 + j % 4][:, 0:TOK], hs.to_features(j), nr[:, :], start=True, stop=True).then_inc(nb_made, 1)
                    continue
                if kind == "bonus":
                    e.wait_ge(bp_ready, 1)
                if kind == "gate":
                    e.wait_ge(r_free, 1)
                for j in range(8):
                    c = slice(j * P, (j + 1) * P)
                    lhs, rhs = {"decay": (w2a2[0:64, c], fr[0:64, 24, :]), "iclr": (w2a2[64:P, c], fr[64:P, 24, :]),
                                "bonus": (cw("bones"), t5[:, j, :]),
                                "gate": (g2[:, c], fr[:, 25, :])}[kind]
                    if n >= 4:
                        e.wait_ge(z_read, n - 3)
                    e.matmul(bank[n % 4][:, 0:TOK], lhs, rhs, start=True, stop=True).then_inc(z_made, 1)
                    n += 1


def rwkv_core(ph, I, O, R):
    nc, pool_dma_sem, sem, bank, cm, cw, pcol, prm, fr = ph
    t1, t2, t3, t4, t5, t6, ar = R["t"]
    yt = t3
    kk, vv = fr[:, 8:16, :], fr[:, 16:24, :]
    with ExitStack() as tmp:
        al = lambda n, s, d=F32: tmp.enter_context(nc.sbuf_tensor(n, s, d))
        mts = al("mt", [P, 2, 4, 8, HD])
        nns = al("nn", [P, 2, 4, 8, HD])
        qys = al("qy", [P, 2, 2, 4, P])
        tm = al("tm", [P, 2, 4, P])
        ab = al("ab", [P, 4, 2, P])
        ak = al("ak", [P, 4, 2, P])
        a1 = al("a1", [P, 4, P])
        pw = al("pw", [P, 2, 2, 4, P])
        xx = al("xx", [P, 4, P])
        bx = al("bx", [P, 2, 8, P])
        vx = al("vx", [P, 2, 8, P])
        wx = al("wx", [P, 4, 8, HD])
        sta = al("sta", [P, 4, HD])
        ends = al("ends", [P, HP, 24])
    t6f = t6.rearrange("p a b -> p (a b)")
    si = t6f[0:HD, 0:16 * HD].rearrange("p (s h j) -> p s h j", s=2, h=8)
    so = t6f[0:HD, 16 * HD:32 * HD].rearrange("p (s a x) -> p s a x", s=2, a=4)
    stb = t6f[:, 32 * HD:36 * HD].rearrange("p (a i) -> p a i", a=4)
    stt = t6f[:, 36 * HD:40 * HD].rearrange("p (a i) -> p a i", a=4)
    ends_ready = sem("ends_ready")
    tm_made, tm_read, ab_made, ab_read = sem("tm_made"), sem("tm_read"), sem("ab_made"), sem("ab_read")
    akv_made, x_begun, xm_made, x_added = sem("akv_made"), sem("x_begun"), sem("xm_made"), sem("x_added")
    sq_made, sq_read, bv_spread, w_spread = sem("sq_made"), sem("sq_read"), sem("bv_spread"), sem("w_spread")
    map_made, map_read, add_read, qy_read = sem("map_made"), sem("map_read"), sem("add_read"), sem("qy_read")
    qy_made, add_made = sem("qy_made"), sem("add_made")
    st_ready, ser_made, y_read, si_turned = sem("state_ready"), sem("step_made"), sem("y_read"), sem("si_turned")
    si_in = [sem("si_in0"), sem("si_in1")]
    so_turned, so_read = sem("so_turned"), sem("so_read")
    so_out = [pool_dma_sem(f"so_out{i}") for i in range(2)]
    cch = sem("core_dve_chain")
    nit = 4
    E = 8
    MAPB, ADDB = (2, 3), (4, 5)
    QYB, CHB = 6, 7
    SQB = [(2, 3), (4, 5), (6,)]
    ident = cw("ident")
    GROUPS = [(hg, ti) for hg in range(2) for ti in (2, 0, 1)]
    NGR = len(GROUPS)
    EXPORTS = [(hg, b) for hg in range(2) for b in list(range(DB)) + [None]]

    def quads():
        for gi, (hg, ti) in enumerate(GROUPS):
            t0, m = TILES[ti]
            for q in range(2):
                yield 2 * gi + q, gi, hg, ti, t0, m, q, 4 * hg + 2 * q

    def parts(gi, place):
        if gi == 0:
            return
        hg, ti = GROUPS[gi - 1]
        c, odd = divmod(place, 2)
        if ti == 2:
            if odd:
                yield "step", gi - 1, c
            else:
                if c:
                    yield "export", gi - 1, c - 1
                yield "load", gi - 1, c
        elif odd:
            yield "step", gi - 1, c
        if place == 15 and ti:
            yield "export", gi - 1, c

    with nc.Block() as block:
        @block.sync
        def _(sp):
            n = 0
            sp.wait_ge(ends_ready, 2)
            for hg in range(2):
                for b in range(DB):
                    if n >= 2:
                        sp.wait_ge(si_turned, n - 1)
                    sp.dma_start(si[:, n % 2, :, :], I["state_wkv"][0, b, 8 * hg:8 * hg + 8].rearrange("h i j -> i h j")).then_inc(si_in[n % 2], 16)
                    n += 1

        @block.gpsimd
        def _(g):
            n = [0]

            def send(gi, places):
                for place in places:
                    for part, cg, c in parts(gi, place):
                        if part != "export":
                            continue
                        hg, b = EXPORTS[n[0]]
                        n[0] += 1
                        g.wait_ge(so_read, n[0])
                        dst = (O["wkv_p"][0, 0] if b is None else O["wkv_s"][0, b])[8 * hg:8 * hg + 8]
                        g.dma_start(dst.rearrange("h i j -> i h j"), so[:, (n[0] - 1) % 2, :, :].rearrange("i a (p j) -> i (a p) j", p=2)).then_inc(so_out[(n[0] - 1) % 2], 16)
            for k, gi, hg, ti, t0, m, q, hp in quads():
                em = cw("em16" if ti < 2 else "em8")[:m, 0:E].unsqueeze(2)
                g.wait_ge(tm_read, 2 * k + 2)
                if k:
                    g.wait_ge(add_made, k)
                for dst, col in ((bx, 1), (vx, 3)):
                    for p_ in range(2):
                        g.tensor_tensor(dst[:m, p_, 0:E, :], tm[:m, p_, col, :].unsqueeze(1).to_broadcast([m, E, P]),
                                        em.to_broadcast([m, E, P]), ALU.mult).then_inc(bv_spread, 1)
                send(gi, range(8 * q, 8 * q + 8))
            send(NGR, range(16))
            for i in range(2):
                g.wait_ge(so_out[i], 16 * (len(EXPORTS) // 2))

        @block.scalar
        def _(a):
            ns = 0
            n = [0]

            def chain(gi, place):
                for part, cg, c in parts(gi, place):
                    if part == "export":
                        a.wait_ge(so_turned, n[0] + 1)
                        if n[0] >= 2:
                            a.wait_ge(so_out[n[0] % 2], 16 * (n[0] // 2))
                        a.activation(so[:, n[0] % 2, :, :], bank[CHB][:HD, :].rearrange("i (a x) -> i a x", a=4), ACT.Copy).then_inc(so_read, 1)
                        n[0] += 1
            for k, gi, hg, ti, t0, m, q, hp in quads():
                for p_ in range(2):
                    a.wait_ge(tm_made, 2 * k + p_ + 1)
                    if k:
                        a.wait_ge(qy_made, k)
                    a.activation(tm[:m, p_, :, :], bank[p_][:m, :].rearrange("t (c x) -> t c x", c=4), ACT.Copy).then_inc(tm_read, 1)
                a.wait_ge(tm_read, 2 * k + 2)
                a.activation(xx[:m, :, 0:HD], tm[:m, :, 0, :].rearrange("t a (p j) -> t a p j", p=2), ACT.Copy).then_inc(x_begun, 1)
                chain(gi, 8 * q)
                a.wait_ge(akv_made, k + 1)
                a.activation(xx[:m, :, HD:P], bank[0][:m, 0:4 * HD].rearrange("t (h j) -> t h j", h=4), ACT.Copy).then_inc(x_begun, 1)
                for it in range(nit - 1):
                    chain(gi, 8 * q + it + 1)
                    for half in range(2 if it < nit - 2 else 1):
                        a.wait_ge(sq_made, ns + 1)
                        a.activation(pw[:m, it % 2, half, :, 0:m], bank[SQB[it][half]][:m, 0:4 * m].rearrange("t (h s) -> t h s", h=4),
                                     ACT.Copy).then_inc(sq_read, 1)
                        ns += 1
                for place in (4, 5):
                    chain(gi, 8 * q + place)
                a.wait_ge(map_made, k + 1)
                for p_ in range(2):
                    ins = a.activation(mts[:, gi % 2, 2 * q + p_, :, :], bank[MAPB[p_]][:, :].rearrange("p (c j) -> p c j", c=E), ACT.Copy)
                ins.then_inc(map_read, 1)
                for place in (6, 7):
                    chain(gi, 8 * q + place)
            for place in range(16):
                chain(NGR, place)

        @block.vector
        def _(v):
            d = chain_of(v, cch)
            n = {"step": 0, "ready": 0, "load": 0, "export": 0}
            v.tensor_copy(ends[:, :, 0:SP_ // CP], t6[:, :, CP - 1:SP_:CP]).then_inc(ends_ready, 1)
            v.tensor_copy(ends[:, :, SP_ // CP:], t6[:, :, SP_ + CS - 1::CS]).then_inc(ends_ready, 1)
            v.wait_ge(ends_ready, 2)

            def chain(gi, place):
                for part, cg, c in parts(gi, place):
                    hg, ti = GROUPS[cg]
                    t0, _ = TILES[ti]
                    C = CP if ti < 2 else CS
                    buf = cg % 2
                    if part == "export":
                        n["export"] += 1
                        continue
                    if part == "load" or (ti == 0 and c == 0):
                        if n["export"]:
                            v.wait_ge(so_turned, n["export"])
                        if part == "load":
                            n["load"] += 1
                            v.wait_ge(si_turned, n["load"])
                            v.tensor_copy(sta[:, :, :], bank[CHB][:, 4 * CP:4 * CP + 4 * HD].rearrange("p (a i) -> p a i", a=4)).then_inc(st_ready, 1)
                        else:
                            v.memset(sta[:, :, :], 0.0).then_inc(st_ready, 1)
                        n["ready"] += 1
                        v.wait_ge(st_ready, n["ready"])
                    if part == "load":
                        continue
                    end = ends[:, 4 * hg:4 * hg + 4, t0 // CP + c].unsqueeze(2).to_broadcast([P, 4, HD])
                    d(v.tensor_tensor(stt[:, :, :], sta[:, :, :], end, ALU.mult))
                    d(v.tensor_tensor(stt[:, :, :], stt[:, :, :], nns[:, buf, :, c, :], ALU.add))
                    n["step"] += 1
                    v.wait_ge(ser_made, n["step"])
                    dst = sta if ti < 2 else stb
                    if ti == 2 and n["export"]:
                        v.wait_ge(so_turned, n["export"])
                    v.tensor_tensor(dst[:, :, :], stt[:, :, :], bank[CHB][:, 4 * CP:4 * CP + 4 * HD].rearrange("p (a i) -> p a i", a=4), ALU.add).then_inc(st_ready, 1)
                    v.tensor_tensor(yt[:, 4 * hg:4 * hg + 4, t0 + C * c:t0 + C * (c + 1)],
                                    bank[CHB][:, 0:4 * C].rearrange("p (a t) -> p a t", a=4),
                                    qys[:, buf, 1, :, C * c:C * (c + 1)], ALU.add).then_inc(y_read, 1)
                    n["ready"] += 1
                    v.wait_ge(st_ready, n["ready"])
            for k, gi, hg, ti, t0, m, q, hp in quads():
                two = cw("ab16" if ti < 2 else "ab8")[:m, :].rearrange("s (a t) -> s a t", a=2)
                low = cw("lo16" if ti < 2 else "lo8")[:m, :]
                for i in range(4):
                    v.wait_ge(ab_made, 6 * k + i + 1)
                    dst = (ab, ak)[i // 2]
                    v.tensor_tensor(dst[:m, i % 2::2, :, 0:m],
                                    bank[2 + i][:m, 0:4 * m].rearrange("s (h a t) -> s h a t", h=2, a=2),
                                    two.unsqueeze(1).to_broadcast([m, 2, 2, m]), ALU.mult).then_inc(ab_read, 1)
                for i in range(2):
                    v.wait_ge(ab_made, 6 * k + 5 + i)
                    v.tensor_tensor(a1[:m, i::2, 0:m], bank[(6, 1)[i]][:m, 0:2 * m].rearrange("s (h t) -> s h t", h=2),
                                    low.unsqueeze(1).to_broadcast([m, 2, m]), ALU.mult).then_inc(ab_read, 1)
                chain(gi, 8 * q)
                v.wait_ge(x_begun, 2 * k + 2)
                for it in range(nit):
                    v.wait_ge(xm_made, 4 * k + it + 1)
                    v.tensor_tensor(xx[:m, :, :], xx[:m, :, :], bank[it % 2][:m, :].rearrange("t (h x) -> t h x", h=4), ALU.add).then_inc(x_added, 1)
                    chain(gi, 8 * q + it + 1)
                    v.wait_ge(x_added, 4 * k + it + 1)
                em = cw("em16" if ti < 2 else "em8")[:m, 0:E].unsqueeze(2).to_broadcast([m, E, HD])
                for h in range(4):
                    v.tensor_tensor(wx[:m, h, 0:E, :], xx[:m, h, HD:P].unsqueeze(1).to_broadcast([m, E, HD]), em, ALU.mult).then_inc(w_spread, 1)
                chain(gi, 8 * q + 5)
                v.wait_ge(add_made, k + 1)
                for p_ in range(2):
                    ins = v.tensor_copy(nns[:, gi % 2, 2 * q + p_, :, :], bank[ADDB[p_]][:, :].rearrange("p (c j) -> p c j", c=E))
                ins.then_inc(add_read, 1)
                chain(gi, 8 * q + 6)
                v.wait_ge(qy_made, k + 1)
                v.tensor_tensor(qys[:, gi % 2, 0, 2 * q:2 * q + 2, 0:m], bank[QYB][:, 0:2 * m].rearrange("p (a t) -> p a t", a=2),
                                ar[:, 1, hp:hp + 2, t0:t0 + m], ALU.add).then_inc(qy_read, 1)
                v.tensor_copy(qys[:, gi % 2, 1, 2 * q:2 * q + 2, 0:m], bank[QYB][:, 2 * m:4 * m].rearrange("p (a t) -> p a t", a=2)).then_inc(qy_read, 1)
                chain(gi, 8 * q + 7)
                v.wait_ge(add_read, k + 1)
                v.wait_ge(qy_read, 2 * k + 2)
            for place in range(16):
                chain(NGR, place)

        @block.tensor
        def _(e):
            n = {"step": 0, "ready": 0, "load": 0, "export": 0}
            half = lambda z, h: z[HD * (h % 2):HD * (h % 2) + HD]

            def chain(gi, place):
                for part, cg, c in parts(gi, place):
                    hg, ti = GROUPS[cg]
                    C = CP if ti < 2 else CS
                    buf = cg % 2
                    if part == "step" and ti == 0 and c == 0:
                        n["ready"] += 1
                    if part == "step" and c == 0:
                        e.wait_ge(map_read, 2 * cg + 2)
                        e.wait_ge(qy_read, 4 * cg + 4)
                    if n["ready"]:
                        e.wait_ge(st_ready, n["ready"])
                    if n["step"]:
                        e.wait_ge(y_read, n["step"])
                    if n["export"]:
                        e.wait_ge(so_read, n["export"])
                    if part == "load":
                        nb = n["load"]
                        e.wait_ge(si_in[nb % 2], 16 * (nb // 2 + 1))
                        for p_ in range(4):
                            ins = e.transpose(bank[CHB][:, 4 * CP + p_ * HD:4 * CP + (p_ + 1) * HD],
                                              si[:, nb % 2, 2 * p_:2 * p_ + 2, :].rearrange("i h j -> i (h j)"), ident[:HD, :HD])
                        ins.then_inc(si_turned, 1)
                        n["load"] += 1
                        n["ready"] += 1
                    elif part == "step":
                        for p_ in range(4):
                            for h in (0, 1):
                                e.matmul(half(bank[CHB][:, 4 * CP + p_ * HD:4 * CP + (p_ + 1) * HD], h), half(mts[:, buf, p_, c, :], h),
                                         half(sta[:, p_, :], h), start=True, stop=True)
                        for p_ in range(4):
                            for h in (0, 1):
                                ins = e.matmul(half(bank[CHB][:, p_ * C:(p_ + 1) * C], h), half(sta[:, p_, :], h),
                                               half(qys[:, buf, 0, p_, C * c:C * (c + 1)], h), start=True, stop=True)
                        ins.then_inc(ser_made, 1)
                        n["step"] += 1
                        n["ready"] += 1
                    else:
                        src = stb if ti == 2 else sta
                        for p_ in range(4):
                            ins = e.transpose(bank[CHB][:HD, p_ * P:(p_ + 1) * P], src[:, p_, :], ident)
                        ins.then_inc(so_turned, 1)
                        n["export"] += 1
            for k, gi, hg, ti, t0, m, q, hp in quads():
                tok = slice(t0, t0 + m)
                for p_ in range(2):
                    for i, src in enumerate((ar[:, 0], t1, t2, vv)):
                        ins = e.transpose(bank[p_][:m, i * P:(i + 1) * P], src[:, hp + p_, tok], ident)
                    ins.then_inc(tm_made, 1)
                if k:
                    e.wait_ge(map_read, k)
                    e.wait_ge(add_read, k)
                for i, src in enumerate((t4, kk)):
                    for h in range(4):
                        ins = e.matmul(bank[2 + 2 * i + h % 2][:m, (h // 2) * 2 * m:(h // 2 + 1) * 2 * m], half(src[:, hp + h // 2, tok], h),
                                       half(ar[:, :, hp + h // 2, tok], h), start=True, stop=True)
                        if h >= 2:
                            ins.then_inc(ab_made, 1)
                if k:
                    e.wait_ge(qy_read, 2 * k)
                e.wait_ge(tm_read, 2 * k + 2)
                for h in range(4):
                    ins = e.matmul(bank[(6, 1)[h % 2]][:m, (h // 2) * m:(h // 2 + 1) * m], half(ar[:, 0, hp + h // 2, tok], h), half(t4[:, hp + h // 2, tok], h),
                                   start=True, stop=True)
                    if h >= 2:
                        ins.then_inc(ab_made, 1)
                chain(gi, 8 * q)
                vh = lambda h: tm[:m, h // 2, 3, HD * (h % 2):HD * (h % 2) + HD]
                e.wait_ge(ab_read, 6 * k + 4)
                for h in range(4):
                    ins = e.matmul(bank[0][:m, h * HD:(h + 1) * HD], ak[:m, h, 0, 0:m], vh(h), start=True, stop=True)
                ins.then_inc(akv_made, 1)
                e.wait_ge(ab_read, 6 * k + 6)
                e.wait_ge(x_begun, 2 * k + 2)
                for it in range(nit):
                    if it:
                        e.wait_ge(x_added, 4 * k + it)
                        e.wait_ge(sq_read, 5 * k + (2, 4, 5)[it - 1])
                    up = (lambda h: ab[:m, h, 0, 0:m]) if it == 0 else (lambda h: pw[:m, (it - 1) % 2, 0, h, 0:m])
                    lo = (lambda h: a1[:m, h, 0:m]) if it == 0 else (lambda h: pw[:m, (it - 1) % 2, 1, h, 0:m])
                    for h in range(4):
                        ins = e.matmul(bank[it % 2][:m, h * P:(h + 1) * P], up(h), xx[:m, h, :], start=True, stop=True)
                    ins.then_inc(xm_made, 1)
                    if it < nit - 1:
                        for h in range(4):
                            ins = e.matmul(bank[SQB[it][0]][:m, h * m:(h + 1) * m], lo(h), up(h), start=True, stop=True)
                        ins.then_inc(sq_made, 1)
                    if it < nit - 2:
                        for h in range(4):
                            ins = e.matmul(bank[SQB[it][1]][:m, h * m:(h + 1) * m], up(h), lo(h), start=True, stop=True)
                        ins.then_inc(sq_made, 1)
                    chain(gi, 8 * q + it + 1)
                e.wait_ge(x_added, 4 * k + 4)
                e.wait_ge(bv_spread, 4 * k + 4)
                cols = lambda h: slice(HD * (h % 2), HD * (h % 2) + HD)
                for h in range(4):
                    ins = e.matmul(half(bank[MAPB[h // 2]][:, :], h), xx[:m, h, 0:HD], bx[:m, h // 2, :, cols(h)], start=True, stop=True)
                ins.then_inc(map_made, 1)
                chain(gi, 8 * q + 5)
                e.wait_ge(w_spread, 4 * k + 4)
                for p_ in range(2):
                    for i in range(2):
                        for h in (2 * p_, 2 * p_ + 1):
                            ins = e.matmul(half(bank[ADDB[p_]][:, :], h), tm[:m, p_, 1 + i, cols(h)],
                                           (wx[:m, h, :, :], vx[:m, p_, :, cols(h)])[i], start=(i == 0), stop=(i == 1))
                ins.then_inc(add_made, 1)
                chain(gi, 8 * q + 6)
                for h0 in (0, 2):
                    for i in range(3):
                        for h in (h0, h0 + 1):
                            out = half(bank[QYB][:, (2 * (i > 0) + h // 2) * m:(2 * (i > 0) + h // 2 + 1) * m], h)
                            lhs, rhs = ((xx[:m, h, 0:HD], ab), (xx[:m, h, HD:P], ab), (vh(h), ak))[i]
                            ins = e.matmul(out, lhs, rhs[:m, h, 1, 0:m], start=(i < 2), stop=(i != 1))
                ins.then_inc(qy_made, 1)
                chain(gi, 8 * q + 7)
            for place in range(16):
                chain(NGR, place)


def rwkv_finish(ph, I, O, C, R):
    nc, pool_dma_sem, sem, bank, cm, cw, pcol, prm, fr = ph
    t1, t2, t3, t4, t5, t6, ar = R["t"]
    s_made, s_read, sq, fch, fdone = sem("gn_sums"), sem("gn_read"), sem("gn_squares"), sem("gn_chain"), sem("gn_sqrt")
    s_c, nb_made, nb_read = sem("gn_consts_in"), sem("gn_spread"), sem("gn_spread_read")
    epsb = R["al"]("gneps", [P, 1])
    heads = R["al"]("gnheads", [P, CONSTS["c_heads"].shape[1]])
    hs = HeadSums(heads)
    nr = R["al"]("gnroot", [NH, TOK])
    bc = lambda name: pcol(name)[:, 0:8].unsqueeze(2).to_broadcast([P, 8, TOK])
    with nc.Block() as block:
        @block.sync
        def _(sp):
            sp.dma_start(heads[:, :], C["c_heads"]).then_inc(s_c, 16)

        @block.tensor
        def _(e):
            for j in range(8):
                if j >= 4:
                    e.wait_ge(s_read, j - 3)
                e.matmul(bank[j % 4][:, 0:TOK], cw("bones"), t3[:, j, :], start=True, stop=True).then_inc(s_made, 1)
            e.wait_ge(sq, 1)
            e.wait_ge(s_c, 16)
            for j in range(8):
                ins = e.matmul(bank[4][0:NH, 0:TOK], hs.to_heads(j), t1[:, j, :], start=(j == 0), stop=(j == 7))
            ins.then_inc(s_made, 1)
            e.wait_ge(sq, 2)
            for j in range(8):
                if j >= 4:
                    e.wait_ge(nb_read, j - 3)
                e.matmul(bank[4 + j % 4][:, 0:TOK], hs.to_features(j), nr[:, :], start=True, stop=True).then_inc(nb_made, 1)

        @block.scalar
        def _(a):
            for n in range(8):
                a.wait_ge(s_made, n + 1)
                a.activation(t2[:, n, :], bank[n % 4][:, 0:TOK], ACT.Copy, scale=-1.0 / HD).then_inc(s_read, 1)
            a.wait_ge(fdone, 1)
            a.wait_ge(s_made, 9)
            a.activation(nr[:, :], bank[4][0:NH, 0:TOK], ACT.Sqrt, scale=1.0 / HD, bias=epsb[0:NH, 0:1]).then_inc(s_read, 1)

        @block.vector
        def _(v):
            d = chain_of(v, fch)
            v.memset(epsb[:, :], GN_EPS).then_inc(fdone, 1)
            v.wait_ge(s_read, 8)
            d(v.tensor_tensor(t3, t3, t2, ALU.add))
            v.tensor_tensor(t1, t3, t3, ALU.mult).then_inc(sq, 1)
            d(v.tensor_tensor(t3, t3, bc("rw_ln_g"), ALU.mult))
            v.wait_ge(s_read, 9)
            v.reciprocal(nr[:, :], nr[:, :]).then_inc(sq, 1)
            for j in range(8):
                v.wait_ge(nb_made, j + 1)
                v.tensor_tensor(t3[:, j, :], t3[:, j, :], bank[4 + j % 4][:, 0:TOK], ALU.mult).then_inc(nb_read, 1)
            v.wait_ge(nb_read, 8)
            d(v.tensor_tensor(t3, t3, bc("rw_ln_b"), ALU.add))
            d(v.tensor_tensor(t3, t3, t5, ALU.add))
            d(v.tensor_tensor(fr[:, 0:8, :], fr[:, 0:8, :], t3, ALU.mult))


def dsa_prepare(ph, I, O, C, fat_d, rev_d, tp_d, bs_d, S):
    nc, pool_dma_sem, sem, bank, cm, cw, pcol, prm, fr = ph
    fa, ik2, vt, ikw, nm, cd = S["fa"], S["ik2"], S["vt"], S["ikw"], S["nm"], S["cd"]
    with ExitStack() as tmp:
        al = lambda n, s, d=F32: tmp.enter_context(nc.sbuf_tensor(n, s, d))
        ktok = al("ktok", [P, 3, AT])
        rb = al("rb", [32, NH])
        bk = al("bk", [32, REV])
        rv = al("rv", [NH, REV])
        rl = al("rl", [P, 2, SP_])
        acc = al("acc", [P, 2, SP_])
        wk = al("wk", [P, 2, SP_])
        m8 = al("m8", [P, 8])
        gt = al("gt", [P, SP_])
        eq = al("eq", [P, SP_])
        cum = al("cum", [P, SP_])
        ones = al("ones", [P, SP_])
        need = al("need", [P, 1])
        wsc = al("wsc", [P, 2, NH])
    s_kvf, s_fa, s_c, s_pt = sem("kv_tiles_in"), sem("fa_in"), sem("dsa_consts_in"), sem("page_table_in")
    s_ki = sem("ki_in_sp"), pool_dma_sem("ki_in_pool")
    pti, ki, ci = S["pti"], S["ki"], I["cache_idx_k"][0]
    kt_made, kt_read, s_kv = sem("kv_turned"), sem("kv_read"), sem("kv_out")
    rv_made, rv_read, s_rv = sem("rev_made"), sem("rev_read"), sem("rev_out")
    dot_made, relu_done, acc_done, dch, wt_made = sem("dots_made"), sem("relu_done"), sem("acc_done"), sem("sel_chain"), sem("wt_made")
    groups = []
    for t, (t0, m) in enumerate(TILES):
        groups += [(t, t0, m, 8 + 4 * i, ktok, 4 * i) for i in range(2)] + [(t, t0, m, 16 + 4 * i, vt, 4 * i) for i in range(2)]
        groups.append((t, t0, m, None, ikw, 0))
    NG_ = len(groups)
    units = [(qt, h) for qt in range(2) for h in range(NH)]
    with nc.Block() as block:
        @block.gpsimd
        def _(g):
            g.wait_ge(s_pt, 16)
            for b in range(DB // 2, DB):
                for n in range(NPG):
                    load_page(g, I, pti, ki[:, b, n, :], ci, NPG * b + n).then_inc(s_ki[1], 16)
            g.wait_ge(s_ki[1], 16 * NPG * DB // 2)

        @block.sync
        def _(sp):
            def bias_rows():
                sp.wait_ge(rv_read, 3)
                sp.dma_start(rev_d, rv[:, :]).then_inc(s_rv, 16)
                sp.wait_ge(s_rv, 16)
                sp.dma_start(tp_d, bass.AP(rev_d.tensor, PAST + T - 1 - P, [[REV, NH], [-1, P], [1, 3 * P]])).then_inc(s_rv, 16)
                L = PAST + T - 1
                sp.dma_start(bs_d[:, :, 0:PAST], bass.AP(rev_d.tensor, T - 1, [[REV, NH], [-1, T], [1, PAST]])).then_inc(s_rv, 16)
                for b in range(DB):
                    sp.dma_start(bs_d[:, :, PAST + T * b:PAST + T * b + T], bass.AP(rev_d.tensor, L, [[REV, NH], [-1, T], [1, T]])).then_inc(s_rv, 16)

            sp.dma_start(cd[:, :], C["c_dsa"]).then_inc(s_c, 16)
            sp.dma_start(bk[:, :], C["c_bkt"]).then_inc(s_c, 16)
            sp.dma_start(rb[:, :], I["rel_bias"]).then_inc(s_c, 16)
            sp.dma_start(fa[:, 8:16, :], fat_d[:, 8:16, :]).then_inc(s_kvf, 16)
            sp.dma_start(fa[:, 16:24, :], fat_d[:, 16:24, :]).then_inc(s_kvf, 16)
            sp.dma_start(fa[0:80, 32, :], fat_d[0:80, 32, :]).then_inc(s_kvf, 16)
            sp.dma_start(fa[:, 24:32, :], fat_d[:, 24:32, :]).then_inc(s_fa, 16)
            sp.dma_start(fa[:, 0:8, :], fat_d[:, 0:8, :]).then_inc(s_fa, 16)
            for i in range(2):
                sp.dma_start(ik2[64 * i:64 * i + 64, :], fat_d[0:64, 32, :]).then_inc(s_fa, 16)
            sp.dma_start(pti[:, :], I["page_table"].rearrange("b n -> (b n)").unsqueeze(0)).then_inc(s_pt, 16)
            sp.wait_ge(s_pt, 16)
            for b in range(DB // 2):
                if b == 1:
                    bias_rows()
                for n in range(NPG):
                    load_page(sp, I, pti, ki[:, b, n, :], ci, NPG * b + n).then_inc(s_ki[0], 16)
            for g, (t, t0, m, c, dst, o) in enumerate(groups):
                if g % 5 == 4:
                    sp.wait_ge(kt_read, g + 1)
                    for src, n, w in ((ktok, "k", AT), (vt, "v", AT), (ikw, "ik", HD)):
                        o_ = O[n + "_p"][0, 0] if t < 2 else O[n + "_s"][0]
                        if n != "ik":
                            o_ = o_.rearrange("s h d -> s (h d)") if t < 2 else o_.rearrange("b s h d -> (b s) (h d)")
                        elif t == 2:
                            o_ = o_.rearrange("b s d -> (b s) d")
                        sp.dma_start(o_[t0 % SP_:t0 % SP_ + m, :], src[:m, t, 0:w]).then_inc(s_kv, 16)
            sp.wait_ge(s_rv, 16 * (3 + DB))
            sp.wait_ge(s_kv, 16 * 9)
            sp.wait_ge(s_ki[0], 16 * NPG * DB // 2)

        @block.tensor
        def _(e):
            e.wait_ge(s_kvf, 48)
            e.wait_ge(s_c, 48)
            for i in range(3):
                e.matmul(bank[5 + i][:NH, :], rb[:, :], bk[:, 512 * i:512 * i + 512], start=True, stop=True).then_inc(rv_made, 1)
            for g, (t, t0, m, c, dst, o) in enumerate(groups):
                if g >= 2:
                    e.wait_ge(kt_read, g - 1)
                if c is None:
                    ins = e.transpose(bank[g % 2][:m, 0:80], fa[:80, 32, t0:t0 + m], cw("ident")[:80, :80])
                else:
                    for i in range(4):
                        ins = e.transpose(bank[g % 2][:m, i * P:(i + 1) * P], fa[:, c + i, t0:t0 + m], cw("ident"))
                ins.then_inc(kt_made, 1)
            e.wait_ge(rv_read, 1)
            e.matmul(bank[5][:, 0:SS], cdw(cd, "reph")[64:80, :], fa[64:80, 32, SP_:], start=True, stop=True).then_inc(wt_made, 1)
            e.wait_ge(kt_read, NG_)
            e.wait_ge(s_fa, 64)
            for n, (qt, h) in enumerate(units):
                nk = P * (qt + 1)
                r = slice(HD * (h % 2), HD * (h % 2) + HD)
                if n >= 4:
                    e.wait_ge(relu_done, n - 3)
                e.matmul(bank[n % 4][:, 0:nk], fa[r, 24 + h // 2, P * qt:P * qt + P], ik2[r, 0:nk], start=True, stop=True).then_inc(dot_made, 1)

        @block.scalar
        def _(a):
            for i in range(3):
                a.wait_ge(rv_made, i + 1)
                a.activation(rv[:, 512 * i:512 * i + 512], bank[5 + i][:NH, :], ACT.Copy).then_inc(rv_read, 1)
            for g, (t, t0, m, c, dst, o) in enumerate(groups):
                a.wait_ge(kt_made, g + 1)
                w = 80 if c is None else 512
                a.activation(dst[:m, t, o * P:o * P + w], bank[g % 2][:m, 0:w], ACT.Copy).then_inc(kt_read, 1)
            for n, (qt, h) in enumerate(units):
                nk = P * (qt + 1)
                a.wait_ge(dot_made, n + 1)
                if n >= 2:
                    a.wait_ge(acc_done, n - 1)
                a.activation(rl[:, n % 2, 0:nk], bank[n % 4][:, 0:nk], ACT.Relu).then_inc(relu_done, 1)

        @block.vector
        def _(v):
            d = chain_of(v, dch)
            d(v.memset(ones[:, :], 1.0))
            for z in (S["iqs"][:, :, :, :, :], S["wts"][:, :], S["qs"][:, :, :]):
                d(v.memset(z, 0.0))
            d(v.memset(acc[:, :, :], 0.0))
            v.wait_ge(s_kvf, 48)
            v.wait_ge(s_fa, 64)
            v.wait_ge(s_c, 48)
            for p_ in range(2):
                r = slice(HD * p_, HD * p_ + HD)
                d(v.tensor_copy(S["iqs"][r, :, :, p_, :], fa[r, 24:32, SP_:].rearrange("p h (b q) -> p b h q", q=T)))
            d(v.tensor_copy(S["qn"][:, :, :], fa[:, 0:8, SP_:]))
            d(v.tensor_copy(S["kn"][:, :, :], fa[:, 8:16, SP_:]))
            v.wait_ge(wt_made, 1)
            d(v.tensor_tensor(S["wts"][:, :].rearrange("p (b x) -> p b x", x=72)[:, :, 0:T], bank[5][:, 0:SS].rearrange("p (b q) -> p b q", q=T),
                              cdw(cd, "dqq").rearrange("p (b q) -> p b q", q=T), ALU.mult))
            v.wait_ge(kt_read, NG_)
            d(v.tensor_scalar(wsc[:, :, :], ikw[:, 0:2, HD:HD + NH], IDXW, None, ALU.mult))
            for n, (qt, h) in enumerate(units):
                nk = P * (qt + 1)
                v.wait_ge(relu_done, n + 1)
                v.scalar_tensor_tensor(acc[:, qt, 0:nk], rl[:, n % 2, 0:nk], wsc[:, qt, h:h + 1], acc[:, qt, 0:nk], ALU.mult, ALU.add).then_inc(acc_done, 1)
                v.wait_ge(acc_done, n + 1)
            for qt in range(2):
                nk = P * (qt + 1)
                cn = cdw(cd, "cn")[:, SP_ * qt:SP_ * qt + nk]
                sc = acc[:, qt, 0:nk]
                d(v.tensor_tensor(sc, sc, cn, ALU.add))
                for r in range(top_turns(TOPK_P)):
                    top_turn(v, d, r, sc, wk, m8, TOPK_P, nk, P)
                top_mask(v, d, sc, m8, gt[:, 0:nk], eq[:, 0:nk], cum[:, 0:nk], ones[:, 0:nk], need, TOPK_P, nm[:, qt, 0:nk], P)
                d(v.tensor_tensor(nm[:, qt, 0:nk], nm[:, qt, 0:nk], cn, ALU.min))


def top_turns(topk):
    return -(-topk // 8)


def top_turn(v, d, r, sc, wk, m8, topk, nk, rows):
    src = sc if r == 0 else wk[:rows, (r - 1) % 2, 0:nk]
    d(v.max(m8[:rows, :], src))
    if r < top_turns(topk) - 1:
        d(v.match_replace(wk[:rows, r % 2, 0:nk], m8[:rows, :], src, NEG * 3))


def top_mask(v, d, sc, m8, gt, eq, cum, ones, need, topk, out, rows):
    last = (topk - 1) % 8
    least = m8[:rows, last:last + 1]
    d(v.tensor_scalar(gt, sc, least, None, ALU.is_gt))
    d(v.tensor_scalar(eq, sc, least, None, ALU.is_equal))
    d(v.tensor_reduce(need[:rows, :], gt, AXX, ALU.add))
    d(v.tensor_scalar(need[:rows, :], need[:rows, :], -1.0, float(topk), ALU.mult, ALU.add))
    d(v.tensor_tensor_scan(cum, ones, eq, 0.0, ALU.mult, ALU.add))
    d(v.scalar_tensor_tensor(eq, cum, need[:rows, :], eq, ALU.is_le, ALU.mult))
    d(v.tensor_tensor(gt, gt, eq, ALU.add))
    if out is not None:
        d(v.tensor_scalar(out, gt, -1.0, -NEG, ALU.add, ALU.mult))


def dsa_prompt(ph, I, O, tp_d, S):
    nc, pool_dma_sem, sem, bank, cm, cw, pcol, prm, fr = ph
    fa, vt, nm = S["fa"], S["vt"], S["nm"]
    with ExitStack() as tmp:
        al = lambda n, s, d=F32: tmp.enter_context(nc.sbuf_tensor(n, s, d))
        bp = al("bp", [P, 2, 2, SP_])
        lg = al("lg", [P, 2, 2, SP_])
        pt = al("pt", [P, 2, 4, P])
        sm = al("sm", [P, 3, 2, 2])
        wk = al("swk", [SS, 2, KEYS])
        m8 = al("sm8", [SS, 8])
        need = al("sneed", [SS, 1])
        gt, eq, cum, ones = [al("s" + n, [SS, KEYS])[:, :] for n in ("gt", "eq", "cum", "ones")]
    sc, nms, cd, pti, kp = S["sc"], S["nms"], S["cd"], S["pti"], S["kp"]
    s_kp = sem("first_keys_in")
    s_bp = [sem("bias_in0"), sem("bias_in1")]
    bm_done, qk_made, lg_done, mx_done, ex_done, rc_done = [sem("p_" + n) for n in ("bm", "qk", "logits", "max", "exp", "recip")]
    nrm, pt_made, pt_read, o_made, o_read, dch = [sem("p_" + n) for n in ("norm", "turned", "taken", "o", "o_read", "chain")]
    units = [(qt, hp) for qt in range(2) for hp in range(HP)]
    def normalize(g, n):
        nk = P * (units[n][0] + 1)
        g.wait_ge(rc_done, n + 1)
        g.tensor_tensor(lg[:, n % 2, :, 0:nk], lg[:, n % 2, :, 0:nk], sm[:, 2, n % 2, :].unsqueeze(2).to_broadcast([P, 2, nk]), ALU.mult).then_inc(nrm, 1)

    def take(a, n):
        qt, hp = units[n]
        a.wait_ge(pt_made, n + 1)
        a.activation(pt[:, n % 2, :, :].rearrange("p (h j) q -> p h j q", h=2)[:, :, 0:qt + 1, :],
                     bank[4 + n % 2][:, :].rearrange("p (h j q) -> p h j q", h=2, j=2)[:, :, 0:qt + 1, :], ACT.Copy).then_inc(pt_read, 1)
        a.wait_ge(o_made, n + 1)
        a.activation(fr[:, 8 + hp, P * qt:P * qt + P], bank[6 + n % 2][:, 0:P], ACT.Copy).then_inc(o_read, 1)

    with nc.Block() as block:
        @block.sync
        def _(sp):
            for n, (qt, hp) in enumerate(units):
                nk = P * (qt + 1)
                if n >= 2:
                    sp.wait_ge(lg_done, 2 * (n - 1))
                src = tp_d[2 * hp:2 * hp + 2, :, P * (1 - qt):P * (1 - qt) + nk].rearrange("h p s -> p h s")
                sp.dma_start(bp[:, n % 2, :, 0:nk], src).then_inc(s_bp[n % 2], 16)
                if n % 2:
                    load_page(sp, I, pti, kp[:, n // 2, :], I["cache_k"][0].rearrange("n p h d -> n p (h d)"), n // 2).then_inc(s_kp, 16)
            sp.wait_ge(s_kp, 16 * NPG)

        @block.gpsimd
        def _(g):
            for n, (qt, hp) in enumerate(units):
                nk = P * (qt + 1)
                g.wait_ge(s_bp[n % 2], 16 * (n // 2 + 1))
                g.tensor_tensor(bp[:, n % 2, :, 0:nk], bp[:, n % 2, :, 0:nk], nm[:, qt, 0:nk].unsqueeze(1).to_broadcast([P, 2, nk]), ALU.add).then_inc(bm_done, 1)
                if n:
                    normalize(g, n - 1)
            normalize(g, len(units) - 1)

        @block.tensor
        def _(e):
            def qk(n):
                qt, hp = units[n]
                nk = P * (qt + 1)
                if n >= 2:
                    e.wait_ge(lg_done, 2 * (n - 1))
                for p_ in range(2):
                    r = slice(HD * p_, HD * p_ + HD)
                    e.matmul(bank[2 * (n % 2) + p_][:, 0:nk], fa[r, hp, P * qt:P * qt + P], fa[r, 8 + hp, 0:nk], start=True, stop=True).then_inc(qk_made, 1)
            qk(0)
            for n, (qt, hp) in enumerate(units):
                if n + 1 < len(units):
                    qk(n + 1)
                e.wait_ge(nrm, n + 1)
                if n >= 2:
                    e.wait_ge(pt_read, n - 1)
                for p_ in range(2):
                    for j in range(qt + 1):
                        ins = e.transpose(bank[4 + n % 2][:, (2 * p_ + j) * P:(2 * p_ + j + 1) * P], lg[:, n % 2, p_, j * P:(j + 1) * P], cw("ident"))
                ins.then_inc(pt_made, 1)
                e.wait_ge(pt_read, n + 1)
                if n >= 2:
                    e.wait_ge(o_read, n - 1)
                for p_ in range(2):
                    for j in range(qt + 1):
                        ins = e.matmul(bank[6 + n % 2][HD * p_:HD * p_ + HD, 0:P], vt[:, j, hp * P + HD * p_:hp * P + HD * p_ + HD],
                                       pt[:, n % 2, 2 * p_ + j, :], start=(j == 0), stop=(j == qt))
                ins.then_inc(o_made, 1)

        @block.scalar
        def _(a):
            for n, (qt, hp) in enumerate(units):
                nk = P * (qt + 1)
                a.wait_ge(mx_done, n + 1)
                for p_ in range(2):
                    a.activation(lg[:, n % 2, p_, 0:nk], lg[:, n % 2, p_, 0:nk], ACT.Exp, bias=sm[:, 0, n % 2, p_:p_ + 1],
                                 accum_out=sm[:, 1, n % 2, p_:p_ + 1]).then_inc(ex_done, 1)
                if n:
                    take(a, n - 1)
            take(a, len(units) - 1)

        @block.vector
        def _(v):
            d = chain_of(v, dch)
            turns_per_unit = top_turns(TOPK_S) // len(units)

            def select(n, half):
                for r in range(turns_per_unit * n + half, turns_per_unit * (n + 1), 2):
                    top_turn(v, d, r, sc[:, :], wk, m8, TOPK_S, KEYS, SS)
            d(v.memset(ones, 1.0))
            for n, (qt, hp) in enumerate(units):
                nk = P * (qt + 1)
                v.wait_ge(bm_done, n + 1)
                if n >= 2:
                    v.wait_ge(pt_made, n - 1)
                for p_ in range(2):
                    v.wait_ge(qk_made, 2 * n + p_ + 1)
                    v.scalar_tensor_tensor(lg[:, n % 2, p_, 0:nk], bank[2 * (n % 2) + p_][:, 0:nk], HD ** -0.5, bp[:, n % 2, p_, 0:nk],
                                           ALU.mult, ALU.add).then_inc(lg_done, 1)
                v.wait_ge(lg_done, 2 * n + 2)
                v.tensor_reduce(sm[:, 0, n % 2, :], lg[:, n % 2, :, 0:nk], AXX, ALU.max, negate=True).then_inc(mx_done, 1)
                select(n, 0)
                v.wait_ge(ex_done, 2 * n + 2)
                v.reciprocal(sm[:, 2, n % 2, :], sm[:, 1, n % 2, :]).then_inc(rc_done, 1)
                select(n, 1)
            top_mask(v, d, sc[:, :], m8, gt, eq, cum, ones, need, TOPK_S, nms[:, :], SS)
            d(v.tensor_tensor(nms[:, PAST:], nms[:, PAST:], cdw(cd, "cns")[0:SS, :], ALU.min))


def load_page(sp, I, pti, dst, src, i):
    page = sp.value_load(pti[0:1, i:i + 1], min_val=0, max_val=I["cache_k"].shape[1] - 1)
    return sp.dma_start(dst, src[bass.DynSlice(page, 1), :, :].squeeze(0))


KEY_COLS = [(0, 512), (512, 1024), (1024, KEYS)]


def sample_scores(ph, I, S):
    nc, pool_dma_sem, sem, bank, cm, cw, pcol, prm, fr = ph
    ik2, cd, iqs, wts, sc, ki = [S[n] for n in ("ik2", "cd", "iqs", "wts", "sc", "ki")]
    with ExitStack() as tmp:
        al = lambda n, s, d=F32: tmp.enter_context(nc.sbuf_tensor(n, s, d))
        kd = al("kd", [P, 2, NPG, 2, HD])
        kit = al("kit", [P, 2, 512])
        rl = al("srl", [P, KEYS])
    kd_done, kit_made, kit_read, dot_made, relu_done, sc_made, sc_read = [sem("s_" + n) for n in (
        "dup", "ki_turned", "ki_taken", "dots", "relu", "scores", "scores_read")]
    cols = KEY_COLS
    with nc.Block() as block:
        @block.scalar
        def _(a):
            def take(b):
                for i in range(2):
                    a.wait_ge(kit_made, 2 * b + i + 1)
                    if b:
                        a.wait_ge(dot_made, 3 * (b - 1) + i + 1)
                    a.activation(kit[:, i, :], bank[i][:, :], ACT.Copy).then_inc(kit_read, 1)
            take(0)
            for b in range(DB):
                for i, (c0, c1) in enumerate(cols):
                    a.wait_ge(dot_made, 3 * b + i + 1)
                    if b:
                        a.wait_ge(sc_made, b)
                    a.activation(rl[:, c0:c1], bank[2 + i][:, 0:c1 - c0], ACT.Relu).then_inc(relu_done, 1)
                if b + 1 < DB:
                    take(b + 1)

        @block.tensor
        def _(e):
            def turn(b):
                e.wait_ge(kd_done, b + 1)
                for i in range(2):
                    if b:
                        e.wait_ge(kit_read, 2 * (b - 1) + i + 1)
                    for n in range(4):
                        ins = e.transpose(bank[i][:, n * P:(n + 1) * P], kd[:, b % 2, 4 * i + n, :, :].rearrange("p a d -> p (a d)"), cw("ident"))
                    ins.then_inc(kit_made, 1)

            def weigh(b):
                for i, (c0, c1) in enumerate(cols):
                    e.wait_ge(relu_done, 3 * b + i + 1)
                    ins = e.matmul(bank[5 + i][:SS, 0:c1 - c0], wts[:, SS * b:SS * b + SS], rl[:, c0:c1], start=(b == 0), stop=(b == DB - 1))
                ins.then_inc(sc_made, 1)
            turn(0)
            for b in range(DB):
                if b + 1 < DB:
                    turn(b + 1)
                for i, (c0, c1) in enumerate(cols):
                    if i < 2:
                        e.wait_ge(kit_read, 2 * b + i + 1)
                    if b:
                        e.wait_ge(relu_done, 3 * (b - 1) + i + 1)
                    rhs = kit[:, i, :] if i < 2 else ik2[:, SP_:]
                    e.matmul(bank[2 + i][:, 0:c1 - c0], iqs[:, b, :, :, :].rearrange("p h a q -> p (h a q)"), rhs, start=True, stop=True).then_inc(dot_made, 1)
                weigh(b)

        @block.vector
        def _(v):
            for b in range(DB):
                if b >= 2:
                    v.wait_ge(kit_made, 2 * (b - 1))
                v.tensor_copy(kd[:, b % 2, :, :, :], ki[:, b, :, :].unsqueeze(2).to_broadcast([P, NPG, 2, HD])).then_inc(kd_done, 1)
            v.wait_ge(sc_made, DB)
            for i, (c0, c1) in enumerate(cols):
                if i < 2:
                    v.tensor_scalar(sc[:, c0:c1], bank[5 + i][:SS, 0:c1 - c0], IDXW, None, ALU.mult).then_inc(sc_read, 1)
                else:
                    v.scalar_tensor_tensor(sc[:, c0:c1], bank[5 + i][:SS, 0:c1 - c0], IDXW, cdw(cd, "cns")[0:SS, :], ALU.mult, ALU.add).then_inc(sc_read, 1)


def sample_attention(ph, I, O, bs_d, S):
    nc, pool_dma_sem, sem, bank, cm, cw, pcol, prm, fr = ph
    vt, cd, qs, qn, kn, pti, nms, kp = [S[n] for n in ("vt", "cd", "qs", "qn", "kn", "pti", "nms", "kp")]
    fa = S["fa"][:, :, :].rearrange("p a b -> p (a b)")
    vp = fa[:, 0:NPG * AT].rearrange("p (n c) -> p n c", n=NPG)
    with ExitStack() as tmp:
        al = lambda n, s, d=F32: tmp.enter_context(nc.sbuf_tensor(n, s, d))
        ktr = al("ktr", [P, HP, 512])
        bs = al("bs", [P, KEYS])
        om = al("som", [P, 2 * P])
        lg = al("slg", [P, KEYS])
        pt = al("spt", [P, 9, P])
        sm = al("ssm", [P, 4])
    s_bs = sem("sample_bias_in")
    s_k = [sem(f"k_pages_in{i}") for i in range(2)]
    s_v = sem("v_pages_in")
    ck = I["cache_k"][0].rearrange("n p h d -> n p (h d)")
    cv = I["cache_v"][0].rearrange("n p h d -> n p (h d)")
    cols = KEY_COLS
    ktr_made, ktr_read, qs_ready, qk_grp, qk_made = [sem("a_" + n) for n in ("k_turned", "k_taken", "q_spread", "qk_group", "logits_made")]
    lg_done, mx_done, ex_done, rc_done, nrm = [sem("a_" + n) for n in ("logits", "max", "exp", "recip", "norm")]
    pt_made, pt_read, o_made, o_taken, o_turned, o_read = [sem("a_" + n) for n in ("p_turned", "p_taken", "o_made", "o_taken", "o_turned", "o_read")]
    HPS = (0, 2, 4, 6, 1, 3, 5, 7)
    GROUP_AFTER = {5: 0, 9: 1, 13: 2}
    with nc.Block() as block:
        @block.sync
        def _(sp):
            def keys(b):
                for i in range(2):
                    sp.wait_ge(ktr_made, 16 * (b - 1) + 8 * i + 8)
                    for n in range(4):
                        load_page(sp, I, pti, kp[:, 4 * i + n, :], ck, NPG * b + 4 * i + n).then_inc(s_k[i], 16)

            sp.dma_start(bs[:, :], bs_d.rearrange("h q s -> (h q) s")).then_inc(s_bs, 16)
            for b in range(DB):
                if b == 0:
                    for n in range(NPG):
                        load_page(sp, I, pti, vp[:, n, :], cv, n).then_inc(s_v, 16)
                    keys(1)
                    continue
                if b + 1 < DB:
                    keys(b + 1)
                sp.wait_ge(o_made, b)
                for n in range(NPG):
                    load_page(sp, I, pti, vp[:, n, :], cv, NPG * b + n).then_inc(s_v, 16)

        @block.tensor
        def _(e):
            def logits(b):
                e.wait_ge(qs_ready, 2 * b + 2)

                def group(x):
                    i, lo = divmod(x, 2)
                    if lo == 0:
                        if b:
                            e.wait_ge(lg_done, 3 * (b - 1) + i + 1)
                        e.matmul(bank[2 + i][:, :], cdw(cd, "rep")[0:SS, P * b:P * b + P], nms[:, 512 * i:512 * i + 512], start=True, stop=False)
                    e.wait_ge(ktr_read, 16 * b + 4 * x + 4)
                    for y in range(4):
                        hp, j = HPS[4 * lo + y], slice(32 * y, 32 * y + 32)
                        ins = e.matmul(bank[2 + i][j, :], qs[:, b % 2, hp * P + 32 * y:hp * P + 32 * y + 32], ktr[:, 4 * lo + y, :],
                                       start=False, stop=(lo == 1))
                    ins.then_inc(qk_grp, 1)
                    if lo == 1:
                        e.wait_ge(qk_grp, 4 * b + x + 1)
                        e.sem_inc(qk_made, 1)
                for turn in range(16):
                    i, y = divmod(turn, 8)
                    g = 16 * b + turn
                    hp = HPS[y]
                    if y == 0 and b:
                        e.wait_ge(s_k[i], 64 * b)
                    if g >= 2:
                        e.wait_ge(ktr_read, g - 1)
                    for n in range(4):
                        ins = e.transpose(bank[g % 2][:, n * P:(n + 1) * P], kp[:, 4 * i + n, hp * P:(hp + 1) * P], cw("ident"))
                    ins.then_inc(ktr_made, 1)
                    if turn in GROUP_AFTER:
                        group(GROUP_AFTER[turn])
                if b:
                    e.wait_ge(lg_done, 3 * b)
                e.matmul(bank[4][:, 0:SS], cdw(cd, "rep")[0:SS, P * b:P * b + P], nms[:, PAST:], start=True, stop=False)
                for y, hp in enumerate(HPS):
                    j = 32 * (y % 4)
                    e.matmul(bank[4][j:j + 32, 0:SS], qs[:, b % 2, hp * P + j:hp * P + j + 32], kn[:, hp, :], start=False, stop=(y >= 4))
                group(3)
                e.sem_inc(qk_made, 1)

            logits(0)
            for b in range(DB):
                if b + 1 < DB:
                    logits(b + 1)
                e.wait_ge(nrm, b + 1)
                for c in range(3):
                    if 3 * b + c >= 2:
                        e.wait_ge(pt_read, 3 * b + c - 1)
                    for n in range(4 * c, min(4 * c + 4, 9)):
                        w = P if n < 8 else SS
                        ins = e.transpose(bank[5 + (3 * b + c) % 2][:w, (n % 4) * P:(n % 4 + 1) * P], lg[:, n * P:n * P + w], cw("ident"))
                    ins.then_inc(pt_made, 1)
                e.wait_ge(pt_read, 3 * b + 3)
                e.wait_ge(s_v, 16 * NPG * (b + 1))
                if b:
                    e.wait_ge(o_read, 4 * b)
                for n in range(9):
                    w = P if n < 8 else SS
                    for j in range(4):
                        rhs = vp[:, n, 2 * P * j:2 * P * j + 2 * P] if n < 8 else vt[0:SS, 2, 2 * P * j:2 * P * j + 2 * P]
                        ins = e.matmul(bank[7][32 * j:32 * j + 32, 0:2 * P], pt[:w, n, 32 * j:32 * j + 32], rhs, start=(n == 0), stop=(n == 8))
                ins.then_inc(o_made, 1)
                e.wait_ge(o_taken, b + 1)
                for c in range(2):
                    ins = e.transpose(bank[7][:, (2 + c) * P:(3 + c) * P], om[:, c * P:(c + 1) * P], cw("ident"))
                ins.then_inc(o_turned, 1)

        @block.scalar
        def _(a):
            def take_keys(b):
                for g in range(16 * b, 16 * b + 16):
                    a.wait_ge(ktr_made, g + 1)
                    if g % 4 == 0 and g >= 8:
                        a.wait_ge(qk_grp, g // 4 - 1)
                    a.activation(ktr[:, g % 8, :], bank[g % 2][:, :], ACT.Copy).then_inc(ktr_read, 1)

            def exponent(b):
                a.wait_ge(mx_done, b + 1)
                a.activation(lg[:, :], lg[:, :], ACT.Exp, bias=sm[:, 0:1], accum_out=sm[:, 1:2]).then_inc(ex_done, 1)
            take_keys(0)
            exponent(0)
            for b in range(DB):
                if b + 1 < DB:
                    take_keys(b + 1)
                for c in range(3):
                    a.wait_ge(pt_made, 3 * b + c + 1)
                    n, w = (4, P) if c < 2 else (1, SS)
                    a.activation(pt[:w, 4 * c:4 * c + n, :], bank[5 + (3 * b + c) % 2][:w, 0:n * P].rearrange("p (n q) -> p n q", n=n), ACT.Copy).then_inc(pt_read, 1)
                a.wait_ge(o_made, b + 1)
                a.activation(om[:, :], bank[7][:, 0:2 * P], ACT.Copy).then_inc(o_taken, 1)
                a.wait_ge(o_turned, b + 1)
                for p_ in range(2):
                    for c in range(2):
                        r = slice(HD * p_, HD * p_ + HD)
                        a.activation(fr[r, 8 + c:16:2, SP_ + T * b:SP_ + T * b + T],
                                     bank[7][r, (2 + c) * P:(3 + c) * P].rearrange("p (j x q) -> p j x q", x=4, q=T)[:, :, 2 * c + p_, :], ACT.Copy).then_inc(o_read, 1)
                if b + 1 < DB:
                    exponent(b + 1)

        @block.vector
        def _(v):
            def spread(b):
                if b >= 2:
                    v.wait_ge(qk_made, 3 * (b - 1))
                for p_ in range(2):
                    r = slice(HD * p_, HD * p_ + HD)
                    v.tensor_copy(qs[r, b % 2, :].rearrange("p (h x) -> p h x", x=144)[:, :, T * p_:T * p_ + T], qn[r, :, T * b:T * b + T]).then_inc(qs_ready, 1)
            spread(0)
            spread(1)
            v.wait_ge(s_bs, 16)
            for b in range(DB):
                if b:
                    v.wait_ge(pt_made, 3 * b)
                for i, (c0, c1) in enumerate(cols):
                    v.wait_ge(qk_made, 3 * b + i + 1)
                    v.scalar_tensor_tensor(lg[:, c0:c1], bank[2 + i][:, 0:c1 - c0], HD ** -0.5, bs[:, c0:c1], ALU.mult, ALU.add).then_inc(lg_done, 1)
                v.wait_ge(lg_done, 3 * b + 3)
                v.tensor_reduce(sm[:, 0:1], lg[:, :], AXX, ALU.max, negate=True).then_inc(mx_done, 1)
                if b + 2 < DB:
                    spread(b + 2)
                v.wait_ge(ex_done, b + 1)
                v.reciprocal(sm[:, 2:3], sm[:, 1:2]).then_inc(rc_done, 1)
                v.wait_ge(rc_done, b + 1)
                v.tensor_scalar(lg[:, :], lg[:, :], sm[:, 2:3], None, ALU.mult).then_inc(nrm, 1)


def mix_out(ph, I, O, S):
    nc, pool_dma_sem, sem, bank, cm, cw, pcol, prm, fr = ph
    x1, mk, mv, mkt, qt_ = S["x1"], S["mk"], S["mv"], S["mkt"], S["qt"]
    with ExitStack() as tmp:
        al = lambda n, s, d=F32: tmp.enter_context(nc.sbuf_tensor(n, s, d))
        xn = al("xn", [P, 3, D])
        junk = al("junk2", [P, D])
        stats = al("stats2", [P, 4, 3])
        stats_m = al("stats_m", [P, 4, 3])
        ht = al("ht2", [P, KT, TOK])
        w = al("wmix", [P, 2, KT, CH])
        sh = al("sh", [SS, CH // 2])
    s_x, s_m, s_w = sem("x1_in"), sem("mem_in"), [sem("wmix0_in"), sem("wmix1_in")]
    s_w0 = sem("wmix_first_half_in")
    t_made, t_read, x_added, s_kv = sem("mix_tiles"), sem("mix_read"), sem("x1_added"), sem("memkv_out")
    mt_made, mt_read, sh_done = sem("mk_turned"), sem("mk_taken"), sem("half_moved")
    kt = lambda a: a.rearrange("(kt p) n -> p kt n", p=P)
    wout = kt(I["w_out"][0])
    chunks = [wout[:, :, CH * i:CH * i + CH] for i in range(4)] + [kt(I[n][0]) for n in ("w_ck", "w_cv", "w_cq")]
    tiles = [3, 3, 3, 3, 2, 2, 4]
    first = [sum(tiles[:i]) for i in range(8)]
    mem = I["mem_prompt"][0]
    am, dm, pm, mem_turned = norm_to_features(ph, "mem", xn, [P, P], pcol("g_mem"), ht, lambda e, t: e.wait_ge(s_m, 32), (6, 7), (junk, stats_m))

    def x_and_space(a, t):
        a.wait_ge(x_added, 12)
        a.wait_ge(*mem_turned)
    ax, dx, px, cross_turned = norm_to_features(ph, "cross", x1, [m for _, m in TILES], pcol("g_cross"), ht, x_and_space,
                                     (6, 7), (junk, stats), out=xn)

    with nc.Block() as block:
        @block.sync
        def _(sp):
            for c, src in enumerate(chunks):
                if c >= 2:
                    sp.wait_ge(t_made, first[c - 1])
                if c == 0:
                    sp.dma_start(w[:, 0, 0:KT // 2, :], src[:, 0:KT // 2, :]).then_inc(s_w0, 16)
                    sp.dma_start(w[:, 0, KT // 2:, :], src[:, KT // 2:, :]).then_inc(s_w[0], 16)
                    continue
                sp.dma_start(w[:, c % 2, :, :], src).then_inc(s_w[c % 2], 16)

        @block.scalar
        def _(a):
            a.wait_ge(s_w[0], 16)
            for t, (t0, m) in enumerate(TILES):
                src = I["x_prompt"][0] if t < 2 else I["x_sample"].rearrange("b t d -> (b t) d")
                a.dma_start(x1[:m, t, :], src[t0 % SP_:t0 % SP_ + m, :]).then_inc(s_x, 16)
            for t in range(2):
                a.dma_start(xn[:, t, :], mem[P * t:P * t + P, :]).then_inc(s_m, 16)
            am(a)
            ax(a)
            for c, dst in ((4, mk), (5, mv)):
                for t in range(2):
                    n = first[c] + t
                    a.wait_ge(t_made, n + 1)
                    a.activation(dst[:, t, :], bank[n % 4][:, :], ACT.Copy).then_inc(t_read, 1)
            a.wait_ge(t_read, 4)
            for t in range(2):
                for n, src in (("mk_p", mk), ("mv_p", mv)):
                    a.dma_start(O[n][0, 0].rearrange("s h d -> s (h d)")[P * t:P * t + P, :], src[:, t, :]).then_inc(s_kv, 16)
            for i in range(2):
                a.wait_ge(mt_made, i + 1)
                a.activation(mkt[:, 2 * i:2 * i + 2, :], bank[4 + i][:, :].rearrange("p (h s) -> p h s", h=2), ACT.Copy).then_inc(mt_read, 1)
            for j in range(XH):
                n = first[6] + j
                a.wait_ge(t_made, n + 1)
                a.activation(qt_[:, j, :], bank[n % 4][:, 0:TOK], ACT.Copy).then_inc(t_read, 1)
            a.wait_ge(s_kv, 64)

        @block.vector
        def _(v):
            v.wait_ge(s_x, 48)
            for c in range(4):
                if c == 2:
                    dm(v)
                for t, (t0, m) in enumerate(TILES):
                    n = 3 * c + t
                    v.wait_ge(t_made, n + 1)
                    if t == 2:
                        v.tensor_copy(sh[:, :], bank[n % 4][SS:2 * SS, 0:CH // 2]).then_inc(sh_done, 1)
                        xs = x1[:m, t, CH * c:CH * c + CH // 2]
                        v.tensor_tensor(xs, xs, bank[n % 4][:m, 0:CH // 2], ALU.add).then_inc(sh_done, 1)
                        v.wait_ge(sh_done, 2 * c + 2)
                        xs = x1[:m, t, CH * c + CH // 2:CH * c + CH]
                        v.tensor_tensor(xs, xs, sh[:, :], ALU.add).then_inc(x_added, 1)
                        v.wait_ge(x_added, n + 1)
                        continue
                    xs = x1[:m, t, CH * c:CH * c + CH]
                    v.tensor_tensor(xs, xs, bank[n % 4][:m, :], ALU.add).then_inc(x_added, 1)
            dx(v)

        @block.tensor
        def _(e):
            def free(n):
                if 4 <= n < 16:
                    e.wait_ge(x_added, n - 3)
                elif n >= 16:
                    e.wait_ge(t_read, n - 15)
            for c in range(7):
                if c == 2:
                    pm(e)
                if c == 6:
                    e.wait_ge(mt_read, 2)
                    px(e)
                    e.wait_ge(*cross_turned)
                if c == 4:
                    e.wait_ge(*mem_turned)
                e.wait_ge(*((s_w[c % 2], 16 * (c // 2 + 1)) if c else (s_w0, 16)))
                for t in range(tiles[c]):
                    n = first[c] + t
                    free(n)
                    if c < 4 and t == 2:
                        for k in range(KT):
                            for a_ in range(2):
                                ins = e.matmul(bank[n % 4][SS * a_:SS * a_ + SS, 0:CH // 2], fr[:, k, SP_:],
                                               w[:, c % 2, k, CH // 2 * a_:CH // 2 * (a_ + 1)], start=(k == 0), stop=(k == KT - 1))
                    elif c < 6:
                        t0, m = TILES[t]
                        lhs = (lambda k: fr[:, k, t0:t0 + m]) if c < 4 else (lambda k: ht[:, k, t0:t0 + m])
                        for k in range(KT):
                            if n == 0 and k == KT // 2:
                                e.wait_ge(s_w[0], 16)
                            ins = e.matmul(bank[n % 4][:m, :], lhs(k), w[:, c % 2, k, :], start=(k == 0), stop=(k == KT - 1))
                    else:
                        for k in range(KT):
                            ins = e.matmul(bank[n % 4][:, 0:TOK], w[:, c % 2, k, P * t:P * t + P], ht[:, k, :], start=(k == 0), stop=(k == KT - 1))
                    ins.then_inc(t_made, 1)
                if c == 5:
                    e.wait_ge(t_read, 4)
                    for i in range(2):
                        for h in (2 * i, 2 * i + 1):
                            for t in range(2):
                                ins = e.transpose(bank[4 + i][:, (h % 2) * MEM + P * t:(h % 2) * MEM + P * t + P], mk[:, t, P * h:P * h + P], cw("ident"))
                        ins.then_inc(mt_made, 1)


def cross(ph, I, O, S):
    nc, pool_dma_sem, sem, bank, cm, cw, pcol, prm, fr = ph
    x1, mk, mv, mkt, qt_ = S["x1"], S["mk"], S["mv"], S["mkt"], S["qt"]
    with ExitStack() as tmp:
        al = lambda n, s, d=F32: tmp.enter_context(nc.sbuf_tensor(n, s, d))
        wco = al("wco", [P, XH, D])
        ot = al("ot", [P, XH, TOK])
        ckk = al("ckk", [P, 4, 2, XW])
        cvv = al("cvv", [P, 4, 2, XW])
        kts = al("kts", [P, 2, XH, MEM])
        qx = al("qx", [P, DB, XH * 40])
        lg = al("clg", [P, 4, 4, MEM])
        pt = al("cpt", [P, 2, 4, P])
        sm = al("csm", [P, 4, 3, 4])
    s_w, s_k, s_v = sem("wco_in"), [sem(f"ckk_in{i}") for i in range(4)], sem("cvv_in")
    qk_made, lg_done, mx_done, ex_done, rc_done, nrm = [sem("c_" + n) for n in ("qk", "logits", "max", "exp", "recip", "norm")]
    pt_made, pt_read, o_made, o_read = [sem("c_" + n) for n in ("turned", "taken", "o", "o_read")]
    kt_made, kt_read, qx_zero, qx_ready, x_made, x_added = [sem("c_" + n) for n in ("k_turned", "k_taken", "q_zero", "q_spread", "x_made", "x_added")]
    UN = [("p", 0), ("p", 1), ("s", 0), ("s", 1)]
    nh = lambda u: 4 if u[0] == "p" else 1
    done = lambda n: sum(nh(u) for u in UN[:n])
    ckd = I["cache_mem_k"][0].rearrange("b (t p) h d -> b p t (h d)", p=P)
    cvd = I["cache_mem_v"][0].rearrange("b (t p) h d -> b p t (h d)", p=P)
    LGB = [(0, 1), (2, 3), (0,), (0,)]
    XOB = (7, 1)
    with nc.Block() as block:
        @block.sync
        def _(sp):
            for b in range(DB):
                if b >= 4:
                    sp.wait_ge(kt_made, 2 * (b - 3))
                sp.dma_start(ckk[:, b % 4, :, :], ckd[b]).then_inc(s_k[b % 4], 16)

        @block.scalar
        def _(a):
            for b in range(4):
                a.dma_start(cvv[:, b, :, :], cvd[b]).then_inc(s_v, 16)
            a.dma_start(wco[:, :, :], I["w_co"][0].rearrange("(h p) n -> p h n", p=P)).then_inc(s_w, 16)

            def exponent(n):
                a.wait_ge(mx_done, n + 1)
                for j in range(nh(UN[n])):
                    a.activation(lg[:, n, j, :], lg[:, n, j, :], ACT.Exp, bias=sm[:, n, 0, j:j + 1], accum_out=sm[:, n, 1, j:j + 1]).then_inc(ex_done, 1)

            def take_keys(g):
                for b in range(4 * g, 4 * g + 4):
                    for i in range(2):
                        a.wait_ge(kt_made, 2 * b + i + 1)
                        if b >= 2:
                            a.wait_ge(qk_made, 4 + b - 1)
                        a.activation(kts[:, b % 2, 2 * i:2 * i + 2, :], bank[2 + i][:, :].rearrange("p (h s) -> p h s", h=2), ACT.Copy).then_inc(kt_read, 1)

            def take_out(n):
                u = UN[n]
                for i in range(2 if u[0] == "p" else 1):
                    a.wait_ge(pt_made, 2 * min(n, 2) + max(n - 2, 0) + i + 1)
                    w = 4 if u[0] == "p" else 2
                    a.activation(pt[:, i, 0:w, :], bank[4 + i][:, 0:w * P].rearrange("p (j q) -> p j q", j=w), ACT.Copy).then_inc(pt_read, 1)
                a.wait_ge(o_made, n + 1)
                if u[0] == "p":
                    a.activation(ot[:, :, P * u[1]:P * u[1] + P], bank[6][:, :].rearrange("p (h q) -> p h q", h=XH), ACT.Copy).then_inc(o_read, 1)
                else:
                    g0 = SP_ + 32 * u[1]
                    a.activation(ot[:, :, g0:g0 + 32].rearrange("p h (b q) -> p b h q", q=T),
                                 bank[6][:, 0:P].rearrange("p (b h q) -> p b h q", b=4, h=XH), ACT.Copy).then_inc(o_read, 1)
                if n == 2:
                    for b in range(4, 8):
                        a.dma_start(cvv[:, b - 4, :, :], cvd[b]).then_inc(s_v, 16)
            exponent(0)
            exponent(1)
            take_keys(0)
            take_out(0)
            take_out(1)
            exponent(2)
            take_keys(1)
            take_out(2)
            exponent(3)
            take_out(3)

        @block.tensor
        def _(e):
            def prompt_logits(n):
                tok = slice(P * n, P * n + P)
                for h in range(XH):
                    ins = e.matmul(bank[LGB[n][h // 2]][:, (h % 2) * MEM:(h % 2 + 1) * MEM], qt_[:, h, tok], mkt[:, h, :], start=True, stop=True)
                    if h % 2:
                        ins.then_inc(qk_made, 1)

            def sample_logits(n):
                e.wait_ge(lg_done, n)
                e.wait_ge(qx_ready, DB)
                g = UN[n][1]

                def turn(b):
                    e.wait_ge(s_k[b % 4], 16 * (b // 4 + 1))
                    for i in range(2):
                        if b:
                            e.wait_ge(kt_read, 2 * (b - 1) + i + 1)
                        for h in (2 * i, 2 * i + 1):
                            for t in range(2):
                                ins = e.transpose(bank[2 + i][:, (h % 2) * MEM + P * t:(h % 2) * MEM + P * t + P], ckk[:, b % 4, t, P * h:P * h + P], cw("ident"))
                        ins.then_inc(kt_made, 1)
                turn(4 * g)
                for b in range(4 * g, 4 * g + 4):
                    if b % 4 < 3:
                        turn(b + 1)
                    e.wait_ge(kt_read, 2 * b + 2)
                    r = 32 * (b % 4)
                    for h in range(XH):
                        ins = e.matmul(bank[LGB[n][0]][r:r + 32, 0:MEM], qx[:, b, 32 * h:32 * h + 32], kts[:, b % 2, h, :], start=(h == 0), stop=(h == XH - 1))
                    ins.then_inc(qk_made, 1)

            def out(n):
                u = UN[n]
                e.wait_ge(nrm, n + 1)
                for i in range(2 if u[0] == "p" else 1):
                    if n:
                        e.wait_ge(pt_read, 2 * min(n, 2) + max(n - 2, 0))
                    if u[0] == "p":
                        for h in (2 * i, 2 * i + 1):
                            for t in range(2):
                                ins = e.transpose(bank[4 + i][:, (2 * (h % 2) + t) * P:(2 * (h % 2) + t + 1) * P], lg[:, n, h, P * t:P * t + P], cw("ident"))
                    else:
                        for t in range(2):
                            ins = e.transpose(bank[4][:, t * P:(t + 1) * P], lg[:, n, 0, P * t:P * t + P], cw("ident"))
                    ins.then_inc(pt_made, 1)
                e.wait_ge(pt_read, 2 * min(n + 1, 2) + max(n - 1, 0))
                if n:
                    e.wait_ge(o_read, n)
                if u[0] == "p":
                    for h in range(XH):
                        for t in range(2):
                            ins = e.matmul(bank[6][:, P * h:P * h + P], mv[:, t, P * h:P * h + P], pt[:, h // 2, 2 * (h % 2) + t, :], start=(t == 0), stop=(t == 1))
                else:
                    e.wait_ge(s_v, 64 * (u[1] + 1))
                    for b in range(4):
                        for h in range(XH):
                            c = 32 * b + T * h
                            for t in range(2):
                                ins = e.matmul(bank[6][:, c:c + T], cvv[:, b, t, P * h:P * h + P], pt[:, 0, t, c:c + T], start=(t == 0), stop=(t == 1))
                ins.then_inc(o_made, 1)

            def x_out(t):
                t0, m = TILES[t]
                e.wait_ge(s_w, 16)
                e.wait_ge(o_read, (1, 2, 4)[t])
                for c in range(4):
                    n = 4 * t + c
                    if n >= 2:
                        e.wait_ge(x_added, n - 1)
                    for h in range(XH):
                        ins = e.matmul(bank[XOB[n % 2]][:m, :], ot[:, h, t0:t0 + m], wco[:, h, CH * c:CH * c + CH], start=(h == 0), stop=(h == XH - 1))
                    ins.then_inc(x_made, 1)
            prompt_logits(0)
            prompt_logits(1)
            sample_logits(2)
            out(0)
            out(1)
            x_out(0)
            sample_logits(3)
            out(2)
            x_out(1)
            out(3)
            x_out(2)

        @block.vector
        def _(v):
            v.memset(qx[:, :, :], 0.0).then_inc(qx_zero, 1)
            v.wait_ge(qx_zero, 1)
            for b in range(DB):
                v.tensor_copy(qx[:, b, :].rearrange("p (h x) -> p h x", x=40)[:, :, 0:T], qt_[:, :, SP_ + T * b:SP_ + T * b + T]).then_inc(qx_ready, 1)

            def softmax(n):
                u = UN[n]
                if u[0] == "p":
                    v.wait_ge(qk_made, 2 * n + 2)
                    for i in range(2):
                        ins = v.tensor_scalar(lg[:, n, 2 * i:2 * i + 2, :], bank[LGB[n][i]][:, :].rearrange("p (h s) -> p h s", h=2), P ** -0.5, None, ALU.mult)
                    ins.then_inc(lg_done, 1)
                else:
                    v.wait_ge(qk_made, 4 + 4 * (u[1] + 1))
                    v.tensor_scalar(lg[:, n, 0, :], bank[LGB[n][0]][:, 0:MEM], P ** -0.5, None, ALU.mult).then_inc(lg_done, 1)
                v.wait_ge(lg_done, n + 1)
                w = nh(u)
                v.tensor_reduce(sm[:, n, 0, 0:w], lg[:, n, 0:w, :], AXX, ALU.max, negate=True).then_inc(mx_done, 1)
                v.wait_ge(ex_done, done(n + 1))
                v.reciprocal(sm[:, n, 2, 0:w], sm[:, n, 1, 0:w]).then_inc(rc_done, 1)
                v.wait_ge(rc_done, n + 1)
                v.tensor_tensor(lg[:, n, 0:w, :], lg[:, n, 0:w, :], sm[:, n, 2, 0:w].unsqueeze(2).to_broadcast([P, w, MEM]), ALU.mult).then_inc(nrm, 1)

            def add(t):
                m = TILES[t][1]
                for c in range(4):
                    n = 4 * t + c
                    v.wait_ge(x_made, n + 1)
                    xs = x1[:m, t, CH * c:CH * c + CH]
                    v.tensor_tensor(xs, xs, bank[XOB[n % 2]][:m, :], ALU.add).then_inc(x_added, 1)
            softmax(0)
            softmax(1)
            softmax(2)
            add(0)
            softmax(3)
            add(1)
            add(2)


def route(ph, I, S):
    nc, pool_dma_sem, sem, bank, cm, cw, pcol, prm, fr = ph
    x1, hn, cmo, gates, slot, rounds = S["x1"], S["hn"], S["cmo"], S["gates"], S["slot"], S["rounds"]
    with ExitStack() as tmp:
        al = lambda n, s, d=F32: tmp.enter_context(nc.sbuf_tensor(n, s, d))
        stats = al("stats3", [P, 4, 3])
        wr = al("wr", [P, KT, NG + NE])
        br = al("br", [P, NG + NE])
        lo = al("rlog", [P, 3, NG + NE])
        gm = al("gm", [P, 3])
        eg = al("eg", [P, 3, NG])
        cg = al("cg", [P, 3, NG])
        xg = al("xge", [P, 3, NG])
        pg = al("pg", [P, 3])
        m8 = al("rm8", [P, 3, 8])
        gt = al("rgt", [P, 3, NE])
        eq = al("req", [P, 3, NE])
        cum = al("rcum", [P, 3, NE])
        ex = al("rex", [P, 3, NE])
        ws = al("rws", [P, 3])
        need = al("rneed", [P, 1])
        mc = al("mc", [P, 1])
        rf = al("rf", [P, 2])
    flat = fr[:, :, :].rearrange("p a b -> p (a b)")
    ht = flat[:, 0:KT * TOK].rearrange("p (k t) -> p k t", k=KT)
    junk = flat[:, KT * TOK:KT * TOK + D]
    s_in, r_made, exps, subs, sel_done, rk_made, rch = [sem("r_" + n) for n in ("in", "logits", "exps", "differences", "selected", "ranks", "chain")]
    an, dn, pn, turned = norm_to_features(ph, "ffn", x1, [m for _, m in TILES], pcol("g_ffn"), ht, lambda e, t: None, (6, 7), (junk, stats), out=hn)
    ones = cmw(cmo, "ones")
    with nc.Block() as block:
        @block.sync
        def _(sp):
            sp.dma_start(cmo[:, :], S["c_moe"]).then_inc(s_in, 16)
            sp.dma_start(wr[:, :, 0:NG], I["w_rg"][0].rearrange("(kt p) n -> p kt n", p=P)).then_inc(s_in, 16)
            sp.dma_start(wr[:, :, NG:], I["w_re"][0].rearrange("(kt p) n -> p kt n", p=P)).then_inc(s_in, 16)
            sp.dma_start(br[:, 0:NG], I["b_rg"][0].partition_broadcast(P)).then_inc(s_in, 16)
            sp.dma_start(br[:, NG:], I["b_re"][0].partition_broadcast(P)).then_inc(s_in, 16)
            for u in range(RING):
                load_expert_unit(sp, I, S, 0, u)

        @block.scalar
        def _(a):
            an(a)
            a.wait_ge(subs, 1)
            a.activation(xg[:, :, :], xg[:, :, :], ACT.Exp).then_inc(exps, 1)
            a.wait_ge(subs, 2)
            a.activation(ex[:, :, :], ex[:, :, :], ACT.Exp).then_inc(exps, 1)

        @block.tensor
        def _(e):
            pn(e)
            e.wait_ge(*turned)
            e.wait_ge(s_in, 80)
            for t, (t0, m) in enumerate(TILES):
                for k in range(KT):
                    ins = e.matmul(bank[t][:m, 0:NG + NE], ht[:, k, t0:t0 + m], wr[:, k, :], start=(k == 0), stop=(k == KT - 1))
                ins.then_inc(r_made, 1)
            e.wait_ge(sel_done, 1)
            for t in range(3):
                for j in range(t + 1):
                    e.matmul(bank[3][:, NE * t:NE * t + NE], ones if j < t else cmw(cmo, "upto"), gt[:, j, :], start=(j == 0), stop=(j == t))
            for j in range(3):
                ins = e.matmul(bank[3][:, NE * 3:NE * 4], ones, gt[:, j, :], start=(j == 0), stop=(j == 2))
            ins.then_inc(rk_made, 1)

        @block.vector
        def _(v):
            d = chain_of(v, rch)
            d(v.memset(lo[:, :, :], 0.0))
            dn(v)
            v.wait_ge(s_in, 80)
            for t, (t0, m) in enumerate(TILES):
                v.wait_ge(r_made, t + 1)
                d(v.tensor_tensor(lo[:m, t, :], bank[t][:m, 0:NG + NE], br[:m, :], ALU.add))
            gl, el = lo[:, :, 0:NG], lo[:, :, NG:]
            b3 = lambda z, n: z.unsqueeze(2).to_broadcast([P, 3, n])
            d(v.tensor_reduce(gm[:, :], gl, AXX, ALU.max))
            v.tensor_tensor(xg[:, :, :], gl, b3(gm[:, :], NG), ALU.subtract).then_inc(subs, 1)
            d(v.tensor_tensor(eg[:, :, :], gl, b3(gm[:, :], NG), ALU.is_equal))
            for t in range(3):
                d(v.tensor_tensor_scan(cg[:, t, :], ones[:, 0:NG], eg[:, t, :], 0.0, ALU.mult, ALU.add))
            d(v.scalar_tensor_tensor(eg[:, :, :], cg[:, :, :], 1.0, eg[:, :, :], ALU.is_le, ALU.mult))
            d(v.tensor_scalar(eg[:, :, :], eg[:, :, :], -1.0, -NEG, ALU.add, ALU.mult))
            d(v.tensor_tensor(el.rearrange("p t (g x) -> p t g x", g=NG), el.rearrange("p t (g x) -> p t g x", g=NG),
                              eg[:, :, :].unsqueeze(3).to_broadcast([P, 3, NG, EPG]), ALU.add))
            for t in range(3):
                top_turn(v, d, 0, el[:, t, :], None, m8[:, t, :], 2, NE, P)
                top_mask(v, d, el[:, t, :], m8[:, t, :], gt[:, t, :], eq[:, t, :], cum[:, t, :], ones[:, 0:NE], need, 2, None, P)
            v.wait_ge(subs, 1)
            v.tensor_tensor(ex[:, :, :], el, m8[:, :, 0:1].to_broadcast([P, 3, NE]), ALU.subtract).then_inc(subs, 1)
            v.memset(gt[64:P, 2, :], 0.0).then_inc(sel_done, 1)
            v.wait_ge(exps, 2)
            d(v.tensor_reduce(pg[:, :], xg[:, :, :], AXX, ALU.add))
            d(v.tensor_tensor(ex[:, :, :], ex[:, :, :], gt[:, :, :], ALU.mult))
            d(v.memset(ex[64:P, 2, :], 1.0))
            d(v.tensor_reduce(ws[:, :], ex[:, :, :], AXX, ALU.add))
            d(v.tensor_tensor(ws[:, :], ws[:, :], pg[:, :], ALU.mult))
            d(v.reciprocal(ws[:, :], ws[:, :]))
            d(v.tensor_tensor(gates[:, :, :], ex[:, :, :], b3(ws[:, :], NE), ALU.mult))
            v.wait_ge(rk_made, 1)
            d(v.tensor_tensor(slot[:, :, :], bank[3][:, 0:3 * NE].rearrange("p (t e) -> p t e", t=3), gt[:, :, :], ALU.mult))
            d(v.tensor_scalar(slot[:, :, :], slot[:, :, :], -1.0, None, ALU.add))
            d(v.tensor_reduce(mc[:, :], bank[3][:, 3 * NE:4 * NE], AXX, ALU.max))
            d(v.memset(rf[:, 0:1], 1.0))
            for r in range(1, -(-TOK // SLOTS)):
                d(v.tensor_scalar(rf[:, 1:2], mc[:, :], float(SLOTS * r), None, ALU.is_gt))
                d(v.tensor_tensor(rf[:, 0:1], rf[:, 0:1], rf[:, 1:2], ALU.add))
            d(v.tensor_copy(rounds[:, :], rf[:, 0:1]))


UNITS = 12


def load_expert_unit(sp, I, S, p, u, ahead=0):
    w, s_w = S["w"], S["s_w"]
    for a_ in range(2):
        weights = I["w_e2" if u >= 8 else ("w_e1", "w_e3")[u // 4]][0]
        if isinstance(p, int):
            weights = weights[2 * p:2 * p + 2]
        else:
            weights = weights[2 * ahead:NE - 2 + 2 * ahead]
        if u < 8:
            src = weights.rearrange("(g a) (kt p) n -> g p a kt n", a=2, p=P)
            src = src[0:1] if isinstance(p, int) else src[bass.DynSlice(p, 1)]
            src = src[:, :, a_, 4 * (u % 4):4 * (u % 4) + 4, :].squeeze(0)
            dst = w[:, u % RING, a_, :].rearrange("p (k n) -> p k n", k=4)
        else:
            src = weights.rearrange("(g a) (f p) n -> g p a f n", a=2, p=P)
            src = src[0:1] if isinstance(p, int) else src[bass.DynSlice(p, 1)]
            src = src[:, :, a_, u - 8, :].squeeze(0)
            dst = w[:, u % RING, a_, :]
        sp.dma_start(dst, src).then_inc(s_w[u % RING], 16)


def experts(ph, I, S):
    nc, pool_dma_sem, sem, bank, cm, cw, pcol, prm, fr = ph
    x1, hn, cmo, gates, slot, rounds = S["x1"], S["hn"], S["cmo"], S["gates"], S["slot"], S["rounds"]
    w, s_w = S["w"], S["s_w"]
    flat = fr[:, :, :].rearrange("p a b -> p (a b)")
    at = [0]

    def view(n):
        at[0] += n
        return flat[:, at[0] - n:at[0]]
    xg = view(KT * P).rearrange("p (k s) -> p k s", k=KT)
    ys = view(D)
    oh = view(3 * P).rearrange("p (t s) -> p t s", t=3)
    og = view(3 * P).rearrange("p (t s) -> p t s", t=3)
    sg = view(TOK)
    u1, u2 = view(DE), view(DE)
    ut = view(DE).rearrange("p (f s) -> p f s", f=4)
    w_used, oh_ready, og_ready, xg_made, xg_read, h_made, silu_done, u_done = [sem("m_" + n) for n in (
        "w_used", "onehots", "gates_spread", "gathered", "gathered_read", "hidden", "silu", "u")]
    ut_made, ut_read, sg_made, sg_read, y_made, y_read, sc_made, sc_read, slot_ready = [sem("m_" + n) for n in (
        "u_turned", "u_taken", "onehots_turned", "onehots_taken", "y_made", "y_read", "scattered", "added", "slots_ready")]
    w2_turn = sem("m_w2_turn")
    half = lambda z, a: z[SLOTS * a:SLOTS * a + SLOTS]
    PAIRS = NE // 2

    def number_of_rounds(eng):
        return eng.value_load(rounds[0:1, 0:1], min_val=1, max_val=-(-TOK // SLOTS))

    with nc.Block() as block:
        @block.sync
        def _(sp):
            def load(r, p, u, ahead=0):
                sp.wait_ge(w_used, (r * PAIRS + p) * UNITS + (UNITS * ahead + u + 1))
                if u == 8:
                    sp.sem_inc(w2_turn, 1)
                load_expert_unit(sp, I, S, p, u, ahead)
            def rest(r):
                with sp.Fori(0, PAIRS - 1) as p:
                    for u in range(RING, UNITS):
                        load(r, p, u)
                    for u in range(RING):
                        load(r, p, u, 1)
                for u in range(RING, UNITS):
                    load(r, PAIRS - 1, u)
            rest(0)
            rounds_ = number_of_rounds(sp)
            with sp.If(rounds_ > 1):
                with sp.Fori(1, rounds_) as r:
                    for u in range(RING):
                        load(r, 0, u)
                    rest(r)

        def pairs(eng, rounds_, step):
            with eng.Fori(0, rounds_) as r:
                step(r, 0, True, False)
                with eng.Fori(1, PAIRS - 1) as p:
                    step(r, p, False, False)
                step(r, PAIRS - 1, False, True)

        @block.vector
        def _(v):
            mine = lambda z, p: z[:, :, bass.DynSlice(2 * p, 2)].unsqueeze(3).to_broadcast([P, 3, 2, SLOTS])
            cut = lambda z: z.rearrange("p t (e s) -> p t e s", e=2)

            def onehots(r, p):
                v.tensor_tensor(cut(oh), cmw(cmo, "iota_slots").unsqueeze(1).unsqueeze(1).to_broadcast([P, 3, 2, SLOTS]), mine(slot, p), ALU.is_equal).then_inc(oh_ready, 1)
                v.wait_ge(oh_ready, r * PAIRS + (p + 1))

            def take_rows(r, p):
                g = r * PAIRS + p
                for q in range(4):
                    v.wait_ge(xg_made, 4 * g + (q + 1))
                    v.tensor_tensor(xg[:, 4 * q:4 * q + 4, :], bank[6 + q % 2][:, :].rearrange("p (k s) -> p k s", k=4),
                                    pcol("g_ffn")[:, 4 * q:4 * q + 4].unsqueeze(2).to_broadcast([P, 4, P]), ALU.mult).then_inc(xg_read, 1)

            def add(r, p):
                g = r * PAIRS + p
                for i in range(12):
                    t, c = divmod(i, 4)
                    m = TILES[t][1]
                    v.wait_ge(sc_made, 12 * g + (i + 1))
                    xs = x1[:m, t, CH * c:CH * c + CH]
                    v.tensor_tensor(xs, xs, bank[6 + i % 2][:m, :], ALU.add).then_inc(sc_read, 1)

            def step(r, p, first, last):
                g = r * PAIRS + p
                if first:
                    v.wait_ge(slot_ready, r + 1)
                    onehots(r, p)
                    take_rows(r, p)
                else:
                    v.wait_ge(sg_made, g)
                v.tensor_tensor(cut(og), cut(oh), mine(gates, p), ALU.mult).then_inc(og_ready, 1)
                v.wait_ge(og_ready, g + 1)
                if not last:
                    onehots(r, p + 1)
                if not first:
                    add(r, p - 1)
                v.wait_ge(silu_done, g + 1)
                v.wait_ge(h_made, 2 * g + 2)
                v.tensor_tensor(u2, u1, bank[1][:, :], ALU.mult).then_inc(u_done, 1)
                if not last:
                    take_rows(r, p + 1)
                else:
                    add(r, p)
                    v.tensor_scalar(slot[:, :, :], slot[:, :, :], -float(SLOTS), None, ALU.add).then_inc(slot_ready, 1)
            v.sem_inc(slot_ready, 1)
            pairs(v, number_of_rounds(v), step)

        @block.scalar
        def _(a):
            def take_gates(g):
                a.wait_ge(sg_made, g + 1)
                a.activation(sg, bank[1][:, 0:TOK], ACT.Copy).then_inc(sg_read, 1)

            def step(r, p, first, last):
                g = r * PAIRS + p
                if not first:
                    take_gates(g - 1)
                a.wait_ge(h_made, 2 * g + 1)
                a.activation(u1, bank[0][:, :], ACT.Silu).then_inc(silu_done, 1)
                a.wait_ge(ut_made, g + 1)
                a.activation(ut, bank[0][:, :].rearrange("p (f s) -> p f s", f=4), ACT.Copy).then_inc(ut_read, 1)
                a.wait_ge(y_made, g + 1)
                for c in range(4):
                    a.activation(ys[:, CH * c:CH * c + CH], bank[2 + c][:, :], ACT.Copy).then_inc(y_read, 1)
                if last:
                    take_gates(g)
            pairs(a, number_of_rounds(a), step)

        @block.tensor
        def _(e):
            def gather(r, p):
                g = r * PAIRS + p
                e.wait_ge(oh_ready, g + 1)
                for q in range(4):
                    if q >= 2:
                        e.wait_ge(xg_read, 4 * g + (q - 1))
                    for k in range(4 * q, 4 * q + 4):
                        for t, (t0, m) in enumerate(TILES):
                            ins = e.matmul(bank[6 + q % 2][:, (k % 4) * P:(k % 4 + 1) * P], hn[:m, t, k * P:(k + 1) * P], oh[:m, t, :],
                                           start=(t == 0), stop=(t == 2))
                    ins.then_inc(xg_made, 1)

            def turn_gates(g):
                e.wait_ge(og_ready, g + 1)
                for t, (t0, m) in enumerate(TILES):
                    ins = e.transpose(bank[1][:, t0:t0 + m], og[:m, t, :], cw("ident")[:m, :m])
                ins.then_inc(sg_made, 1)

            def hidden(g, units):
                for u in units:
                    e.wait_ge(s_w[u % RING], 64 * g + 32 * (u // RING + 1))
                    for k in range(4):
                        for a_ in range(2):
                            kk = 4 * (u % 4) + k
                            ins = e.matmul(half(bank[u // 4], a_), xg[:, kk, SLOTS * a_:SLOTS * a_ + SLOTS],
                                           w[:, u % RING, a_, DE * k:DE * k + DE], start=(kk == 0), stop=(kk == KT - 1))
                    ins.then_inc(w_used, 1)
                e.wait_ge(w_used, g * UNITS + (u + 1 + RING))
                e.sem_inc(h_made, 1)

            def scatter(g):
                e.wait_ge(sg_read, g + 1)
                e.wait_ge(y_read, 4 * g + 4)
                for i in range(12):
                    t, c = divmod(i, 4)
                    t0, m = TILES[t]
                    if i >= 2:
                        e.wait_ge(sc_read, 12 * g + (i - 1))
                    e.matmul(bank[6 + i % 2][:m, :], sg[:, t0:t0 + m], ys[:, CH * c:CH * c + CH], start=True, stop=True).then_inc(sc_made, 1)

            def step(r, p, first, last):
                g = r * PAIRS + p
                if first:
                    gather(r, p)
                else:
                    turn_gates(g - 1)
                e.wait_ge(xg_read, 4 * g + 4)
                hidden(g, range(0, 4))
                if not first:
                    scatter(g - 1)
                    e.wait_ge(sg_read, g)
                hidden(g, range(4, 8))
                if not last:
                    if not first:
                        e.wait_ge(sc_read, 12 * g)
                    gather(r, p + 1)
                e.wait_ge(u_done, g + 1)
                for f in range(4):
                    ins = e.transpose(bank[0][:, f * P:(f + 1) * P], u2[:, f * P:(f + 1) * P], cw("ident"))
                ins.then_inc(ut_made, 1)
                e.wait_ge(ut_read, g + 1)
                for f in range(4):
                    u = 8 + f
                    e.wait_ge(s_w[u % RING], 64 * g + 32 * (u // RING + 1))
                    for c in range(4):
                        for a_ in range(2):
                            ins = e.matmul(half(bank[2 + c], a_), ut[:, f, SLOTS * a_:SLOTS * a_ + SLOTS],
                                           w[:, u % RING, a_, CH * c:CH * c + CH], start=(f == 0), stop=(f == 3))
                    ins.then_inc(w_used, 1)
                e.wait_ge(w_used, g * UNITS + (UNITS + RING))
                e.sem_inc(y_made, 1)
                if last:
                    turn_gates(g)
                    scatter(g)
                    e.wait_ge(sc_read, 12 * g + 12)
            e.sem_inc(w_used, RING)
            pairs(e, number_of_rounds(e), step)


def finish(ph, I, O, S):
    nc, pool_dma_sem, sem, bank, cm, cw, pcol, prm, fr = ph
    x1 = S["x1"]
    with ExitStack() as tmp:
        al = lambda n, s, d=F32: tmp.enter_context(nc.sbuf_tensor(n, s, d))
        junk = al("junk4", [P, D])
        st_ = al("stats4", [P, 4, 3])
        gf = al("gf", [P, D])
    s_g, sq, ms, rt, rc, fo, s_o = [sem("f_" + n) for n in ("gain_in", "squares", "mean", "root", "recip", "out", "stored")]
    with nc.Block() as block:
        @block.sync
        def _(sp):
            sp.dma_start(gf[:, :], I["g_final"].partition_broadcast(P)).then_inc(s_g, 16)
            for t, (t0, m) in enumerate(TILES):
                sp.wait_ge(fo, t + 1)
                dst = O["y_p"][0] if t < 2 else O["y_s"].rearrange("b t d -> (b t) d")
                sp.dma_start(dst[t0 % SP_:t0 % SP_ + m, :], x1[:m, t, :]).then_inc(s_o, 16)
            sp.wait_ge(s_o, 48)

        @block.scalar
        def _(a):
            for t, (t0, m) in enumerate(TILES):
                if t:
                    a.wait_ge(sq, t)
                a.activation(junk[:m, :], x1[:m, t, :], ACT.Square, accum_out=st_[:m, 0, t:t + 1]).then_inc(sq, 1)
            for t, (t0, m) in enumerate(TILES):
                a.wait_ge(ms, t + 1)
                a.activation(st_[:m, 2, t:t + 1], st_[:m, 1, t:t + 1], ACT.Sqrt).then_inc(rt, 1)

        @block.vector
        def _(v):
            for t, (t0, m) in enumerate(TILES):
                v.wait_ge(sq, t + 1)
                v.tensor_scalar(st_[:m, 1, t:t + 1], st_[:m, 0, t:t + 1], 1.0 / D, EPS, ALU.mult, ALU.add).then_inc(ms, 1)
            v.wait_ge(s_g, 16)
            for t, (t0, m) in enumerate(TILES):
                v.wait_ge(rt, t + 1)
                v.reciprocal(st_[:m, 3, t:t + 1], st_[:m, 2, t:t + 1]).then_inc(rc, 1)
                v.wait_ge(rc, t + 1)
                v.scalar_tensor_tensor(x1[:m, t, :], x1[:m, t, :], st_[:m, 3, t:t + 1], gf[:m, :], ALU.mult, ALU.mult).then_inc(fo, 1)


_INS = ["x_prompt", "x_sample", "mem_prompt", "cache_k", "cache_v", "cache_idx_k", "page_table", "state_wkv",
        "state_shift", "cache_mem_k", "cache_mem_v", "g_mix", "w_in", "mu_shift", "rw_w0", "rw_w2", "rw_a0", "rw_a2",
        "rw_g2", "rw_kk", "rw_ka", "rw_rk", "rw_ln_g", "rw_ln_b", "w_out", "g_cross", "g_mem", "w_cq", "w_ck", "w_cv",
        "w_co", "g_ffn", "w_rg", "b_rg", "w_re", "b_re", "w_e1", "w_e3", "w_e2", "rel_bias", "g_final"]
_OUTS = [("y_p", (1, 256, 2048)), ("y_s", (8, 8, 2048)), ("k_p", (1, 1, 256, 16, 64)), ("v_p", (1, 1, 256, 16, 64)),
         ("ik_p", (1, 1, 256, 64)), ("wkv_p", (1, 1, 16, 64, 64)), ("shift_p", (1, 1, 3328)),
         ("mk_p", (1, 1, 256, 4, 128)), ("mv_p", (1, 1, 256, 4, 128)), ("k_s", (1, 8, 8, 16, 64)),
         ("v_s", (1, 8, 8, 16, 64)), ("ik_s", (1, 8, 8, 64)), ("wkv_s", (1, 8, 16, 64, 64)), ("shift_s", (1, 8, 3328))]


def kernel(**inputs):
    import numpy as _np
    import concourse.bacc as _bacc
    from concourse import mybir as _mybir
    from concourse.bass_utils import run_bass_kernel_spmd as _run

    nc = _bacc.Bacc("TRN2", target_bir_lowering=False, num_devices=1)
    arrays, ins, cons, outs = {}, {}, {}, {}
    for name in _INS:
        a = _np.ascontiguousarray(inputs[name])
        arrays[f"in_{name}"] = a
        ins[name] = nc.dram_tensor(f"in_{name}", a.shape, _mybir.dt.from_np(a.dtype), kind="ExternalInput").ap()
    for name, a in CONSTS.items():
        arrays[name] = a
        cons[name] = nc.dram_tensor(name, a.shape, _mybir.dt.from_np(a.dtype), kind="ExternalInput").ap()
    for name, shape in _OUTS:
        outs[name] = nc.dram_tensor(f"out_{name}", shape, F32, kind="ExternalOutput").ap()
    build(nc, ins, outs, cons)
    r = _run(nc, [arrays], core_ids=[0])
    return tuple(r.results[0][f"out_{name}"] for name, _ in _OUTS)
```
